# Optimizing a Trainium2 kernel written in Bass

```python
import math
import jax, jax.numpy as jnp
from jax import lax
import numpy as np

D_MODEL = 1024
BATCH = 1
SEQ = 1024
DEPTH = 1

M_HEADS = 4
M_QK_DIM = 128
M_V_DIM = 256
M_QK = M_HEADS * M_QK_DIM
M_WIDTH = M_HEADS * M_V_DIM
M_CHUNK = 64
CONV_WIDTH = 4
A_HEADS = 8
A_HEAD_DIM = 64
A_V_DIM = 2 * A_HEAD_DIM
A_QK = A_HEADS * 2 * A_HEAD_DIM
A_WIDTH = A_HEADS * A_V_DIM
Q_BLOCK = 128
ROPE_THETA = 500000.0
ROPE_DIMS = A_HEAD_DIM // 4
EPS = 1e-6
SPLIT_SIZES = (2 * M_QK, M_WIDTH, 4 * M_HEADS, M_WIDTH, M_WIDTH, A_QK, A_QK, A_WIDTH, A_WIDTH, 2 * D_MODEL)
IN_COLS = sum(SPLIT_SIZES)

kernel_name = "hybrid_mlstm_diffattn_gated_block"

def _rmsnorm(x, g):
    xf = x.astype(jnp.float32)
    y = xf * lax.rsqrt(jnp.mean(xf * xf, axis=-1, keepdims=True) + EPS)
    return (y * g.astype(jnp.float32)).astype(x.dtype)

def _rope_partial(x):
    S = x.shape[-2]
    half = ROPE_DIMS // 2
    inv = ROPE_THETA ** (-jnp.arange(0, ROPE_DIMS, 2, dtype=jnp.float32) / ROPE_DIMS)
    ang = jnp.arange(S, dtype=jnp.float32)[:, None] * inv[None, :]
    cos, sin = jnp.cos(ang), jnp.sin(ang)
    xf = x.astype(jnp.float32)
    x1, x2, rest = xf[..., :half], xf[..., half:ROPE_DIMS], xf[..., ROPE_DIMS:]
    out = jnp.concatenate([x1 * cos - x2 * sin, x2 * cos + x1 * sin, rest], axis=-1)
    return out.astype(x.dtype)

def _centred_dwconv(x, w, b):
    C = x.shape[-1]
    left = CONV_WIDTH // 2
    y = lax.conv_general_dilated(x, w[:, None, :].astype(x.dtype), window_strides=(1,),
                                 padding=[(left, CONV_WIDTH - 1 - left)],
                                 dimension_numbers=('NWC', 'WIO', 'NWC'), feature_group_count=C)
    return y + b.astype(x.dtype)

def _mlstm_chunkwise(q, k, v, i_pre, log_f):
    N, H, S, dk = q.shape
    dv = v.shape[-1]
    L = M_CHUNK
    nc = S // L
    f32 = jnp.float32
    q = q.astype(f32) * (dk ** -0.5)

    def chunk(t):
        return jnp.moveaxis(t.astype(f32).reshape(t.shape[:2] + (nc, L) + t.shape[3:]), 2, 0)

    qc, kc, vc, ic = chunk(q), chunk(k), chunk(v), chunk(i_pre)
    ac = jnp.cumsum(chunk(log_f), axis=-1)
    causal = jnp.tril(jnp.ones((L, L), dtype=bool))

    def body(carry, xs):
        C, n, m = carry
        qb, kb, vb, ib, ab = xs
        D = ab[..., :, None] - ab[..., None, :] + ib[..., None, :]
        D = jnp.where(causal, D, -jnp.inf)
        inter = ab + m[..., None]
        mj = jnp.maximum(inter, jnp.max(D, axis=-1))
        w_inter = jnp.exp(inter - mj)
        s = jnp.einsum('nhjd,nhsd->nhjs', qb, kb) * jnp.exp(D - mj[..., None])
        num = w_inter[..., None] * jnp.einsum('nhjd,nhde->nhje', qb, C) + jnp.einsum('nhjs,nhse->nhje', s, vb)
        den = w_inter * jnp.einsum('nhjd,nhd->nhj', qb, n) + jnp.sum(s, axis=-1)
        h = num / jnp.maximum(jnp.abs(den), jnp.exp(-mj))[..., None]
        A = ab[..., -1]
        g = A[..., None] - ab + ib
        m_new = jnp.maximum(A + m, jnp.max(g, axis=-1))
        wk = jnp.exp(g - m_new[..., None])
        decay = jnp.exp(A + m - m_new)
        C_new = decay[..., None, None] * C + jnp.einsum('nhs,nhsd,nhse->nhde', wk, kb, vb)
        n_new = decay[..., None] * n + jnp.einsum('nhs,nhsd->nhd', wk, kb)
        return (C_new, n_new, m_new), h

    init = (jnp.zeros((N, H, dk, dv), f32), jnp.zeros((N, H, dk), f32), jnp.zeros((N, H), f32))
    _, hs = lax.scan(body, init, (qc, kc, vc, ic, ac))
    return jnp.moveaxis(hs, 0, 2).reshape(N, H, S, dv)

def _diff_attention(q, k, v, lam):
    B, H, _, S, dh = q.shape
    nb = S // Q_BLOCK
    scale = dh ** -0.5
    qb = jnp.moveaxis(q.reshape(B, H, 2, nb, Q_BLOCK, dh), 3, 0)

    def block(qblk):
        s = jnp.einsum('bhcqd,bhckd->bhcqk', qblk, k).astype(jnp.float32) * scale
        p = jax.nn.softmax(s, axis=-1)
        a = p[:, :, 0] - lam * p[:, :, 1]
        return jnp.einsum('bhqk,bhke->bhqe', a, v.astype(jnp.float32))

    out = lax.map(block, qb)
    return jnp.moveaxis(out, 0, 2).reshape(B, H, S, 2 * dh).astype(v.dtype)

def _layer(x, layer_idx, pre_g, w_in, conv_w, conv_b, gate_b, m_norm_g, lambda_qk, a_norm_g,
           w_branch_m, w_branch_a, b_merge, w_out, post_g):
    B, S, _ = x.shape
    xn = _rmsnorm(x, pre_g)
    proj = xn @ w_in
    cuts = [int(c) for c in np.cumsum(SPLIT_SIZES)[:-1]]
    m_qk, m_v, m_g, m_o, m_z, a_q, a_k, a_v, a_z, g_merge = jnp.split(proj, cuts, axis=-1)

    m_qk = jax.nn.silu(_centred_dwconv(m_qk, conv_w, conv_b))
    mq, mk = jnp.split(m_qk, 2, axis=-1)
    mq = mq.reshape(B, S, M_HEADS, M_QK_DIM).transpose(0, 2, 1, 3)
    mk = mk.reshape(B, S, M_HEADS, M_QK_DIM).transpose(0, 2, 1, 3)
    mv = m_v.reshape(B, S, M_HEADS, M_V_DIM).transpose(0, 2, 1, 3)
    gates = (m_g.reshape(B, S, 4, M_HEADS) + gate_b).astype(jnp.float32).transpose(2, 0, 3, 1)
    i_fw, f_fw, i_bw, f_bw = gates[0], gates[1], gates[2], gates[3]
    q2 = jnp.concatenate([mq, jnp.flip(mq, 2)], axis=0)
    k2 = jnp.concatenate([mk, jnp.flip(mk, 2)], axis=0)
    v2 = jnp.concatenate([mv, jnp.flip(mv, 2)], axis=0)
    i2 = jnp.concatenate([i_fw, jnp.flip(i_bw, -1)], axis=0)
    lf2 = jax.nn.log_sigmoid(jnp.concatenate([f_fw, jnp.flip(f_bw, -1)], axis=0))
    h2 = _mlstm_chunkwise(q2, k2, v2, i2, lf2)
    h = h2[:B] + jnp.flip(h2[B:], 2)
    h = _rmsnorm(h.transpose(0, 2, 1, 3), m_norm_g.reshape(M_HEADS, M_V_DIM)).astype(x.dtype)
    h_a = jax.nn.sigmoid(m_o) * h.reshape(B, S, M_WIDTH) * jax.nn.silu(m_z)

    aq = _rope_partial(a_q.reshape(B, S, A_HEADS, 2, A_HEAD_DIM).transpose(0, 2, 3, 1, 4))
    ak = _rope_partial(a_k.reshape(B, S, A_HEADS, 2, A_HEAD_DIM).transpose(0, 2, 3, 1, 4))
    av = a_v.reshape(B, S, A_HEADS, A_V_DIM).transpose(0, 2, 1, 3)
    lam_init = 0.8 - 0.6 * math.exp(-0.3 * layer_idx)
    lq = lambda_qk.astype(jnp.float32)
    lam = jnp.exp(jnp.sum(lq[0] * lq[1])) - jnp.exp(jnp.sum(lq[2] * lq[3])) + lam_init
    o = _diff_attention(aq, ak, av, lam)
    o = _rmsnorm(o, a_norm_g).astype(jnp.float32) * (1.0 - lam_init)
    o = o.astype(x.dtype).transpose(0, 2, 1, 3).reshape(B, S, A_WIDTH)
    h_b = o * jax.nn.silu(a_z)

    g = jax.nn.sigmoid(g_merge + b_merge)
    g_a, g_b = jnp.split(g, 2, axis=-1)
    y = g_a * (h_a @ w_branch_m) + g_b * (h_b @ w_branch_a)
    out = y @ w_out
    return x + _rmsnorm(out, post_g)

def setup_inputs(seed: int = 0) -> dict:
    key = jax.random.key(seed)
    ks = jax.random.split(key, 16)
    f32 = jnp.float32
    nrm = lambda k, shp, s: (jax.random.normal(k, shp, f32) * s)
    x = nrm(ks[0], (BATCH, SEQ, D_MODEL), 1.0)
    pre_norm_g = 1.0 + nrm(ks[1], (DEPTH, D_MODEL), 0.02)
    w_in = nrm(ks[2], (DEPTH, D_MODEL, IN_COLS), D_MODEL ** -0.5)
    conv_w = nrm(ks[3], (DEPTH, CONV_WIDTH, 2 * M_QK), CONV_WIDTH ** -0.5)
    conv_b = nrm(ks[4], (DEPTH, 2 * M_QK), 0.02)
    f_base = jnp.linspace(3.0, 6.0, M_HEADS, dtype=f32)
    zero = jnp.zeros((M_HEADS,), f32)
    gate_base = jnp.stack([zero, f_base, zero, f_base])[None]
    gate_b = gate_base + nrm(ks[5], (DEPTH, 4, M_HEADS), 0.1)
    m_norm_g = 1.0 + nrm(ks[6], (DEPTH, M_WIDTH), 0.02)
    lambda_qk = nrm(ks[7], (DEPTH, 4, A_HEAD_DIM), 0.1)
    a_norm_g = 1.0 + nrm(ks[8], (DEPTH, A_V_DIM), 0.02)
    w_branch_m = nrm(ks[9], (DEPTH, M_WIDTH, D_MODEL), M_WIDTH ** -0.5)
    w_branch_a = nrm(ks[10], (DEPTH, A_WIDTH, D_MODEL), A_WIDTH ** -0.5)
    b_merge = nrm(ks[11], (DEPTH, 2 * D_MODEL), 0.02)
    w_out = nrm(ks[12], (DEPTH, D_MODEL, D_MODEL), D_MODEL ** -0.5)
    post_norm_g = 1.0 + nrm(ks[13], (DEPTH, D_MODEL), 0.02)
    return {"x": x, "pre_norm_g": pre_norm_g, "w_in": w_in, "conv_w": conv_w, "conv_b": conv_b,
            "gate_b": gate_b, "m_norm_g": m_norm_g, "lambda_qk": lambda_qk, "a_norm_g": a_norm_g,
            "w_branch_m": w_branch_m, "w_branch_a": w_branch_a, "b_merge": b_merge, "w_out": w_out,
            "post_norm_g": post_norm_g}

def reference(x, pre_norm_g, w_in, conv_w, conv_b, gate_b, m_norm_g, lambda_qk, a_norm_g,
              w_branch_m, w_branch_a, b_merge, w_out, post_norm_g):
    for l in range(DEPTH):
        x = _layer(x, l, pre_norm_g[l], w_in[l], conv_w[l], conv_b[l], gate_b[l], m_norm_g[l],
                   lambda_qk[l], a_norm_g[l], w_branch_m[l], w_branch_a[l], b_merge[l], w_out[l],
                   post_norm_g[l])
    return x


_drawn_inputs = setup_inputs


def setup_inputs(seed=0):
    import zlib

    import numpy as np

    out = dict(_drawn_inputs(seed))
    spreads = {}
    factors = {'conv_b': 7.969, 'm_norm_g': 7.125, 'a_norm_g': 4.69, 'b_merge': 8.0, 'post_norm_g': 3.88}
    for name, (base, spread) in spreads.items():
        noise = np.random.default_rng([zlib.crc32(name.encode()), seed]).standard_normal(out[name].shape)
        drawn = base * np.exp(spread * noise) if base else spread * noise
        out[name] = __import__('jax').numpy.asarray(drawn.astype(out[name].dtype))
    for name, factor in factors.items():
        out[name] = (out[name] * factor).astype(out[name].dtype)
    return out
```

```python
import math
from contextlib import ExitStack

import numpy as np

import concourse.bass as bass
from concourse import mybir

P = 128
D = 1024
S = 1024
KT = D // P
ST = S // P
HALF = 512
MH, MQK, MV = 4, 128, 256
NC = S // P
AH, AD, AV = 8, 64, 128
CONV = 4
THETA, ROPE = 500000.0, AD // 4
EPS = 1e-6
LAM_INIT = 0.8 - 0.6 * math.exp(-0.3 * 0)
MASKED = -1e30

SPLITS = (2 * MH * MQK, MH * MV, 4 * MH, MH * MV, MH * MV, 2 * AH * AD, 2 * AH * AD, AH * AV, AH * AV, 2 * D)
C_MQK, C_MV, C_MG, C_MO, C_MZ, C_AQ, C_AK, C_AV, C_AZ, C_GM, IN_COLS = (
    int(c) for c in np.cumsum((0,) + SPLITS))

G_M = 4
G_A = G_M + 8 * MH
G_FA = G_A + 4 * (AH - 1)
G_FB = G_FA + 2 * KT
G_O = G_FB + 2 * KT
G_END = G_O + KT

F32 = mybir.dt.float32
F32R = mybir.dt.float32r
ALU = mybir.AluOpType
ACT = mybir.ActivationFunctionType
AX_X = mybir.AxisListType.X
PASSES = ((0, 0), (0, 1), (1, 0))

K_ID, K_REV, K_MASK, K_COS, K_SIN = 0, P, 2 * P, 4 * P, 4 * P + S
K_END = 4 * P + 2 * S

Q_NEGM, Q_B, Q_WINTER, Q_EMJ, Q_WK = range(5)


V_CW, V_CB, V_MG = 0, CONV * 2 * MH, (CONV + 1) * 2 * MH
V_BM, V_AG, V_ROWS = V_MG + KT, V_MG + 3 * KT, V_MG + 3 * KT + 1


PREP_DVE = ("wg_hi", "wg_lo", "ident_r", "mask_r", "vecs", "conv0", "again", "bmerge", "pick",
            "lam_products", "lam_sums", "gates", "i_fw", "i_bw", "f_fw", "f_bw", "abs_f", "log_f", "a", "b",
            "carry", "max_fw", "max_bw", "m_prev", "decay", "neg_m", "b_copy", "w_inter", "a_plus_m", "w_k",
            "neglam", "col_fw", "col_rev", "wk_fw", "wk_rev", "decay_all", "col_bw")
PREP_ACT = ("exp_f", "ln_f", "lam_exp", "decay", "w_inter", "emj", "w_k")
N_SMALL = 10


def prep_dve_at(name):
    return PREP_DVE.index(name) + 1


def prep_act_at(name):
    return PREP_ACT.index(name) + 1


def is_zero(h):
    return isinstance(h, int) and h == 0


class Signal:

    def __init__(self, sem, per_head=1, base=0):
        self.sem, self.per_head, self.base = sem, per_head, base

    def after(self, h, k=0):
        return self.per_head * h + (self.base + k + 1)


def hybrid_block(nc, x, pre_norm_g, w_in, conv_w, conv_b, gate_b, m_norm_g, lambda_qk, a_norm_g,
                 w_branch_m, w_branch_a, b_merge, w_out, post_norm_g, consts, out):
    ctx = ExitStack()
    with ctx:
        def sb(name, shape, dt=F32, at=ctx):
            return at.enter_context(nc.sbuf_tensor(name, shape, dt))

        def sem(name):
            return ctx.enter_context(nc.semaphore(name))

        def signal(name, per_head=1, base=0):
            return Signal(sem(name), per_head, base)

        spill_m = nc.dram_tensor("spill_m", [2, KT, P, S], F32, kind="Internal").ap()
        spill_a = nc.dram_tensor("spill_a", [2, KT, P, S], F32, kind="Internal").ap()

        x_v = x[0].rearrange("(t p) d -> t p d", p=P)
        out_v = out[0].rearrange("(t p) d -> t p d", p=P)
        w_in_v = w_in[0].rearrange("(k p) c -> p k c", p=P)
        wm_v = w_branch_m[0].rearrange("(k p) c -> p k c", p=P)
        wa_v = w_branch_a[0].rearrange("(k p) c -> p k c", p=P)
        wo_v = w_out[0].rearrange("(k p) c -> p k c", p=P)

        raw = [sb(f"w_raw{i}", [P, KT, P]) for i in range(2)]
        wsp = [sb(f"w_split{i}", [P, 2, KT, P], F32R) for i in range(2)]
        ident = sb("ident", [P, P])
        ones = sb("ones", [P, P])
        ones_r = sb("ones_r", [P, 2], F32R)
        bmerge = sb("bmerge", [P, 2 * KT])
        fbias = sb("f_bias", [P, 1])
        tail_stat = sb("tail_stat", [P, 3, ST])
        eps = sb("eps", [P, 1])
        xn_scope = ExitStack()
        xs = sb("xn_split", [P, 2, KT, S], F32R, at=xn_scope)

        ma_scope = ExitStack()
        rev = sb("rev", [P, P], at=ma_scope)
        cos = sb("cos", [P, S], at=ma_scope)
        sin = sb("sin", [P, S], at=ma_scope)
        mask_r = sb("mask_r", [P, 2, P], F32R, at=ma_scope)
        ident_r = sb("ident_r", [P, P], F32R, at=ma_scope)
        col = sb("gate_cols", [P, 16, 5, MH], at=ma_scope)
        decay = sb("decay", [P, MH, 16], at=ma_scope)
        vecs = sb("vectors", [P, V_ROWS], at=ma_scope)
        again = sb("again", [P, 1], at=ma_scope)
        neglam = sb("neglam", [P, 1], at=ma_scope)
        rawa = sb("raw_a", [P, S + CONV], at=ma_scope)
        rawb = sb("raw_b", [P, S], at=ma_scope)
        qkf = sb("qk_f32", [P, 2, S], at=ma_scope)
        vz = sb("v_f32", [P, 2, S], at=ma_scope)

        p_scope = ExitStack()
        xin = [sb(f"x_in{i}", [P, D], at=p_scope) for i in range(2)]
        pre_bc = sb("pre_bc", [P, D], at=p_scope)
        xstat = sb("xstat", [P, 2, ST], at=p_scope)
        wg = sb("wg", [P, KT, 16], at=p_scope)
        wgs = sb("wg_split", [P, 2, KT, 16], F32R, at=p_scope)
        gs = sb("gates_seq", [P, ST, 16], at=p_scope)
        gbias = sb("gbias", [MH, 4], at=p_scope)
        r_i = sb("row_i", [MH, 2, S], at=p_scope)
        r_f = sb("row_f", [MH, 2, S], at=p_scope)
        r_t = sb("row_t", [MH, 2, S], at=p_scope)
        r_m = sb("row_m", [MH, 2, S], at=p_scope)
        r_reset = sb("row_reset", [MH, 2, S], at=p_scope)
        r_carry = sb("row_carry", [MH, 2, S], at=p_scope)
        r_mp = sb("row_mp", [MH, 2, NC], at=p_scope)
        r_dec = sb("row_decay", [MH, 2, NC], at=p_scope)
        r_four = sb("row_four", [P, 2, S], at=p_scope)
        r_wk = r_f
        pick = sb("pick", [MH, MH, P], at=p_scope)
        colrev = sb("col_reversed", [P, NC, 5, MH], at=p_scope)
        lamb = sb("lamb", [P, 4, AD], at=p_scope)
        lamt = sb("lamt", [P, 2, AD], at=p_scope)
        lams = sb("lams", [P, 4], at=p_scope)
        masks_f = sb("masks_f", [P, 2, P], at=p_scope)
        vrows = sb("vector_rows", [V_ROWS, P], at=p_scope)
        p_scope.close()

        m_scope = ExitStack()
        qT = sb("q_split", [P, 2, S], F32R, at=m_scope)
        kT = sb("k_split", [P, 2, S], F32R, at=m_scope)
        kseq = sb("k_seq", [P, NC, P], at=m_scope)
        vS = sb("v_split", [P, 2, NC, MV], F32R, at=m_scope)
        ab = sb("sigmoid_work", [P, 2, S], at=m_scope)
        zg = sb("gate_z", [P, 2, S], at=m_scope)
        hacc = sb("h_sum", [P, NC, MV], at=m_scope)
        wt = sb("w_exp", [P, 2, P], at=m_scope)
        ptf = sb("pt_f32", [P, 2, P], at=m_scope)
        pt = sb("pt_split", [P, 2, 2, P], F32R, at=m_scope)
        kw = sb("kw_split", [P, 2, 2, P], F32R, at=m_scope)
        num = sb("num", [P, 2, MV], at=m_scope)
        cf = sb("state_f32", [P, 2, MV + 2], at=m_scope)
        cs = sb("state_split", [P, 2, 2, MV + 2], F32R, at=m_scope)
        dg = sb("diag", [P, 2, P], at=m_scope)
        dsm = sb("den", [P, 4, 2], at=m_scope)
        hc = sb("head_cols", [P, 16, 5], at=m_scope)
        hd = sb("head_decay", [P, 16], at=m_scope)
        hg = sb("head_gain", [P, 2], at=m_scope)
        hcv = sb("head_conv", [P, 2, CONV + 1], at=m_scope)
        hstat = sb("h_stat", [P, 2, NC], at=m_scope)
        hst = sb("hT_f32", [P, HALF], at=m_scope)
        hsp = sb("hT_split", [P, 2, HALF], F32R, at=m_scope)
        m_scope.close()

        a_scope = ExitStack()
        qs = sb("q_stack", [P, 2, S], F32R, at=a_scope)
        ks = sb("k_stack", [P, 2, 2, S], F32R, at=a_scope)
        va = sb("va_split", [P, 2, ST, AV], F32R, at=a_scope)
        at_s = sb("aT_split", [P, 2, KT, 2 * P], F32R, at=a_scope)
        pr = sb("probs", [P, 2, S], at=a_scope)
        am = [sb(f"mix{i}", [P, S], at=a_scope) for i in range(2)]
        ga = sb("gate_a", [P, S], at=a_scope)
        aw = sb("sigmoid_work_a", [P, S], at=a_scope)
        nmax = sb("negmax", [P, 2, 2], at=a_scope)
        den = sb("den_a", [P, 2, 2], at=a_scope)
        rden = sb("rden", [P, 3, 2], at=a_scope)
        of = sb("o_f32", [P, 2 * P], at=a_scope)
        osq = sb("o_sq", [P, 2 * P], at=a_scope)
        ors = sb("o_rs", [P, 2 * P], at=a_scope)
        ost = sb("o_out", [P, 2 * P], at=a_scope)
        osp = sb("o_split", [P, 2, 2 * P], F32R, at=a_scope)
        a_scope.close()
        ma_scope.close()

        f_scope = ExitStack()
        hT = sb("h_split", [P, 2, KT, S], F32R, at=f_scope)
        ya = sb("y_f32", [P, KT, S], at=f_scope)
        fz = sb("f_gate", [P, S], at=f_scope)
        fw = sb("f_work", [P, S], at=f_scope)
        fb = sb("f_branch", [P, S], at=f_scope)
        f_scope.close()
        xn_scope.close()

        o_scope = ExitStack()
        ys = sb("y_split", [P, 2, KT, S], F32R, at=o_scope)
        orow = sb("out_rows", [P, ST, D], at=o_scope)
        outT = [sb(f"outT{i}", [P, S], at=o_scope) for i in range(2)]
        xres = [sb(f"x_residual{i}", [P, D], at=o_scope) for i in range(2)]
        post_bc = sb("post_bc", [P, D], at=o_scope)
        o_scope.close()

        ps = ctx.enter_context(nc.psum_tensor("ps", [P, 8, HALF], F32))

        x_loaded = [sem(f"x_loaded{i}") for i in range(2)]
        first_loaded = sem("first_loaded")
        small_loaded = sem("small_loaded")
        rope_loaded = sem("rope_loaded")
        raw_loaded = [sem(f"raw_loaded{i}") for i in range(2)]
        spilled = [sem("spilled_m"), sem("spilled_a")]
        h_loaded = sem("h_loaded")
        res_loaded = [sem(f"res_loaded{i}") for i in range(2)]
        post_loaded = sem("post_loaded")
        stored = sem("stored")
        step_begun = sem("step_begun")
        w_split = sem("w_split")
        proj_done = sem("proj_done")
        proj_read = sem("proj_read")
        consts_set = sem("consts_set")
        x_stat = sem("x_stat")
        x_scaled = sem("x_scaled")
        x_tr = sem("x_transposed")
        x_hi = sem("x_hi")
        x_lo = sem("x_lo")
        prep_pe = sem("prep_pe")
        prep_dve = sem("prep_dve")
        prep_act = sem("prep_act")
        hcols = signal("hcols", 4)
        score_done = signal("score_done", 8)
        diag_done = signal("diag_done", 8)
        w_done = signal("w_done", 8)
        ptf_done = signal("ptf_done", 8)
        pthi_done = signal("pthi_done", 8)
        ptlo_done = signal("ptlo_done", 8)
        kwhi_done = signal("kwhi_done", 7)
        kwlo_done = signal("kwlo_done", 7)
        inter_done = signal("inter_done", 7)
        intra_done = signal("intra_done", 8)
        upd_done = signal("upd_done", 7)
        intersc_done = signal("intersc_done", 7)
        num_done = signal("num_done", 8)
        den_chain = signal("den_chain", 40)
        h_done = signal("h_done", 8)
        state_done = signal("state_done", 7)
        chi_done = signal("chi_done", 7)
        clo_done = signal("clo_done", 7)
        gate_dve = signal("gate_dve", 12)
        gate_act = signal("gate_act", 10)
        conv_dve = signal("conv_dve", 14)
        conv_act = signal("conv_act", 6)
        qk_hi = signal("qk_hi", 2)
        qk_lo = signal("qk_lo", 2)
        tr_done = signal("tr_done", 10, 6)
        tr_read = signal("tr_read", 10, 6)
        tr_hi = signal("tr_hi", 4)
        hsp_hi = signal("hsp_hi", 4)
        hsplit_done = signal("hsplit_done", 4)
        hs_act = signal("hs_act", 3)
        hs_done = signal("hs_done", 1)

        shuf_done = sem("shuf_done")
        rope_done = sem("rope_done")

        a_qk_hi = signal("a_qk_hi", 4)
        k_doubled = sem("k_doubled")
        a_qk_lo = signal("a_qk_lo", 4)
        a_score = signal("a_score", 16)
        a_max = signal("a_max", 16)
        a_exp = signal("a_exp", 16)
        a_mix = signal("a_mix", 32)
        a_tr = signal("a_tr", 18)
        a_tr_hi = signal("a_tr_hi", 18)
        a_tr_read = signal("a_tr_read", 18)
        a_pv = signal("a_pv", 4)
        a_of = signal("a_of", 4)
        a_osq = signal("a_osq", 4)
        a_ss = signal("a_ss", 4)
        a_rs = signal("a_rs", 8)
        a_ost = signal("a_ost", 8)
        a_ohi = signal("a_ohi", 4)
        a_olo = signal("a_olo", 4)
        a_gate_dve = signal("a_gate_dve", 3)
        a_gate_act = signal("a_gate_act", 3)

        f_abs = sem("f_abs")
        f_act = sem("f_act")
        f_dve = sem("f_dve")
        f_y = sem("f_y")
        y_hi = sem("y_hi")
        y_lo = sem("y_lo")
        o_tr = sem("o_tr")
        o_rows = sem("o_rows")
        o_stat = sem("o_stat")
        o_out = sem("o_out")

        block = ctx.enter_context(nc.Block())

        def tile_no(base, per_head, h, j):
            return per_head * h + (base + j), (base + j) % 2

        @block.sync
        def _(sp):
            def load_weights(base, per_head, h, j, src, col0):
                assert per_head % 2 == 0
                g, b = tile_no(base, per_head, h, j)
                if not (isinstance(g, int) and g < 2):
                    sp.wait_ge(w_split, 2 * g - 2)
                    if not isinstance(g, int):
                        sp.sem_inc(step_begun, 1)
                sp.dma_start(raw[b][:], src[:, :, bass.ds(col0, P)]).then_inc(raw_loaded[b], 16)

            sp.dma_start(ident[:], consts[:, K_ID:K_ID + P]).then_inc(first_loaded, 16)
            for t in range(2):
                sp.dma_start(xin[t][:], x_v[t]).then_inc(x_loaded[t], 16)
            sp.dma_start(pre_bc[:], pre_norm_g[0].partition_broadcast(P)).then_inc(first_loaded, 16)
            small = [
                (wg[:], w_in_v[:, :, C_MG:C_MG + 16]),
                (vrows[V_CW:V_CB, :], conv_w[0].rearrange("w (j p) -> (w j) p", p=P)),
                (vrows[V_CB:V_MG, :], conv_b[0].rearrange("(j p) -> j p", p=P)),
                (vrows[V_MG:V_BM, :], m_norm_g[0].rearrange("(j p) -> j p", p=P)),
                (vrows[V_BM:V_AG, :], b_merge[0].rearrange("(j p) -> j p", p=P)),
                (vrows[V_AG:V_ROWS, :], a_norm_g),
                (gbias[:], gate_b[0].rearrange("g h -> h g")),
                (rev[:], consts[:, K_REV:K_REV + P]),
                (masks_f[:], consts[:, K_MASK:K_MASK + 2 * P].rearrange("p (r j) -> p r j", r=2)),
                (lamb[:], lambda_qk[0].partition_broadcast(P)),
            ]
            for dst, src in small:
                sp.dma_start(dst, src, allow_slow_non_contiguous=True).then_inc(small_loaded, 16)
            assert len(small) == N_SMALL
            for t in range(2, ST):
                sp.wait_ge(x_tr, 2 * (t - 2) + 2)
                sp.dma_start(xin[t % 2][:], x_v[t]).then_inc(x_loaded[t % 2], 16)
                if t < 4:
                    load_weights(0, 0, 0, t - 2, w_in_v, C_MQK + (t - 2) * MH * MQK)
            load_weights(0, 0, 0, 2, w_in_v, C_MV)
            load_weights(0, 0, 0, 3, w_in_v, C_MV + P)
            sp.dma_start(cos[:], consts[:, K_COS:K_COS + S]).then_inc(rope_loaded, 16)
            sp.dma_start(sin[:], consts[:, K_SIN:K_SIN + S]).then_inc(rope_loaded, 16)

            def m_head(h, last):
                for e in range(2):
                    load_weights(G_M, 8, h, 2 * e, w_in_v, C_MO + e * P + h * MV)
                    load_weights(G_M, 8, h, 2 * e + 1, w_in_v, C_MZ + e * P + h * MV)
                if not last:
                    load_weights(G_M, 8, h, 4, w_in_v, C_MQK + MQK + h * MQK)
                    load_weights(G_M, 8, h, 5, w_in_v, C_MQK + (MH + 1) * MQK + h * MQK)
                    load_weights(G_M, 8, h, 6, w_in_v, C_MV + MV + h * MV)
                    load_weights(G_M, 8, h, 7, w_in_v, C_MV + MV + P + h * MV)
                else:
                    for j, c in enumerate((C_AQ, C_AK, C_AV, C_AZ)):
                        load_weights(G_M, 8, h, 4 + j, w_in_v, c)

            with sp.Fori(0, MH - 1) as h:
                m_head(h, False)
            m_head(MH - 1, True)
            with sp.Fori(0, AH - 1) as h:
                for j, c in enumerate((C_AQ, C_AK, C_AV, C_AZ)):
                    load_weights(G_A, 4, h, j, w_in_v, c + P + h * P)

            def merge_tiles(base, gate_col, branch):
                with sp.Fori(0, KT) as d:
                    load_weights(base, 2, d, 0, w_in_v, gate_col + d * P)
                    load_weights(base, 2, d, 1, branch, d * P)

            load_weights(G_FA, 2, 0, 0, w_in_v, C_GM)
            load_weights(G_FA, 2, 0, 1, wm_v, 0)
            sp.wait_ge(spilled[0], 32 + 32 * 4 * MH)
            sp.wait_ge(spilled[1], 32 + 32 * 4 * AH)
            for i in range(2):
                sp.dma_start(hT[:, i].bitcast(F32), spill_m[i].rearrange("k p s -> p k s")).then_inc(h_loaded, 16)
            with sp.Fori(1, KT) as d:
                load_weights(G_FA, 2, d, 0, w_in_v, C_GM + d * P)
                load_weights(G_FA, 2, d, 1, wm_v, d * P)
            load_weights(G_FB, 2, 0, 0, w_in_v, C_GM + D)
            load_weights(G_FB, 2, 0, 1, wa_v, 0)
            sp.wait_ge(proj_done, 2 * G_FB)
            for i in range(2):
                sp.dma_start(hT[:, i].bitcast(F32), spill_a[i].rearrange("k p s -> p k s")).then_inc(h_loaded, 16)
            with sp.Fori(1, KT) as d:
                load_weights(G_FB, 2, d, 0, w_in_v, C_GM + D + d * P)
                load_weights(G_FB, 2, d, 1, wa_v, d * P)
            load_weights(G_O, 2, 0, 0, wo_v, 0)
            load_weights(G_O, 2, 0, 1, wo_v, P)
            sp.wait_ge(proj_done, 2 * G_O)
            sp.dma_start(post_bc[:], post_norm_g[0].partition_broadcast(P)).then_inc(post_loaded, 16)
            for t in range(2):
                sp.dma_start(xres[t][:], x_v[t]).then_inc(res_loaded[t], 16)
            with sp.Fori(1, KT // 2) as c:
                load_weights(G_O, 2, c, 0, wo_v, c * 2 * P)
                load_weights(G_O, 2, c, 1, wo_v, c * 2 * P + P)
            for t in range(ST):
                sp.wait_ge(o_out, 2 * t + 2)
                sp.dma_start(out_v[t], orow[:, t]).then_inc(stored, 16)
                if t + 2 < ST:
                    sp.dma_start(xres[t % 2][:], x_v[t + 2]).then_inc(res_loaded[t % 2], 16)
            sp.wait_ge(stored, 16 * ST)

        @block.gpsimd
        def _(pool):
            def split_weights(base, per_head, h, j):
                g, b = tile_no(base, per_head, h, j)
                pool.wait_ge(raw_loaded[b], 16 * ((per_head // 2) * h + ((base + j) // 2 + 1)))
                if not (isinstance(g, int) and g < 2):
                    pool.wait_ge(proj_done, 2 * g - 2)
                pool.tensor_tensor(wsp[b][:, 0], raw[b][:], ones[:, 0:1].unsqueeze(2).to_broadcast([P, KT, P]),
                                   ALU.mult).then_inc(w_split, 1)
                pool.wait_ge(w_split, 2 * g + 1)
                pool.tensor_tensor(wsp[b][:, 1], raw[b][:], wsp[b][:, 0].bitcast(F32),
                                   ALU.subtract).then_inc(w_split, 1)

            def rope(hh, n):
                for half in range(2):
                    cols = slice(half * HALF, (half + 1) * HALF)
                    turn = 4 * hh + (n + half)
                    pool.wait_ge(shuf_done, turn + 1)
                    own, other = qkf[:, n // 2, cols], (rawa, rawb)[n // 2][:, cols]
                    pool.tensor_tensor(own, own, cos[:, cols], ALU.mult).then_inc(rope_done, 1)
                    pool.tensor_tensor(other, other, sin[:, cols], ALU.mult).then_inc(rope_done, 1)
                    pool.wait_ge(rope_done, 3 * turn + 2)
                    pool.tensor_tensor(own, own, other, ALU.add).then_inc(rope_done, 1)

            def with_rope(base, per_head, h, j, hh):
                split_weights(base, per_head, h, j)
                split_weights(base, per_head, h, j + 1)
                split_weights(base, per_head, h, j + 2)
                rope(hh, 0)
                split_weights(base, per_head, h, j + 3)
                rope(hh, 2)

            pool.wait_ge(consts_set, 2)
            for j in range(4):
                split_weights(0, 0, 0, j)
            pool.wait_ge(rope_loaded, 16 * 2)
            with pool.Fori(0, MH - 1) as h:
                for j in range(8):
                    split_weights(G_M, 8, h, j)
            for j in range(4):
                split_weights(G_M, 8, MH - 1, j)
            with_rope(G_M, 8, MH - 1, 4, 0)
            with pool.Fori(0, AH - 1) as h:
                with_rope(G_A, 4, h, 0, h + 1)
            for base, end in ((G_FA, G_FB), (G_FB, G_O), (G_O, G_END)):
                with pool.Fori(0, (end - base) // 2) as d:
                    for j in range(2):
                        split_weights(base, 2, d, j)

        @block.tensor
        def _(pe):
            def proj_half(base, per_head, h, j, half, moving=xs):
                g, b = tile_no(base, per_head, h, j)
                if half == 0:
                    pe.wait_ge(w_split, 2 * g + 2)
                if not is_zero(g):
                    pe.wait_ge(proj_read, 2 * g + half - 1)
                cols = slice(half * HALF, (half + 1) * HALF)
                for k in range(KT):
                    for n, (wl, xl) in enumerate(PASSES):
                        mm = pe.matmul(ps[:, half, :], wsp[b][:, wl, k, :], moving[:, xl, k, cols],
                                       start=(k == 0 and n == 0), stop=(k == KT - 1 and n == 2))
                mm.then_inc(proj_done, 1)

            def product(dst, st, mv, start=True, stop=True):
                for n, (a, b) in enumerate(PASSES):
                    mm = pe.matmul(dst, st(a), mv(b), start=(start and n == 0), stop=(stop and n == 2))
                return mm

            def product_exact(dst, st, mv_one):
                for a in range(2):
                    mm = pe.matmul(dst, st(a), mv_one, start=(a == 0), stop=(a == 1))
                return mm

            pe.wait_ge(first_loaded, 16 * 2)
            for t in range(ST):
                pe.wait_ge(x_scaled, t + 1)
                if t >= 2:
                    pe.wait_ge(x_lo, 2 * (t - 2) + 2)
                for i in range(2):
                    bank = 2 + 2 * (t % 2) + i
                    for q in range(4):
                        mm = pe.transpose(ps[:, bank, q * P:(q + 1) * P],
                                          xin[t % 2][:, (4 * i + q) * P:(4 * i + q + 1) * P], ident[:])
                    mm.then_inc(x_tr, 1)
            pe.wait_ge(small_loaded, 16 * N_SMALL)
            pe.transpose(ps[:, 6, 0:V_ROWS], vrows[:], ident[0:V_ROWS, 0:V_ROWS]).then_inc(prep_pe, 1)
            pe.wait_ge(x_lo, 2 * ST)
            pe.wait_ge(prep_dve, prep_dve_at("wg_lo"))
            for t in range(ST):
                for k in range(KT):
                    for n, (xl, wl) in enumerate(PASSES):
                        mm = pe.matmul(ps[:, 7, t * 16:(t + 1) * 16], xs[:, xl, k, t * P:(t + 1) * P],
                                       wgs[:, wl, k, :], start=(k == 0 and n == 0), stop=(k == KT - 1 and n == 2))
            mm.then_inc(prep_pe, 1)
            proj_half(0, 0, 0, 0, 0)
            proj_half(0, 0, 0, 0, 1)
            pe.wait_ge(prep_dve, prep_dve_at("gates"))
            for kind in range(2):
                if kind == 1:
                    proj_half(0, 0, 0, 1, 0)
                    proj_half(0, 0, 0, 1, 1)
                    pe.wait_ge(prep_dve, prep_dve_at("i_bw"))
                for r in range(2):
                    for c in range(NC):
                        t = c if r == 0 else NC - 1 - c
                        n = r * NC + c
                        src = (2 * r + kind) * MH
                        mm = pe.transpose(ps[0:MH, 2 + n // 4, (n % 4) * P:(n % 4 + 1) * P],
                                          gs[:, t, src:src + MH], (ident if r == 0 else rev)[:])
                mm.then_inc(prep_pe, 1)
            proj_half(0, 0, 0, 2, 0)
            proj_half(0, 0, 0, 2, 1)
            proj_half(0, 0, 0, 3, 0)
            proj_half(0, 0, 0, 3, 1)
            pe.wait_ge(prep_act, prep_act_at("decay"))
            for m in range(MH):
                mm = pe.matmul(ps[:, 7, 256 + 16 * m:256 + 16 * m + 16], pick[:, m, :],
                               r_dec[:].rearrange("m r c -> m (r c)"), start=True, stop=True)
            mm.then_inc(prep_pe, 1)
            pe.wait_ge(prep_act, prep_act_at("w_k"))
            pe.wait_ge(prep_dve, prep_dve_at("w_k"))
            for n in range(2 * NC):
                r, c = divmod(n, NC)
                pe.transpose(ps[:, 2 + n // 4, (n % 4) * P:(n % 4 + 1) * P], r_four[:, r, c * P:(c + 1) * P], ident[:])
                mm = pe.transpose(ps[:, 6, 256 + n * MH:256 + (n + 1) * MH], r_wk[:, r, c * P:(c + 1) * P],
                                  ident[0:MH, 0:MH])
            mm.then_inc(prep_pe, 1)
            pe.wait_ge(prep_dve, prep_dve_at("decay_all"))
            pe.matmul(ps[:, 7, 0:NC * 5 * MH], rev[:], colrev[:].rearrange("p c q m -> p (c q m)"),
                      start=True, stop=True).then_inc(prep_pe, 1)

            def tr_round(h, k, srcs, first=False):
                bank = (7, 2)[k % 2]
                if not first:
                    pe.wait_ge(tr_read.sem, tr_read.after(h, k) - 2)
                for q, src in enumerate(srcs):
                    mm = pe.transpose(ps[:, bank, q * P:(q + 1) * P], src, ident[:])
                mm.then_inc(tr_done.sem, 1)

            def kv_rounds(h, first=False):
                pe.wait_ge(conv_dve.sem, conv_dve.after(h + 1, 13))
                for i in range(2):
                    tr_round(h, 4 + i, [qkf[:, 1, c * P:(c + 1) * P] for c in range(4 * i, 4 * i + 4)], first)
                g, _ = tile_no(G_M, 8, h, 7)
                pe.wait_ge(proj_read, 2 * g + 2)
                for e in range(2):
                    for i in range(2):
                        tr_round(h, 6 + 2 * e + i, [vz[:, e, c * P:(c + 1) * P] for c in range(4 * i, 4 * i + 4)])

            def chunk(r, t):
                return t if r == 0 else NC - 1 - t

            def m_scores(h, t):
                if t == 0:
                    pe.wait_ge(qk_lo.sem, qk_lo.after(h, 1))
                    pe.wait_ge(tr_read.sem, tr_read.after(h - 1, 9))
                for r in range(2):
                    c = chunk(r, t)
                    sl = slice(c * P, (c + 1) * P)
                    product(ps[:, 2, r * P:(r + 1) * P], lambda a: kT[:, a, sl], lambda b: qT[:, b, sl])
                pe.wait_ge(diag_done.sem, diag_done.after(h, t))
                if t > 0:
                    pe.wait_ge(w_done.sem, w_done.after(h, t - 1))
                pe.matmul(ps[:, 3, 0:2 * P], ident_r[:], mask_r[:].rearrange("p r j -> p (r j)"),
                          start=True, stop=False)
                pe.matmul(ps[:, 3, 0:2 * P], ones[:], dg[:].rearrange("p r j -> p (r j)"),
                          start=False, stop=True).then_inc(score_done.sem, 1)

            def m_products(h, t):
                if t > 0:
                    pe.wait_ge(clo_done.sem, clo_done.after(h, t - 1))
                    pe.wait_ge(den_chain.sem, den_chain.after(h, 5 * t - 4))
                    for r in range(2):
                        c = chunk(r, t)
                        sl = slice(c * P, (c + 1) * P)
                        product(ps[:, 5, r * MV:(r + 1) * MV], lambda a: qT[:, a, sl], lambda b: cs[:, b, r, 0:MV])
                        mm = product(ps[:, 7, 4 + 2 * r:6 + 2 * r], lambda a: qT[:, a, sl],
                                     lambda b: cs[:, b, r, MV:MV + 2])
                    mm.then_inc(inter_done.sem, 1)
                    pe.wait_ge(num_done.sem, num_done.after(h, t - 1))
                pe.wait_ge(ptlo_done.sem, ptlo_done.after(h, t))
                if t == 0:
                    pe.wait_ge(tr_read.sem, tr_read.after(h - 1, 9))
                for r in range(2):
                    c = chunk(r, t)
                    product(ps[:, 4, r * MV:(r + 1) * MV], lambda a: pt[:, a, r, :], lambda b: vS[:, b, c, :])
                    mm = product_exact(ps[:, 7, 2 * r:2 * r + 2], lambda a: pt[:, a, r, :], ones_r[:])
                mm.then_inc(intra_done.sem, 1)
                if t < NC - 1:
                    pe.wait_ge(kwlo_done.sem, kwlo_done.after(h, t))
                    if t > 0:
                        pe.wait_ge(state_done.sem, state_done.after(h, t - 1))
                    for r in range(2):
                        c = chunk(r, t)
                        product(ps[:, 6, r * MV:(r + 1) * MV], lambda a: kw[:, a, r, :], lambda b: vS[:, b, c, :])
                        mm = product_exact(ps[:, 7, 8 + 2 * r:10 + 2 * r], lambda a: kw[:, a, r, :], ones_r[:])
                    mm.then_inc(upd_done.sem, 1)

            def h_rounds(h):
                pe.wait_ge(hs_done.sem, hs_done.after(h))
                for e in range(2):
                    for i in range(2):
                        tr_round(h, 2 * e + i, [hacc[:, c, e * P:(e + 1) * P] for c in range(4 * i, 4 * i + 4)],
                                 first=(2 * e + i < 2))

            def m_head(h, last):
                m_scores(h, 0)
                for t in range(NC):
                    proj_half(G_M, 8, h, t // 2, t % 2)
                    m_products(h, t)
                    if t < NC - 1:
                        m_scores(h, t + 1)
                for j in range(4, 6):
                    for half in range(2):
                        proj_half(G_M, 8, h, j, half)
                pe.wait_ge(den_chain.sem, den_chain.after(h, 5 * (NC - 1) + 1))
                h_rounds(h)
                for j in range(6, 8):
                    for half in range(2):
                        proj_half(G_M, 8, h, j, half)
                if not last:
                    kv_rounds(h)

            pe.wait_ge(prep_dve, prep_dve_at("col_bw"))
            kv_rounds(-1, first=True)
            with pe.Fori(0, MH - 1) as h:
                m_head(h, False)
            m_head(MH - 1, True)

            def a_scores(h, q):
                if q == 0:
                    pe.wait_ge(k_doubled, 64 * h + 64)
                    pe.wait_ge(a_qk_lo.sem, a_qk_lo.after(h, 3))
                for c in range(2):
                    if q > 0:
                        pe.wait_ge(a_exp.sem, a_exp.after(h, 2 * (q - 1) + c))
                    elif not is_zero(h):
                        pe.wait_ge(a_exp.sem, a_exp.after(h, c) - 2)
                    for i in range(2):
                        for b in range(2):
                            mm = pe.matmul(ps[:, 2 + 2 * c + i, :], qs[:, c, q * P:(q + 1) * P],
                                           ks[:, c, b, i * HALF:(i + 1) * HALF], start=(b == 0), stop=(b == 1))
                    mm.then_inc(a_score.sem, 1)

            def a_round(h, k, srcs, first=False):
                if not first:
                    pe.wait_ge(a_tr_read.sem, a_tr_read.after(h, k) - 1)
                for n, src in enumerate(srcs):
                    mm = pe.transpose(ps[:, 6, n * P:(n + 1) * P], src, ident[:])
                mm.then_inc(a_tr.sem, 1)

            def mix_round(h, q, i):
                if i == 0:
                    pe.wait_ge(a_mix.sem, a_mix.after(h, 4 * q + 3))
                a_round(h, 2 + 2 * q + i, [am[q % 2][:, k * P:(k + 1) * P] for k in range(4 * i, 4 * i + 4)])

            def pv(h, n):
                pe.wait_ge(a_tr_read.sem, a_tr_read.after(h, 2 + 4 * n + 3))
                if n > 0:
                    pe.wait_ge(a_rs.sem, a_rs.after(h, 2 * (n - 1)))
                elif not is_zero(h):
                    pe.wait_ge(a_rs.sem, a_rs.after(h, 0) - 2)
                for k in range(KT):
                    mm = product(ps[:, 7, 0:2 * P], lambda a: va[:, a, k, :], lambda b: at_s[:, b, k, :],
                                 start=(k == 0), stop=(k == KT - 1))
                mm.then_inc(a_pv.sem, 1)

            def squares(h, n):
                pe.wait_ge(a_osq.sem, a_osq.after(h, n))
                pe.matmul(ps[:, 7, 2 * P:4 * P], ones[:], osq[:], start=True, stop=True).then_inc(a_ss.sem, 1)

            def a_head(h, first, last):
                def filler(n):
                    if not last:
                        proj_half(G_A, 4, h, n // 2, n % 2)

                a_scores(h, 0)
                filler(0)
                v_src = [vz[:, 0, c * P:(c + 1) * P] for c in range(ST)]
                if first:
                    pe.wait_ge(proj_read, 2 * (G_M + 8 * (MH - 1) + 7))
                a_round(h, 0, v_src[0:4], first=first)
                if not first:
                    squares(h - 1, 3)
                a_round(h, 1, v_src[4:8])
                for q in range(ST):
                    mix_round(h, q, 0)
                    if q + 1 < ST:
                        a_scores(h, q + 1)
                    mix_round(h, q, 1)
                    if q % 2 == 0 and q > 0:
                        squares(h, q // 2 - 1)
                    if q + 1 < ST:
                        filler(q + 1)
                    if q % 2 == 1:
                        pv(h, q // 2)

            a_head(0, True, False)
            with pe.Fori(1, AH - 1) as h:
                a_head(h, False, False)
            a_head(AH - 1, False, True)
            squares(AH - 1, 3)

            for n, base in ((0, G_FA), (1, G_FB)):
                with pe.Fori(0, KT) as d:
                    proj_half(base, 2, d, 0, 0)
                    proj_half(base, 2, d, 0, 1)
                    pe.wait_ge(h_loaded, 16 * 2 * (n + 1))
                    proj_half(base, 2, d, 1, 0, moving=hT)
                    proj_half(base, 2, d, 1, 1, moving=hT)

            def out_rounds(c, par):
                g = G_O + c
                for i in range(2):
                    pe.wait_ge(proj_read, 2 * g + i + 1)
                    if not isinstance(c, int):
                        pe.wait_ge(o_rows, 2 * c + i - 3)
                    for q in range(4):
                        t = 4 * i + q
                        mm = pe.transpose(ps[:, 2 + 2 * par + i, q * P:(q + 1) * P],
                                          outT[par][:, t * P:(t + 1) * P], ident[:])
                    mm.then_inc(o_tr, 1)

            pe.wait_ge(y_lo, KT)
            for c in range(2):
                proj_half(G_O, 2, 0, c, 0, moving=ys)
                proj_half(G_O, 2, 0, c, 1, moving=ys)
            out_rounds(0, 0)
            with pe.Fori(1, KT // 2) as c2:
                for par in range(2):
                    proj_half(G_O, 2, c2, par, 0, moving=ys)
                    proj_half(G_O, 2, c2, par, 1, moving=ys)
                    g = 2 * c2 + par - 1
                    for i in range(2):
                        pe.wait_ge(proj_read, 2 * (g + G_O) + i + 1)
                        if par == 0:
                            pe.wait_ge(o_rows, 2 * g + i - 1)
                        else:
                            pe.wait_ge(o_rows, 2 * g + i - 3)
                        for q in range(4):
                            t = 4 * i + q
                            mm = pe.transpose(ps[:, 2 + 2 * (1 - par) + i, q * P:(q + 1) * P],
                                              outT[1 - par][:, t * P:(t + 1) * P], ident[:])
                        mm.then_inc(o_tr, 1)
            c = KT - 1
            for i in range(2):
                pe.wait_ge(proj_read, 2 * (c + G_O) + i + 1)
                pe.wait_ge(o_rows, 2 * c + i - 3)
                for q in range(4):
                    t = 4 * i + q
                    mm = pe.transpose(ps[:, 4 + i, q * P:(q + 1) * P], outT[1][:, t * P:(t + 1) * P], ident[:])
                mm.then_inc(o_tr, 1)

        @block.vector
        def _(dve):
            def mark(ins, name):
                assert name in PREP_DVE
                ins.then_inc(prep_dve, 1)

            def after_step(name):
                dve.wait_ge(prep_dve, prep_dve_at(name))

            dve.memset(eps[:], EPS).then_inc(consts_set, 1)
            dve.memset(ones[:], 1.0).then_inc(consts_set, 1)
            dve.memset(rawa[:], 0.0).then_inc(consts_set, 1)
            dve.memset(r_reset[:], 1.0).then_inc(consts_set, 1)
            dve.memset(r_carry[:], 0.0).then_inc(consts_set, 1)
            dve.memset(r_mp[:], 0.0).then_inc(consts_set, 1)
            dve.memset(r_four[:], 0.0).then_inc(consts_set, 1)
            dve.wait_ge(consts_set, 4)
            dve.tensor_copy(ones_r[:], ones[:, 0:2]).then_inc(consts_set, 1)
            starts = r_reset[:].rearrange("m r (c j) -> m r c j", j=P)[:, :, :, 0]
            dve.memset(starts, 0.0).then_inc(consts_set, 1)

            def x_low(t):
                for i in range(2):
                    dve.wait_ge(x_hi, 2 * t + i + 1)
                    dst = slice(4 * i, 4 * i + 4), slice(t * P, (t + 1) * P)
                    dve.tensor_tensor(xs[:, 1, dst[0], dst[1]],
                                      ps[:, 2 + 2 * (t % 2) + i, :].rearrange("p (k s) -> p k s", k=4),
                                      xs[:, 0, dst[0], dst[1]].bitcast(F32), ALU.subtract).then_inc(x_lo, 1)

            dve.wait_ge(first_loaded, 16 * 2)
            for t in range(ST):
                dve.wait_ge(x_stat, 3 * t + 3)
                dve.scalar_tensor_tensor(xin[t % 2][:], xin[t % 2][:], xstat[:, 1, t:t + 1], pre_bc[:],
                                         ALU.mult, ALU.mult).then_inc(x_scaled, 1)
                if t > 0:
                    x_low(t - 1)
            dve.wait_ge(small_loaded, 16 * N_SMALL)
            mark(dve.tensor_copy(wgs[:, 0], wg[:]), "wg_hi")
            x_low(ST - 1)
            after_step("wg_hi")
            mark(dve.tensor_tensor(wgs[:, 1], wg[:], wgs[:, 0].bitcast(F32), ALU.subtract), "wg_lo")
            mark(dve.tensor_copy(ident_r[:], ident[:]), "ident_r")
            mark(dve.tensor_copy(mask_r[:], masks_f[:]), "mask_r")
            dve.wait_ge(prep_pe, 1)
            mark(dve.tensor_copy(vecs[:], ps[:, 6, 0:V_ROWS]), "vecs")
            after_step("vecs")
            conv_cols = vecs[:, V_CW:V_MG].rearrange("p (w q m) -> p q w m", q=2, m=MH)
            mark(dve.tensor_copy(hcv[:], conv_cols[:, :, :, 0]), "conv0")
            mark(dve.tensor_scalar(again[:], vecs[:, V_AG:V_AG + 1], 1.0 - LAM_INIT, None, ALU.mult), "again")
            mark(dve.tensor_copy(bmerge[:], vecs[:, V_BM:V_AG]), "bmerge")
            mark(dve.tensor_copy(pick[:], ident[0:MH, 0:MH].unsqueeze(2).to_broadcast([MH, MH, P])), "pick")
            lam2 = lamb[:].rearrange("p (j two) d -> p j two d", two=2)
            mark(dve.tensor_tensor(lamt[:], lam2[:, :, 0], lam2[:, :, 1], ALU.mult), "lam_products")
            after_step("lam_products")
            mark(dve.tensor_reduce(lams[:, 0:2], lamt[:], AX_X, ALU.add), "lam_sums")
            dve.wait_ge(prep_pe, 2)
            mark(dve.tensor_copy(gs[:], ps[:, 7, 0:ST * 16].rearrange("p (t g) -> p t g", t=ST)), "gates")

            def gate_rows(dst, kind, names):
                for r in range(2):
                    mark(dve.tensor_scalar(dst[:, r, :], ps[0:MH, 2 + 2 * r:4 + 2 * r, :].rearrange("m b j -> m (b j)"),
                                           gbias[:, 2 * r + kind:2 * r + kind + 1], None, ALU.add), names[r])

            def flat(t):
                return t[:].rearrange("m r j -> m (r j)")

            def chunks(t):
                return t[:].rearrange("m r (c j) -> m r c j", j=P)

            def conv_taps(hn, j):
                n = 7 * j
                g, _ = tile_no(0, 0, 0, j) if is_zero(hn) else tile_no(G_M, 8, hn - 1, 4 + j)
                if j == 1:
                    dve.wait_ge(conv_dve.sem, conv_dve.after(hn, 6))
                dve.wait_ge(proj_read, 2 * g + 2)
                dve.tensor_scalar(rawb[:], rawa[:, 0:S], hcv[:, j, 0:1], hcv[:, j, CONV:CONV + 1],
                                  ALU.mult, ALU.add).then_inc(conv_dve.sem, 1)
                for w in range(1, CONV):
                    dve.wait_ge(conv_dve.sem, conv_dve.after(hn, n + w - 1))
                    dve.scalar_tensor_tensor(rawb[:], rawa[:, w:w + S], hcv[:, j, w:w + 1], rawb[:],
                                             ALU.mult, ALU.add).then_inc(conv_dve.sem, 1)
                dve.wait_ge(conv_dve.sem, conv_dve.after(hn, n + CONV - 1))
                dve.scalar_tensor_tensor(qkf[:, j], rawb[:], -1.0, rawb[:], ALU.mult, ALU.min).then_inc(conv_dve.sem, 1)

            def conv_logsig(hn, j):
                dve.wait_ge(conv_act.sem, conv_act.after(hn, 3 * j + 1))
                dve.scalar_tensor_tensor(qkf[:, j], rawb[:], 0.0, qkf[:, j], ALU.min,
                                         ALU.subtract).then_inc(conv_dve.sem, 1)

            def conv_final(hn, j):
                dve.wait_ge(conv_act.sem, conv_act.after(hn, 3 * j + 2))
                dve.scalar_tensor_tensor(qkf[:, j], rawb[:], (MQK ** -0.5, 1.0)[j], qkf[:, j], ALU.mult,
                                         ALU.mult).then_inc(conv_dve.sem, 1)

            def qk_low(hn, j):
                dve.wait_ge(qk_hi.sem, qk_hi.after(hn, j))
                dve.tensor_tensor((qT, kT)[j][:, 1], qkf[:, j], (qT, kT)[j][:, 0].bitcast(F32),
                                  ALU.subtract).then_inc(qk_lo.sem, 1)

            def v_low(hn):
                for k in range(4):
                    e, i = divmod(k, 2)
                    dve.wait_ge(tr_hi.sem, tr_hi.after(hn, k))
                    dve.tensor_tensor(vS[:, 1, 4 * i:4 * i + 4, e * P:(e + 1) * P],
                                      ps[:, (7, 2)[k % 2], :].rearrange("p (c d) -> p c d", c=4),
                                      vS[:, 0, 4 * i:4 * i + 4, e * P:(e + 1) * P].bitcast(F32),
                                      ALU.subtract).then_inc(tr_read.sem, 1)

            dve.wait_ge(prep_pe, 3)
            gate_rows(r_i, 0, ("i_fw", "i_bw"))
            conv_taps(0, 0)
            dve.wait_ge(prep_pe, 4)
            gate_rows(r_f, 1, ("f_fw", "f_bw"))
            after_step("f_bw")
            mark(dve.scalar_tensor_tensor(flat(r_t), flat(r_f), -1.0, flat(r_f), ALU.mult, ALU.min), "abs_f")
            conv_logsig(0, 0)
            dve.wait_ge(prep_act, prep_act_at("ln_f"))
            mark(dve.scalar_tensor_tensor(flat(r_f), flat(r_f), 0.0, flat(r_t), ALU.min, ALU.subtract), "log_f")
            after_step("log_f")
            dve.wait_ge(consts_set, 9)
            mark(dve.tensor_tensor_scan(flat(r_t), flat(r_reset), flat(r_f), 0.0, ALU.mult, ALU.add), "a")
            after_step("a")
            mark(dve.tensor_tensor(flat(r_i), flat(r_i), flat(r_t), ALU.subtract), "b")
            mark(dve.tensor_copy(chunks(r_carry)[:, :, 1:NC, 0], chunks(r_t)[:, :, 0:NC - 1, P - 1]), "carry")
            after_step("carry")
            for r, name in enumerate(("max_fw", "max_bw")):
                mark(dve.tensor_tensor_scan(r_m[:, r], r_carry[:, r], r_i[:, r], 0.0, ALU.add, ALU.max), name)
            after_step("max_bw")
            a_end, m_end = chunks(r_t)[:, :, :, P - 1], chunks(r_m)[:, :, :, P - 1]
            mark(dve.tensor_tensor(r_mp[:, :, 1:NC], a_end[:, :, 0:NC - 1], m_end[:, :, 0:NC - 1], ALU.add), "m_prev")
            after_step("m_prev")
            mark(dve.tensor_tensor(r_dec[:], r_mp[:], m_end, ALU.subtract), "decay")

            def four(q):
                return r_four[32 * q:32 * q + MH]

            wide = [MH, 2, NC, P]
            mark(dve.tensor_scalar(four(Q_NEGM), r_m[:], -1.0, None, ALU.mult), "neg_m")
            mark(dve.tensor_copy(four(Q_B), r_i[:]), "b_copy")
            mark(dve.tensor_tensor(four(Q_WINTER).rearrange("m r (c j) -> m r c j", j=P),
                                   r_mp[:].unsqueeze(3).to_broadcast(wide), chunks(r_m), ALU.subtract), "w_inter")
            mark(dve.tensor_tensor(four(Q_EMJ), r_t[:], r_m[:], ALU.add), "a_plus_m")
            mark(dve.tensor_tensor(chunks(r_wk), chunks(r_i), m_end.unsqueeze(3).to_broadcast(wide),
                                   ALU.subtract), "w_k")
            dve.wait_ge(prep_act, prep_act_at("lam_exp"))
            mark(dve.scalar_tensor_tensor(neglam[:], lams[:, 3:4], -LAM_INIT, lams[:, 2:3], ALU.add,
                                          ALU.subtract), "neglam")
            conv_final(0, 0)
            conv_taps(0, 1)
            dve.wait_ge(prep_pe, 6)

            def col_banks(b):
                return ps[:, b:b + 2, :].rearrange("p b (c q x) -> p (b c) q x", c=4, q=4)[:, :, :, 0:MH]

            def wk_cols(r):
                n = NC * MH
                return ps[:, 6, 256 + r * n:256 + (r + 1) * n].rearrange("p (c m) -> p c m", c=NC)

            mark(dve.tensor_copy(col[:, 0:NC, 0:4, :], col_banks(2)), "col_fw")
            mark(dve.tensor_copy(colrev[:, :, 0:4, :], col_banks(4)), "col_rev")
            mark(dve.tensor_copy(col[:, 0:NC, Q_WK, :], wk_cols(0)), "wk_fw")
            mark(dve.tensor_copy(colrev[:, :, Q_WK, :], wk_cols(1)), "wk_rev")
            mark(dve.tensor_copy(decay[:], ps[:, 7, 256:256 + 16 * MH].rearrange("p (m c) -> p m c", m=MH)), "decay_all")
            dve.wait_ge(prep_pe, 7)
            mark(dve.tensor_copy(col[:, NC:2 * NC], ps[:, 7, 0:NC * 5 * MH].rearrange(
                "p (c q m) -> p c q m", c=NC, q=5)), "col_bw")
            after_step("col_bw")
            conv_logsig(0, 1)
            conv_final(0, 1)
            qk_low(0, 0)
            qk_low(0, 1)
            v_low(0)

            def gate_abs(h, e, part):
                g, _ = tile_no(G_M, 8, h, 2 * e + part)
                dve.wait_ge(proj_read, 2 * g + 2)
                src = rawb[:] if part == 0 else zg[:, e]
                if part == 0 and e == 1:
                    dve.wait_ge(gate_dve.sem, gate_dve.after(h, 5))
                dve.scalar_tensor_tensor(ab[:, part], src, -1.0, src, ALU.mult, ALU.min).then_inc(gate_dve.sem, 1)

            def gate_logsig(h, e, part):
                n = 6 * e + 2 * part
                dve.wait_ge(gate_act.sem, gate_act.after(h, 5 * e + 2 * part + 1))
                src = rawb[:] if part == 0 else zg[:, e]
                dve.scalar_tensor_tensor(ab[:, part], src, 0.0, ab[:, part], ALU.min,
                                         ALU.subtract).then_inc(gate_dve.sem, 1)
                if part == 1:
                    dve.wait_ge(gate_dve.sem, gate_dve.after(h, n + 1))
                    dve.tensor_tensor(ab[:, 1], ab[:, 0], ab[:, 1], ALU.add).then_inc(gate_dve.sem, 1)

            def gate_final(h, e):
                dve.wait_ge(gate_act.sem, gate_act.after(h, 5 * e + 4))
                dve.scalar_tensor_tensor(zg[:, e], zg[:, e], hg[:, e:e + 1], ab[:, 1], ALU.mult,
                                         ALU.mult).then_inc(gate_dve.sem, 1)

            def chunk(r, t):
                return t if r == 0 else NC - 1 - t

            def diagonals(h, t):
                if t == 0:
                    dve.wait_ge(hcols.sem, hcols.after(h, 0))
                else:
                    dve.wait_ge(score_done.sem, score_done.after(h, t - 1))
                for r in range(2):
                    d = dve.tensor_scalar(dg[:, r], ident[:], hc[:, 8 * r + t, Q_NEGM:Q_NEGM + 1], None, ALU.mult)
                d.then_inc(diag_done.sem, 1)

            def m_step(h, t):
                if t < NC - 1:
                    diagonals(h, t + 1)
                dve.wait_ge(w_done.sem, w_done.after(h, t))
                if t > 0:
                    dve.wait_ge(ptlo_done.sem, ptlo_done.after(h, t - 1))
                dve.tensor_tensor(ptf[:], ps[:, 2, 0:2 * P].rearrange("p (r j) -> p r j", r=2), wt[:],
                                  ALU.mult).then_inc(ptf_done.sem, 1)
                dve.wait_ge(pthi_done.sem, pthi_done.after(h, t))
                dve.tensor_tensor(pt[:, 1], ptf[:], pt[:, 0].bitcast(F32), ALU.subtract).then_inc(ptlo_done.sem, 1)
                if t < NC - 1:
                    dve.wait_ge(kwhi_done.sem, kwhi_done.after(h, t))
                    for r in range(2):
                        lo = dve.scalar_tensor_tensor(kw[:, 1, r], kseq[:, chunk(r, t)], hc[:, 8 * r + t, Q_WK:Q_WK + 1],
                                                      kw[:, 0, r].bitcast(F32), ALU.mult, ALU.subtract)
                    lo.then_inc(kwlo_done.sem, 1)
                if t == 2:
                    gate_abs(h, 0, 0)
                elif t == 3:
                    gate_logsig(h, 0, 0)
                elif t == 4:
                    gate_abs(h, 0, 1)
                elif t == 5:
                    gate_logsig(h, 0, 1)
                elif t == 6:
                    gate_final(h, 0)
                    gate_abs(h, 1, 0)
                elif t == 7:
                    gate_logsig(h, 1, 0)
                dve.wait_ge(intra_done.sem, intra_done.after(h, t))
                intra = ps[:, 4, :].rearrange("p (r e) -> p r e", r=2)
                if t > 0:
                    dve.wait_ge(intersc_done.sem, intersc_done.after(h, t - 1))
                    dve.tensor_tensor(num[:], intra, num[:], ALU.add).then_inc(num_done.sem, 1)
                else:
                    dve.tensor_copy(num[:], intra).then_inc(num_done.sem, 1)
                if t < NC - 1:
                    dve.wait_ge(upd_done.sem, upd_done.after(h, t))
                    upd = ps[:, 6, :].rearrange("p (r e) -> p r e", r=2)
                    nup = ps[:, 7, 8:12].rearrange("p (r two) -> p r two", r=2)
                    if t == 0:
                        dve.tensor_copy(cf[:, :, 0:MV], upd)
                        d = dve.tensor_copy(cf[:, :, MV:MV + 2], nup)
                    else:
                        dve.wait_ge(clo_done.sem, clo_done.after(h, t - 1))
                        for r in range(2):
                            dve.scalar_tensor_tensor(cf[:, r, 0:MV], cf[:, r, 0:MV], hd[:, 8 * r + t:8 * r + t + 1],
                                                     upd[:, r], ALU.mult, ALU.add)
                            d = dve.scalar_tensor_tensor(cf[:, r, MV:MV + 2], cf[:, r, MV:MV + 2],
                                                         hd[:, 8 * r + t:8 * r + t + 1], nup[:, r], ALU.mult, ALU.add)
                    d.then_inc(state_done.sem, 1)
                dve.tensor_copy(dsm[:, 0], ps[:, 7, 0:4].rearrange("p (r two) -> p r two", two=2)[:, :, 0]) \
                    .then_inc(den_chain.sem, 1)
                dve.wait_ge(den_chain.sem, den_chain.after(h, 5 * t))
                if t > 0:
                    for r in range(2):
                        d = dve.scalar_tensor_tensor(dsm[:, 1, r:r + 1], ps[:, 7, 4 + 2 * r:5 + 2 * r],
                                                     hc[:, 8 * r + t, Q_WINTER:Q_WINTER + 1], dsm[:, 0, r:r + 1],
                                                     ALU.mult, ALU.add)
                    d.then_inc(den_chain.sem, 1)
                else:
                    dve.tensor_copy(dsm[:, 1], dsm[:, 0]).then_inc(den_chain.sem, 1)
                dve.wait_ge(den_chain.sem, den_chain.after(h, 5 * t + 1))
                dve.tensor_scalar(dsm[:, 0], dsm[:, 1], -1.0, None, ALU.mult).then_inc(den_chain.sem, 1)
                dve.wait_ge(den_chain.sem, den_chain.after(h, 5 * t + 2))
                for r in range(2):
                    d = dve.scalar_tensor_tensor(dsm[:, 2, r:r + 1], dsm[:, 1, r:r + 1],
                                                 hc[:, 8 * r + t, Q_EMJ:Q_EMJ + 1], dsm[:, 0, r:r + 1],
                                                 ALU.max, ALU.max)
                d.then_inc(den_chain.sem, 1)
                dve.wait_ge(den_chain.sem, den_chain.after(h, 5 * t + 3))
                dve.reciprocal(dsm[:, 3], dsm[:, 2]).then_inc(den_chain.sem, 1)
                if t < NC - 1:
                    dve.wait_ge(chi_done.sem, chi_done.after(h, t))
                    dve.tensor_tensor(cs[:, 1], cf[:], cs[:, 0].bitcast(F32), ALU.subtract).then_inc(clo_done.sem, 1)
                dve.wait_ge(den_chain.sem, den_chain.after(h, 5 * t + 4))
                dve.wait_ge(num_done.sem, num_done.after(h, t))
                if t > 0:
                    dve.wait_ge(h_done.sem, h_done.after(h, t - 1))
                for r in range(2):
                    c = chunk(r, t)
                    if t < NC // 2:
                        d = dve.tensor_scalar(hacc[:, c], num[:, r], dsm[:, 3, r:r + 1], None, ALU.mult)
                    else:
                        d = dve.scalar_tensor_tensor(hacc[:, c], num[:, r], dsm[:, 3, r:r + 1], hacc[:, c],
                                                     ALU.mult, ALU.add)
                d.then_inc(h_done.sem, 1)

            def h_out(h):
                for k in range(4):
                    e, i = divmod(k, 2)
                    dve.wait_ge(tr_done.sem, tr_done.after(h, k))
                    if k > 0:
                        dve.wait_ge(hsplit_done.sem, hsplit_done.after(h, k - 1))
                    dve.tensor_tensor(hst[:], ps[:, (7, 2)[k % 2], :], zg[:, e, i * HALF:(i + 1) * HALF],
                                      ALU.mult).then_inc(tr_read.sem, 1)
                    dve.wait_ge(hsp_hi.sem, hsp_hi.after(h, k))
                    dve.tensor_tensor(hsp[:, 1], hst[:], hsp[:, 0].bitcast(F32), ALU.subtract) \
                        .then_inc(hsplit_done.sem, 1)

            def shuffle(hh, n):
                swap = [(i + ROPE // 2) % ROPE if i < ROPE else i for i in range(32)]
                for half in range(2):
                    cols = slice(half * HALF, (half + 1) * HALF)
                    if is_zero(hh):
                        g, _ = tile_no(G_M, 8, MH - 1, 4 + n // 2)
                    else:
                        g, _ = tile_no(G_A, 4, hh - 1, n // 2)
                    dve.wait_ge(proj_read, 2 * g + half + 1)
                    dve.sem_inc(step_begun, 1)
                    dve.stream_shuffle((rawa, rawb)[n // 2][:, cols], qkf[:, n // 2, cols], swap).then_inc(shuf_done, 1)

            own = (slice(0, AD), slice(AD, P))

            def k_low(hh):
                for c in range(2):
                    dve.wait_ge(a_qk_hi.sem, a_qk_hi.after(hh, c))
                    dve.tensor_tensor(ks[own[c], c, 1], qkf[own[c], 1], ks[own[c], c, 0].bitcast(F32),
                                      ALU.subtract).then_inc(a_qk_lo.sem, 1)

            def q_low(hh):
                for c in range(2):
                    dve.wait_ge(a_qk_hi.sem, a_qk_hi.after(hh, 2 + c))
                    dve.tensor_tensor(qs[own[1 - c], c], qkf[own[c], 0], qs[own[c], c].bitcast(F32),
                                      ALU.subtract).then_inc(a_qk_lo.sem, 1)

            def m_head(h, last):
                dve.tensor_copy(hc[:], col[:, :, :, bass.ds(h, 1)].rearrange("p c q one -> p c (q one)")) \
                    .then_inc(hcols.sem, 1)
                dve.tensor_copy(hd[:], decay[:, bass.ds(h, 1), :].rearrange("p one c -> p (one c)")).then_inc(hcols.sem, 1)
                dve.tensor_copy(hg[:], vecs[:, bass.ds(V_MG + 2 * h, 2)]).then_inc(hcols.sem, 1)
                nxt = (h + 1) if not last else 0
                dve.tensor_copy(hcv[:], conv_cols[:, :, :, bass.ds(nxt, 1)].rearrange("p q w one -> p q (w one)")) \
                    .then_inc(hcols.sem, 1)
                diagonals(h, 0)
                for t in range(NC):
                    m_step(h, t)
                gate_abs(h, 1, 1)
                gate_logsig(h, 1, 1)
                if not last:
                    conv_taps(h + 1, 0)
                else:
                    shuffle(0, 0)
                gate_final(h, 1)
                dve.wait_ge(hs_act.sem, hs_act.after(h, 2))
                for c in range(NC):
                    d = dve.tensor_scalar(hacc[:, c], hacc[:, c], hstat[:, 1, c:c + 1], None, ALU.mult)
                d.then_inc(hs_done.sem, 1)
                if not last:
                    conv_logsig(h + 1, 0)
                    conv_final(h + 1, 0)
                    conv_taps(h + 1, 1)
                else:
                    shuffle(0, 2)
                h_out(h)
                if not last:
                    conv_logsig(h + 1, 1)
                    conv_final(h + 1, 1)
                    qk_low(h + 1, 0)
                    qk_low(h + 1, 1)
                    v_low(h + 1)
                else:
                    k_low(0)
                    q_low(0)

            with dve.Fori(0, MH - 1) as h:
                m_head(h, False)
            m_head(MH - 1, True)

            def mix(h, q):
                b = q % 2
                dve.wait_ge(a_exp.sem, a_exp.after(h, 2 * q + 1))
                dve.reciprocal(rden[:, 0], den[:, b]).then_inc(a_mix.sem, 1)
                dve.wait_ge(a_mix.sem, a_mix.after(h, 4 * q))
                dve.tensor_scalar(rden[:, 1, 0:1], rden[:, 0, 1:2], neglam[:], None, ALU.mult).then_inc(a_mix.sem, 1)
                if q >= 2:
                    dve.wait_ge(a_tr.sem, a_tr.after(h, 2 + 2 * (q - 2) + 1))
                dve.tensor_scalar(am[b][:], pr[:, 0], rden[:, 0, 0:1], None, ALU.mult).then_inc(a_mix.sem, 1)
                dve.wait_ge(a_mix.sem, a_mix.after(h, 4 * q + 2))
                dve.scalar_tensor_tensor(am[b][:], pr[:, 1], rden[:, 1, 0:1], am[b][:], ALU.mult,
                                         ALU.add).then_inc(a_mix.sem, 1)

            def maxima(h, q):
                for c in range(2):
                    dve.wait_ge(a_score.sem, a_score.after(h, 2 * q + c))
                    dve.tensor_reduce(nmax[:, q % 2, c:c + 1], ps[:, 2 + 2 * c:4 + 2 * c, :].rearrange("p b k -> p (b k)"),
                                      AX_X, ALU.max, negate=True).then_inc(a_max.sem, 1)

            def a_low_round(h, k, dst):
                dve.wait_ge(a_tr_hi.sem, a_tr_hi.after(h, k))
                dve.tensor_tensor(dst(1), ps[:, 6, :].rearrange("p (k s) -> p k s", k=4), dst(0).bitcast(F32),
                                  ALU.subtract).then_inc(a_tr_read.sem, 1)

            def v_dst(i):
                return lambda p: va[:, p, 4 * i:4 * i + 4, :]

            def at_dst(q, i):
                return lambda p: at_s[:, p, 4 * i:4 * i + 4, (q % 2) * P:(q % 2 + 1) * P]

            def o_square(h, n):
                dve.wait_ge(a_of.sem, a_of.after(h, n))
                dve.tensor_tensor(osq[:], of[:], of[:], ALU.mult).then_inc(a_osq.sem, 1)

            def o_out_gate(h, n):
                dve.wait_ge(a_rs.sem, a_rs.after(h, 2 * n + 1))
                if n > 0:
                    dve.wait_ge(a_olo.sem, a_olo.after(h, n - 1))
                dve.tensor_tensor(ost[:], of[:], ors[:], ALU.mult).then_inc(a_ost.sem, 1)
                dve.wait_ge(a_ost.sem, a_ost.after(h, 2 * n))
                dve.tensor_tensor(ost[:], ost[:], ga[:, 2 * n * P:2 * (n + 1) * P], ALU.mult).then_inc(a_ost.sem, 1)
                dve.wait_ge(a_ohi.sem, a_ohi.after(h, n))
                dve.tensor_tensor(osp[:, 1], ost[:], osp[:, 0].bitcast(F32), ALU.subtract).then_inc(a_olo.sem, 1)

            def a_head(h, first, last):
                maxima(h, 0)
                dve.scalar_tensor_tensor(aw[:], vz[:, 1], -1.0, vz[:, 1], ALU.mult, ALU.min) \
                    .then_inc(a_gate_dve.sem, 1)
                mix(h, 0)
                a_low_round(h, 0, v_dst(0))
                if not first:
                    o_out_gate(h - 1, 3)
                a_low_round(h, 1, v_dst(1))
                dve.wait_ge(a_gate_act.sem, a_gate_act.after(h, 1))
                dve.scalar_tensor_tensor(aw[:], vz[:, 1], 0.0, aw[:], ALU.min, ALU.subtract) \
                    .then_inc(a_gate_dve.sem, 1)
                for q in range(ST):
                    a_low_round(h, 2 + 2 * q, at_dst(q, 0))
                    if q + 1 < ST:
                        maxima(h, q + 1)
                    a_low_round(h, 2 + 2 * q + 1, at_dst(q, 1))
                    if q + 1 < ST:
                        mix(h, q + 1)
                    if q == 0:
                        dve.wait_ge(a_gate_act.sem, a_gate_act.after(h, 2))
                        dve.scalar_tensor_tensor(ga[:], vz[:, 1], again[:], aw[:], ALU.mult, ALU.mult) \
                            .then_inc(a_gate_dve.sem, 1)
                    if q % 2 == 0 and q > 0:
                        o_out_gate(h, q // 2 - 1)
                    if not last and q in (1, 3):
                        shuffle(h + 1, q - 1)
                    if not last and q == 6:
                        k_low(h + 1)
                    if not last and q == 7:
                        q_low(h + 1)
                    if q % 2 == 1:
                        o_square(h, q // 2)

            a_head(0, True, False)
            with dve.Fori(1, AH - 1) as h:
                a_head(h, False, False)
            a_head(AH - 1, False, True)
            o_out_gate(AH - 1, 3)

            def merge(n, base):
                with dve.Fori(0, KT) as d:
                    at = (4 + n) * d + 4 * KT * n
                    dve.tensor_copy(fbias[:], bmerge[:, bass.ds(KT * n + d, 1)]).then_inc(f_dve, 1)
                    g, _ = tile_no(base, 2, d, 0)
                    dve.wait_ge(proj_read, 2 * g + 2)
                    dve.scalar_tensor_tensor(fw[:], fz[:], -1.0, fz[:], ALU.mult, ALU.min).then_inc(f_dve, 1)
                    dve.wait_ge(f_act, 3 * (KT * n + d) + 2)
                    dve.scalar_tensor_tensor(fw[:], fz[:], 0.0, fw[:], ALU.min, ALU.subtract).then_inc(f_dve, 1)
                    dve.wait_ge(proj_read, 2 * g + 4)
                    dve.wait_ge(f_act, 3 * (KT * n + d) + 3)
                    yd = ya[:, bass.ds(d, 1), :].rearrange("p one s -> p (one s)")
                    if n == 0:
                        dve.tensor_tensor(yd, fw[:], fb[:], ALU.mult).then_inc(f_dve, 1)
                    else:
                        dve.tensor_tensor(fw[:], fw[:], fb[:], ALU.mult).then_inc(f_dve, 1)
                        dve.wait_ge(f_dve, at + 4)
                        dve.tensor_tensor(yd, yd, fw[:], ALU.add).then_inc(f_dve, 1)

            merge(0, G_FA)
            merge(1, G_FB)
            for k in range(KT):
                dve.wait_ge(y_hi, k + 1)
                dve.tensor_tensor(ys[:, 1, k], ya[:, k], ys[:, 0, k].bitcast(F32), ALU.subtract).then_inc(y_lo, 1)

            def rows(c, par):
                for i in range(2):
                    dve.wait_ge(o_tr, 2 * c + i + 1)
                    dst = orow[:, 4 * i:4 * i + 4, bass.ds(c * P, P)]
                    dve.tensor_copy(dst, ps[:, 2 + 2 * par + i, :].rearrange("p (t s) -> p t s", t=4)).then_inc(o_rows, 1)

            with dve.Fori(0, KT // 2) as c2:
                for par in range(2):
                    rows(2 * c2 + par, par)
            dve.wait_ge(post_loaded, 16)
            for t in range(ST):
                dve.wait_ge(o_stat, 3 * t + 3)
                dve.scalar_tensor_tensor(orow[:, t], orow[:, t], tail_stat[:, 2, t:t + 1], post_bc[:], ALU.mult,
                                         ALU.mult).then_inc(o_out, 1)
                dve.wait_ge(res_loaded[t % 2], 16 * (t // 2 + 1))
                dve.wait_ge(o_out, 2 * t + 1)
                dve.tensor_tensor(orow[:, t], orow[:, t], xres[t % 2][:], ALU.add).then_inc(o_out, 1)

        @block.scalar
        def _(act):
            def mark(ins, name):
                assert name in PREP_ACT
                ins.then_inc(prep_act, 1)

            def read_half(base, per_head, h, j, half, dst, scale=1.0, bias=None):
                g, _ = tile_no(base, per_head, h, j)
                act.wait_ge(proj_done, 2 * g + half + 1)
                if bias is None:
                    act.activation(dst, ps[:, half, :], ACT.Copy, scale=scale).then_inc(proj_read, 1)
                else:
                    act.activation(dst, ps[:, half, :], ACT.Identity, bias=bias).then_inc(proj_read, 1)

            def exp_ln(t, sig, waits_own):
                act.activation(t, t, ACT.Exp).then_inc(sig, 1)
                act.wait_ge(sig, waits_own)
                act.activation(t, t, ACT.Ln, bias=1.0).then_inc(sig, 1)

            act.preload_act_table_set("natural_log_exp_and_others")
            act.sem_inc(spilled[0], 32)
            act.sem_inc(spilled[1], 32)

            def x_high(t):
                for i in range(2):
                    act.wait_ge(x_tr, 2 * t + i + 1)
                    act.activation(xs[:, 0, 4 * i:4 * i + 4, t * P:(t + 1) * P],
                                   ps[:, 2 + 2 * (t % 2) + i, :].rearrange("p (k s) -> p k s", k=4),
                                   ACT.Copy).then_inc(x_hi, 1)

            act.wait_ge(consts_set, 1)
            for t in range(ST):
                act.wait_ge(x_loaded[t % 2], 16 * (t // 2 + 1))
                act.activation(rawb[:], xin[t % 2][:], ACT.Square, accum_out=xstat[:, 0, t:t + 1]).then_inc(x_stat, 1)
                act.wait_ge(x_stat, 3 * t + 1)
                act.activation(xstat[:, 1, t:t + 1], xstat[:, 0, t:t + 1], ACT.Ln, bias=eps[:], scale=1.0 / D) \
                    .then_inc(x_stat, 1)
                act.wait_ge(x_stat, 3 * t + 2)
                act.activation(xstat[:, 1, t:t + 1], xstat[:, 1, t:t + 1], ACT.Exp, scale=-0.5).then_inc(x_stat, 1)
                if t > 0:
                    x_high(t - 1)
            x_high(ST - 1)

            def conv_exp_ln(hn, j):
                act.wait_ge(conv_dve.sem, conv_dve.after(hn, 7 * j + CONV))
                exp_ln(qkf[:, j], conv_act.sem, conv_act.after(hn, 3 * j))

            def conv_exp(hn, j):
                act.wait_ge(conv_dve.sem, conv_dve.after(hn, 7 * j + 5))
                act.activation(qkf[:, j], qkf[:, j], ACT.Exp).then_inc(conv_act.sem, 1)

            def qk_high(hn, j):
                act.wait_ge(conv_dve.sem, conv_dve.after(hn, 7 * j + 6))
                act.activation((qT, kT)[j][:, 0], qkf[:, j], ACT.Copy).then_inc(qk_hi.sem, 1)

            def read_conv(base, per_head, h, hn, j, tile):
                if j == 1:
                    act.wait_ge(conv_dve.sem, conv_dve.after(hn, CONV - 1))
                for half in range(2):
                    at = CONV // 2 + half * HALF
                    read_half(base, per_head, h, tile, half, rawa[:, at:at + HALF])

            def kv_high(h):
                for i in range(2):
                    act.wait_ge(tr_done.sem, tr_done.after(h, 4 + i))
                    act.activation(kseq[:, 4 * i:4 * i + 4], ps[:, (7, 2)[i], :].rearrange("p (c d) -> p c d", c=4),
                                   ACT.Copy).then_inc(tr_read.sem, 1)
                for k in range(4):
                    e, i = divmod(k, 2)
                    act.wait_ge(tr_done.sem, tr_done.after(h, 6 + k))
                    act.activation(vS[:, 0, 4 * i:4 * i + 4, e * P:(e + 1) * P],
                                   ps[:, (7, 2)[k % 2], :].rearrange("p (c d) -> p c d", c=4),
                                   ACT.Copy).then_inc(tr_hi.sem, 1)

            act.wait_ge(consts_set, 3)
            read_conv(0, 0, 0, 0, 0, 0)
            conv_exp_ln(0, 0)
            read_conv(0, 0, 0, 0, 1, 1)
            act.wait_ge(prep_dve, prep_dve_at("abs_f"))
            t_flat = r_t[:].rearrange("m r j -> m (r j)")
            mark(act.activation(t_flat, t_flat, ACT.Exp), "exp_f")
            act.wait_ge(prep_act, prep_act_at("exp_f"))
            mark(act.activation(t_flat, t_flat, ACT.Ln, bias=1.0), "ln_f")
            conv_exp(0, 0)
            for e in range(2):
                for half in range(2):
                    read_half(0, 0, 0, 2 + e, half, vz[:, e, half * HALF:(half + 1) * HALF])
            mark(act.activation(lams[:, 2:4], lams[:, 0:2], ACT.Exp), "lam_exp")
            act.wait_ge(prep_dve, prep_dve_at("decay"))
            mark(act.activation(r_dec[:], r_dec[:], ACT.Exp), "decay")
            act.wait_ge(prep_dve, prep_dve_at("w_inter"))
            w_row, e_row = r_four[64:64 + MH], r_four[96:96 + MH]
            mark(act.activation(w_row, w_row, ACT.Exp), "w_inter")
            act.wait_ge(prep_dve, prep_dve_at("a_plus_m"))
            mark(act.activation(e_row, e_row, ACT.Exp, scale=-1.0), "emj")
            act.wait_ge(prep_dve, prep_dve_at("w_k"))
            mark(act.activation(r_wk[:], r_wk[:], ACT.Exp), "w_k")
            conv_exp_ln(0, 1)
            conv_exp(0, 1)
            qk_high(0, 0)
            qk_high(0, 1)
            kv_high(-1)

            def chunk(r, t):
                return t if r == 0 else NC - 1 - t

            def gate_exp_ln(h, e, part):
                n = 6 * e + (0, 2)[part]
                act.wait_ge(gate_dve.sem, gate_dve.after(h, n))
                exp_ln(ab[:, part], gate_act.sem, gate_act.after(h, 5 * e + 2 * part))

            def gate_exp(h, e):
                act.wait_ge(gate_dve.sem, gate_dve.after(h, 6 * e + 4))
                act.activation(ab[:, 1], ab[:, 1], ACT.Exp).then_inc(gate_act.sem, 1)

            def m_step(h, t):
                act.wait_ge(score_done.sem, score_done.after(h, t))
                if t == 0:
                    act.wait_ge(hcols.sem, hcols.after(h, 0))
                else:
                    act.wait_ge(ptf_done.sem, ptf_done.after(h, t - 1))
                for r in range(2):
                    a = act.activation(wt[:, r], ps[:, 3, r * P:(r + 1) * P], ACT.Exp,
                                       bias=hc[:, 8 * r + t, Q_B:Q_B + 1])
                a.then_inc(w_done.sem, 1)
                act.wait_ge(ptf_done.sem, ptf_done.after(h, t))
                if t > 0:
                    act.wait_ge(intra_done.sem, intra_done.after(h, t - 1))
                act.activation(pt[:, 0], ptf[:], ACT.Copy).then_inc(pthi_done.sem, 1)
                if t < NC - 1:
                    if t > 0:
                        act.wait_ge(upd_done.sem, upd_done.after(h, t - 1))
                    else:
                        act.wait_ge(tr_read.sem, tr_read.after(h - 1, 5))
                    for r in range(2):
                        a = act.activation(kw[:, 0, r], kseq[:, chunk(r, t)], ACT.Copy,
                                           scale=hc[:, 8 * r + t, Q_WK:Q_WK + 1])
                    a.then_inc(kwhi_done.sem, 1)
                if t == 3:
                    gate_exp_ln(h, 0, 0)
                elif t == 5:
                    gate_exp_ln(h, 0, 1)
                elif t == 6:
                    gate_exp(h, 0)
                elif t == 7:
                    gate_exp_ln(h, 1, 0)
                j, half = divmod(t, 2)
                cols = slice(half * HALF, (half + 1) * HALF)
                if t == 4:
                    act.wait_ge(gate_dve.sem, gate_dve.after(h, 1))
                read_half(G_M, 8, h, j, half, rawb[:, cols] if j % 2 == 0 else zg[:, j // 2, cols])
                if t > 0:
                    act.wait_ge(inter_done.sem, inter_done.after(h, t - 1))
                    act.wait_ge(h_done.sem, h_done.after(h, t - 1))
                    for r in range(2):
                        a = act.activation(num[:, r], ps[:, 5, r * MV:(r + 1) * MV], ACT.Copy,
                                           scale=hc[:, 8 * r + t, Q_WINTER:Q_WINTER + 1])
                    a.then_inc(intersc_done.sem, 1)
                if t < NC - 1:
                    act.wait_ge(state_done.sem, state_done.after(h, t))
                    act.activation(cs[:, 0], cf[:], ACT.Copy).then_inc(chi_done.sem, 1)

            own = (slice(0, AD), slice(AD, P))

            def k_high(hh):
                act.wait_ge(rope_done, 3 * (4 * hh + 3) + 3)
                for c in range(2):
                    act.activation(ks[own[c], c, 0], qkf[own[c], 1], ACT.Copy).then_inc(a_qk_hi.sem, 1)
                for c in range(2):
                    act.wait_ge(a_qk_hi.sem, a_qk_hi.after(hh, c))
                    k_double(c, 0)

            def k_double(c, part):
                act.dma_start(ks[own[1 - c], c, part].bitcast(F32), ks[own[c], c, part].bitcast(F32)) \
                    .then_inc(k_doubled, 16)

            def q_high(hh):
                for c in range(2):
                    act.activation(qs[own[c], c], qkf[own[c], 0], ACT.Copy).then_inc(a_qk_hi.sem, 1)

            def k_low_double(hh):
                for c in range(2):
                    act.wait_ge(a_qk_lo.sem, a_qk_lo.after(hh, c))
                    k_double(c, 1)

            def read_rope(base, per_head, h, hh, n, half):
                if half == 0 and not is_zero(hh):
                    act.wait_ge(a_qk_lo.sem, a_qk_lo.after(hh, 3) - 4)
                read_half(base, per_head, h, (4 if is_zero(hh) else 0) + n // 2, half,
                          qkf[:, n // 2, half * HALF:(half + 1) * HALF], scale=(AD ** -0.5 if n == 0 else 1.0))

            def m_head(h, last):
                for t in range(NC):
                    m_step(h, t)
                gate_exp_ln(h, 1, 1)
                if not last:
                    read_conv(G_M, 8, h, h + 1, 0, 4)
                else:
                    for half in range(2):
                        read_rope(G_M, 8, h, 0, 0, half)
                gate_exp(h, 1)
                act.wait_ge(h_done.sem, h_done.after(h, NC - 1))
                junk = kseq[:].rearrange("p c d -> p (c d)").bitcast(mybir.dt.bfloat16)
                for c in range(NC):
                    a = act.activation(junk[:, c * MV:(c + 1) * MV], hacc[:, c], ACT.Square,
                                       accum_out=hstat[:, 0, c:c + 1])
                a.then_inc(hs_act.sem, 1)
                act.wait_ge(hs_act.sem, hs_act.after(h, 0))
                act.activation(hstat[:, 1], hstat[:, 0], ACT.Ln, bias=eps[:], scale=1.0 / MV).then_inc(hs_act.sem, 1)
                act.wait_ge(hs_act.sem, hs_act.after(h, 1))
                act.activation(hstat[:, 1], hstat[:, 1], ACT.Exp, scale=-0.5).then_inc(hs_act.sem, 1)
                if not last:
                    conv_exp_ln(h + 1, 0)
                    conv_exp(h + 1, 0)
                    read_conv(G_M, 8, h, h + 1, 1, 5)
                else:
                    for half in range(2):
                        read_rope(G_M, 8, h, 0, 2, half)
                for k in range(4):
                    e, i = divmod(k, 2)
                    act.wait_ge(tr_read.sem, tr_read.after(h, k))
                    act.wait_ge(spilled[0], 32 * (4 * h + (k + 1)))
                    act.activation(hsp[:, 0], hst[:], ACT.Copy).then_inc(hsp_hi.sem, 1)
                    act.wait_ge(hsplit_done.sem, hsplit_done.after(h, k))
                    for p in range(2):
                        act.dma_start(spill_m[p, bass.ds(2 * h + e, 1), :, i * HALF:(i + 1) * HALF].rearrange(
                            "one p s -> (one p) s"), hsp[:, p].bitcast(F32)).then_inc(spilled[0], 16)
                if not last:
                    conv_exp_ln(h + 1, 1)
                    for e in range(2):
                        for half in range(2):
                            read_half(G_M, 8, h, 6 + e, half, vz[:, e, half * HALF:(half + 1) * HALF])
                        if e == 0:
                            conv_exp(h + 1, 1)
                            qk_high(h + 1, 0)
                            qk_high(h + 1, 1)
                    kv_high(h)
                else:
                    for e in range(2):
                        for half in range(2):
                            read_half(G_M, 8, h, 6 + e, half, vz[:, e, half * HALF:(half + 1) * HALF])
                    k_high(0)
                    q_high(0)
                    k_low_double(0)

            with act.Fori(0, MH - 1) as h:
                m_head(h, False)
            m_head(MH - 1, True)

            def exps(h, q, comps=(0, 1)):
                b = q % 2
                if q > 0 and 0 in comps:
                    act.wait_ge(a_mix.sem, a_mix.after(h, 4 * q - 1))
                for c in comps:
                    act.wait_ge(a_max.sem, a_max.after(h, 2 * q + c))
                    act.activation(pr[:, c], ps[:, 2 + 2 * c:4 + 2 * c, :].rearrange("p b k -> p (b k)"), ACT.Exp,
                                   bias=nmax[:, b, c:c + 1], accum_out=den[:, b, c:c + 1]).then_inc(a_exp.sem, 1)

            def high_round(h, k, dst):
                act.wait_ge(a_tr.sem, a_tr.after(h, k))
                act.activation(dst, ps[:, 6, :].rearrange("p (k s) -> p k s", k=4), ACT.Copy).then_inc(a_tr_hi.sem, 1)

            def at_dst(q, i):
                return at_s[:, 0, 4 * i:4 * i + 4, (q % 2) * P:(q % 2 + 1) * P]

            def o_read(h, n):
                act.wait_ge(a_pv.sem, a_pv.after(h, n))
                if n > 0:
                    act.wait_ge(a_ost.sem, a_ost.after(h, 2 * (n - 1)))
                act.activation(of[:], ps[:, 7, 0:2 * P], ACT.Copy).then_inc(a_of.sem, 1)

            def o_rstd(h, n):
                act.wait_ge(a_ss.sem, a_ss.after(h, n))
                if n > 0:
                    act.wait_ge(a_ost.sem, a_ost.after(h, 2 * (n - 1)))
                act.activation(ors[:], ps[:, 7, 2 * P:4 * P], ACT.Ln, bias=eps[:], scale=1.0 / AV).then_inc(a_rs.sem, 1)
                act.wait_ge(a_rs.sem, a_rs.after(h, 2 * n))
                act.activation(ors[:], ors[:], ACT.Exp, scale=-0.5).then_inc(a_rs.sem, 1)

            def o_store(h, n):
                act.wait_ge(a_ost.sem, a_ost.after(h, 2 * n + 1))
                act.wait_ge(spilled[1], 32 * (4 * h + (n + 1)))
                act.activation(osp[:, 0], ost[:], ACT.Copy).then_inc(a_ohi.sem, 1)
                act.wait_ge(a_olo.sem, a_olo.after(h, n))
                for p in range(2):
                    act.dma_start(spill_a[p, bass.ds(h, 1), :, 2 * n * P:2 * (n + 1) * P].rearrange(
                        "one p s -> (one p) s"), osp[:, p].bitcast(F32)).then_inc(spilled[1], 16)

            def a_head(h, first, last):
                def read_filler(n):
                    if last:
                        return
                    j, half = divmod(n, 2)
                    if j < 2:
                        read_rope(G_A, 4, h, h + 1, 2 * j, half)
                        return
                    if n == 4:
                        act.wait_ge(a_tr.sem, a_tr.after(h, 1))
                    if n == 6:
                        act.wait_ge(a_gate_dve.sem, a_gate_dve.after(h, 2))
                    read_half(G_A, 4, h, j, half, vz[:, j - 2, half * HALF:(half + 1) * HALF])

                exps(h, 0)
                act.wait_ge(a_gate_dve.sem, a_gate_dve.after(h, 0))
                exp_ln(aw[:], a_gate_act.sem, a_gate_act.after(h, 0))
                read_filler(0)
                if not first:
                    act.wait_ge(a_pv.sem, a_pv.after(h - 1, 3))
                high_round(h, 0, va[:, 0, 0:4, :])
                if not first:
                    o_rstd(h - 1, 3)
                high_round(h, 1, va[:, 0, 4:8, :])
                if not first:
                    o_store(h - 1, 3)
                act.wait_ge(a_gate_dve.sem, a_gate_dve.after(h, 1))
                act.activation(aw[:], aw[:], ACT.Exp).then_inc(a_gate_act.sem, 1)
                for q in range(ST):
                    if q % 2 == 0 and q > 0:
                        act.wait_ge(a_pv.sem, a_pv.after(h, q // 2 - 1))
                    high_round(h, 2 + 2 * q, at_dst(q, 0))
                    if q + 1 < ST:
                        exps(h, q + 1, (0,))
                    high_round(h, 2 + 2 * q + 1, at_dst(q, 1))
                    if q + 1 < ST:
                        exps(h, q + 1, (1,))
                    if q % 2 == 0 and q > 0:
                        o_rstd(h, q // 2 - 1)
                    if not last and q == 6:
                        act.wait_ge(a_score.sem, a_score.after(h, 15))
                        k_high(h + 1)
                    if not last and q == 7:
                        q_high(h + 1)
                        k_low_double(h + 1)
                    if q + 1 < ST:
                        read_filler(q + 1)
                    if q % 2 == 0 and q > 0:
                        o_store(h, q // 2 - 1)
                    if q % 2 == 1:
                        o_read(h, q // 2)

            act.wait_ge(spilled[0], 32 + 32 * 4 * MH)
            a_head(0, True, False)
            with act.Fori(1, AH - 1) as h:
                a_head(h, False, False)
            a_head(AH - 1, False, True)
            o_rstd(AH - 1, 3)
            o_store(AH - 1, 3)

            def merge(n, base):
                with act.Fori(0, KT) as d:
                    at = (4 + n) * d + 4 * KT * n
                    i = KT * n + d
                    act.wait_ge(f_dve, at + 1)
                    for half in range(2):
                        read_half(base, 2, d, 0, half, fz[:, half * HALF:(half + 1) * HALF], bias=fbias[:])
                    act.wait_ge(f_dve, at + 2)
                    act.activation(fw[:], fw[:], ACT.Exp).then_inc(f_act, 1)
                    act.wait_ge(f_act, 3 * i + 1)
                    act.activation(fw[:], fw[:], ACT.Ln, bias=1.0).then_inc(f_act, 1)
                    for half in range(2):
                        read_half(base, 2, d, 1, half, fb[:, half * HALF:(half + 1) * HALF])
                        if half == 0:
                            act.wait_ge(f_dve, at + 3)
                            act.activation(fw[:], fw[:], ACT.Exp).then_inc(f_act, 1)

            merge(0, G_FA)
            merge(1, G_FB)
            act.wait_ge(proj_done, 2 * (G_O - 1))
            for k in range(KT):
                act.wait_ge(f_dve, 4 * KT + 5 * (k + 1))
                act.activation(ys[:, 0, k], ya[:, k], ACT.Copy).then_inc(y_hi, 1)
            def out_tile(c, par):
                g = G_O + c
                for half in range(2):
                    if half == 0 and not isinstance(c, int):
                        act.wait_ge(o_tr, 2 * c - 2)
                    act.wait_ge(proj_done, 2 * g + half + 1)
                    act.activation(outT[par][:, half * HALF:(half + 1) * HALF], ps[:, half, :], ACT.Copy) \
                        .then_inc(proj_read, 1)

            for c in range(2):
                out_tile(c, c)
            with act.Fori(1, KT // 2) as c2:
                for par in range(2):
                    out_tile(2 * c2 + par, par)
            for t in range(ST):
                if t == 0:
                    act.wait_ge(o_rows, 2 * KT)
                act.activation(outT[t % 2][:], orow[:, t], ACT.Square, accum_out=tail_stat[:, 0, t:t + 1]) \
                    .then_inc(o_stat, 1)
                act.wait_ge(o_stat, 3 * t + 1)
                act.activation(tail_stat[:, 1, t:t + 1], tail_stat[:, 0, t:t + 1], ACT.Ln, bias=eps[:], scale=1.0 / D) \
                    .then_inc(o_stat, 1)
                act.wait_ge(o_stat, 3 * t + 2)
                act.activation(tail_stat[:, 2, t:t + 1], tail_stat[:, 1, t:t + 1], ACT.Exp, scale=-0.5) \
                    .then_inc(o_stat, 1)


_INS = ["x", "pre_norm_g", "w_in", "conv_w", "conv_b", "gate_b", "m_norm_g", "lambda_qk", "a_norm_g",
        "w_branch_m", "w_branch_a", "b_merge", "w_out", "post_norm_g"]


def constants():
    c = np.zeros((P, K_END), np.float32)
    i = np.arange(P)
    c[:, K_ID:K_ID + P] = i[:, None] == i[None, :]
    c[:, K_REV:K_REV + P] = i[:, None] + i[None, :] == P - 1
    c[:, K_MASK:K_MASK + P] = np.where(i[:, None] > i[None, :], MASKED, 0.0)
    c[:, K_MASK + P:K_MASK + 2 * P] = np.where(i[:, None] < i[None, :], MASKED, 0.0)
    inv = np.float32(THETA) ** (-np.arange(0, ROPE, 2, dtype=np.float32) / np.float32(ROPE))
    ang = (np.arange(S, dtype=np.float32)[None, :] * inv[:, None].astype(np.float32)).astype(np.float32)
    c[:, K_COS:K_COS + S] = 1.0
    half = ROPE // 2
    for first in (0, AD):
        for part, sign in ((0, -1.0), (1, 1.0)):
            rows = slice(first + part * half, first + (part + 1) * half)
            c[rows, K_COS:K_COS + S] = np.cos(ang)
            c[rows, K_SIN:K_SIN + S] = sign * np.sin(ang)
    return c


def kernel(**inputs):
    import concourse.bacc as bacc
    from concourse.bass_utils import run_bass_kernel_spmd

    nc = bacc.Bacc("TRN2", target_bir_lowering=False, num_devices=1)
    arrays = {f"in_{n}": np.ascontiguousarray(inputs[n]) for n in _INS}
    arrays["consts"] = constants()
    args = [nc.dram_tensor(n, a.shape, mybir.dt.from_np(a.dtype), kind="ExternalInput").ap()
            for n, a in arrays.items()]
    out = nc.dram_tensor("out", (1, S, D), F32, kind="ExternalOutput").ap()
    hybrid_block(nc, *args, out)
    r = run_bass_kernel_spmd(nc, [arrays], core_ids=[0])
    return r.results[0]["out"]
```

```python
import math
from contextlib import ExitStack

import numpy as np

import concourse.bass as bass
from concourse import mybir

P = 128
D = 1024
S = 1024
KT = D // P
ST = S // P
HALF = 512
MH, MQK, MV = 4, 128, 256
NC = S // P
AH, AD, AV = 8, 64, 128
CONV = 4
THETA, ROPE = 500000.0, AD // 4
EPS = 1e-6
LAM_INIT = 0.8 - 0.6 * math.exp(-0.3 * 0)
MASKED = -1e30

SPLITS = (2 * MH * MQK, MH * MV, 4 * MH, MH * MV, MH * MV, 2 * AH * AD, 2 * AH * AD, AH * AV, AH * AV, 2 * D)
C_MQK, C_MV, C_MG, C_MO, C_MZ, C_AQ, C_AK, C_AV, C_AZ, C_GM, IN_COLS = (
    int(c) for c in np.cumsum((0,) + SPLITS))

G_M = 8
G_A = G_M + 8 * MH
G_GL = G_A + 4 * (AH - 1)
G_G = G_GL + 4
G_FA = G_G + 8
G_FB = G_FA + KT
G_O = G_FB + KT
G_END = G_O + KT

F32 = mybir.dt.float32
F32R = mybir.dt.float32r
ALU = mybir.AluOpType
ACT = mybir.ActivationFunctionType
AX_X = mybir.AxisListType.X
PASSES = ((0, 0), (0, 1), (1, 0))

K_ID, K_REV, K_MASK, K_COS, K_SIN = 0, P, 2 * P, 4 * P, 4 * P + S
K_END = 4 * P + 2 * S

Q_NEGM, Q_B, Q_WINTER, Q_EMJ, Q_WK = range(5)


V_CW, V_CB, V_MG = 0, CONV * 2 * MH, (CONV + 1) * 2 * MH
V_BM, V_AG, V_PG = V_MG + KT, V_MG + 3 * KT, V_MG + 3 * KT + 1
V_ROWS = V_PG + KT


PREP_DVE = ("wg_hi", "wg_lo", "ident_r", "mask_r", "vecs", "conv0", "again", "bmerge", "post_g", "pick",
            "lam_products", "lam_sums", "gates", "i_fw", "i_bw", "f_fw", "f_bw", "abs_f", "log_f", "a", "b",
            "carry", "max_fw", "max_bw", "m_prev", "decay", "neg_m", "b_copy", "w_inter", "a_plus_m", "w_k",
            "neglam", "col_fw", "col_rev", "wk_fw", "wk_rev", "decay_all", "col_bw")
PREP_ACT = ("exp_f", "ln_f", "lam_exp", "decay", "w_inter", "emj", "w_k")
N_SMALL = 11


def prep_dve_at(name):
    return PREP_DVE.index(name) + 1


def prep_act_at(name):
    return PREP_ACT.index(name) + 1


def is_zero(h):
    return isinstance(h, int) and h == 0


def round_of(q, i):
    return 1 + i if q == 0 else 2 + 2 * q + i


V_ROUND = (0, 3)


class Signal:

    def __init__(self, sem, per_head=1, base=0):
        self.sem, self.per_head, self.base = sem, per_head, base

    def after(self, h, k=0):
        return self.per_head * h + (self.base + k + 1)


def hybrid_block(nc, x, pre_norm_g, w_in, conv_w, conv_b, gate_b, m_norm_g, lambda_qk, a_norm_g,
                 w_branch_m, w_branch_a, b_merge, w_out, post_norm_g, consts, out):
    ctx = ExitStack()
    with ctx:
        def sb(name, shape, dt=F32, at=ctx):
            return at.enter_context(nc.sbuf_tensor(name, shape, dt))

        def sem(name):
            return ctx.enter_context(nc.semaphore(name))

        def signal(name, per_head=1, base=0):
            return Signal(sem(name), per_head, base)

        spill_m = nc.dram_tensor("spill_m", [2, KT, P, S], F32, kind="Internal").ap()
        spill_a = nc.dram_tensor("spill_a", [2, KT, P, S], F32, kind="Internal").ap()
        spill_g = nc.dram_tensor("spill_g", [2 * KT, P, S], F32, kind="Internal").ap()

        x_v = x[0].rearrange("(t p) d -> t p d", p=P)
        out_v = out[0].rearrange("(t p) d -> t p d", p=P)
        w_in_v = w_in[0].rearrange("(k p) c -> p k c", p=P)
        wm_v = w_branch_m[0].rearrange("(k p) c -> p k c", p=P)
        wa_v = w_branch_a[0].rearrange("(k p) c -> p k c", p=P)
        wo_v = w_out[0].rearrange("(k p) c -> p k c", p=P)

        raw = [sb(f"w_raw{i}", [P, KT, P]) for i in range(2)]
        wsp = [sb(f"w_split{i}", [P, 2, KT, P], F32R) for i in range(2)]
        ident = sb("ident", [P, P])
        ones = sb("ones", [P, P])
        ones_r = sb("ones_r", [P, 2], F32R)
        bmerge = sb("bmerge", [P, 2 * KT])
        gcol = sb("post_g_col", [P, 2])
        fbias = sb("f_bias", [P, 2])
        tail_stat = sb("tail_stat", [P, ST])
        eps = sb("eps", [P, 1])
        post_g = sb("post_g", [P, KT])
        qkf = sb("qk_f32", [P, 2, S])
        xn_scope = ExitStack()
        xs = sb("xn_split", [P, 2, KT, S], F32R, at=xn_scope)

        ma_scope = ExitStack()
        rev = sb("rev", [P, P], at=ma_scope)
        cos = sb("cos", [P, S], at=ma_scope)
        sin = sb("sin", [P, S], at=ma_scope)
        mask_r = sb("mask_r", [P, 2, P], F32R, at=ma_scope)
        ident_r = sb("ident_r", [P, P], F32R, at=ma_scope)
        col = sb("gate_cols", [P, 16, 5, MH], at=ma_scope)
        decay = sb("decay", [P, MH, 16], at=ma_scope)
        vecs = sb("vectors", [P, V_ROWS], at=ma_scope)
        again = sb("again", [P, 1], at=ma_scope)
        neglam = sb("neglam", [P, 1], at=ma_scope)
        rawa = sb("raw_a", [P, S + CONV], at=ma_scope)
        rawb = sb("raw_b", [P, S], at=ma_scope)
        vz = sb("v_f32", [P, 2, S], at=ma_scope)

        p_scope = ExitStack()
        xin = [vz[:, 0], vz[:, 1], qkf[:, 0], qkf[:, 1]]
        gate_fill = sb("gate_fill", [P, 2, S], at=p_scope)
        pre_bc = sb("pre_bc", [P, D], at=p_scope)
        xstat = sb("xstat", [P, 2, ST], at=p_scope)
        wg = sb("wg", [P, KT, 16], at=p_scope)
        wgs = sb("wg_split", [P, 2, KT, 16], F32R, at=p_scope)
        gs = sb("gates_seq", [P, ST, 16], at=p_scope)
        gbias = sb("gbias", [MH, 4], at=p_scope)
        r_i = sb("row_i", [MH, 2, S], at=p_scope)
        r_f = sb("row_f", [MH, 2, S], at=p_scope)
        r_t = sb("row_t", [MH, 2, S], at=p_scope)
        r_m = sb("row_m", [MH, 2, S], at=p_scope)
        r_reset = sb("row_reset", [MH, 2, S], at=p_scope)
        r_carry = sb("row_carry", [MH, 2, S], at=p_scope)
        r_mp = sb("row_mp", [MH, 2, NC], at=p_scope)
        r_dec = sb("row_decay", [MH, 2, NC], at=p_scope)
        r_four = sb("row_four", [P, 2, S], at=p_scope)
        r_wk = r_f
        pick = sb("pick", [MH, MH, P], at=p_scope)
        colrev = sb("col_reversed", [P, NC, 5, MH], at=p_scope)
        lamb = sb("lamb", [P, 4, AD], at=p_scope)
        lamt = sb("lamt", [P, 2, AD], at=p_scope)
        lams = sb("lams", [P, 4], at=p_scope)
        masks_f = sb("masks_f", [P, 2, P], at=p_scope)
        vrows = sb("vector_rows", [V_ROWS, P], at=p_scope)
        p_scope.close()

        m_scope = ExitStack()
        qT = sb("q_split", [P, 2, S], F32R, at=m_scope)
        kT = sb("k_split", [P, 2, S], F32R, at=m_scope)
        kseq = sb("k_seq", [P, NC, P], at=m_scope)
        vS = sb("v_split", [P, 2, NC, MV], F32R, at=m_scope)
        ab = sb("sigmoid_work", [P, 2, S], at=m_scope)
        zg = sb("gate_z", [P, 2, S], at=m_scope)
        hacc = sb("h_sum", [P, NC, MV], at=m_scope)
        wt = sb("w_exp", [P, 2, P], at=m_scope)
        ptf = sb("pt_f32", [P, 2, P], at=m_scope)
        pt = sb("pt_split", [P, 2, 2, P], F32R, at=m_scope)
        kw = sb("kw_split", [P, 2, 2, P], F32R, at=m_scope)
        num = sb("num", [P, 2, MV], at=m_scope)
        cf = sb("state_f32", [P, 2, MV + 2], at=m_scope)
        cs = sb("state_split", [P, 2, 2, MV + 2], F32R, at=m_scope)
        dg = sb("diag", [P, 2, P], at=m_scope)
        dsm = sb("den", [P, 4, 2], at=m_scope)
        hc = sb("head_cols", [P, 16, 5], at=m_scope)
        hd = sb("head_decay", [P, 16], at=m_scope)
        hg = sb("head_gain", [P, 2], at=m_scope)
        hcv = sb("head_conv", [P, 2, CONV + 1], at=m_scope)
        hstat = sb("h_stat", [P, 2, NC], at=m_scope)
        hst = sb("hT_f32", [P, HALF], at=m_scope)
        hsp = sb("hT_split", [P, 2, HALF], F32R, at=m_scope)
        m_scope.close()

        a_scope = ExitStack()
        qs = sb("q_stack", [P, 2, S], F32R, at=a_scope)
        ks = sb("k_stack", [P, 2, 2, S], F32R, at=a_scope)
        va = sb("va_split", [P, 2, ST, AV], F32R, at=a_scope)
        at_s = sb("aT_split", [P, 2, KT, 2 * P], F32R, at=a_scope)
        pr = sb("probs", [P, 2, S], at=a_scope)
        am = [sb(f"mix{i}", [P, S], at=a_scope) for i in range(2)]
        ga = sb("gate_a", [P, S], at=a_scope)
        aw = sb("sigmoid_work_a", [P, S], at=a_scope)
        nmax = sb("negmax", [P, 2, 2], at=a_scope)
        den = sb("den_a", [P, 2, 2], at=a_scope)
        rden = sb("rden", [P, 3, 2], at=a_scope)
        of = sb("o_f32", [P, 2 * P], at=a_scope)
        osq = sb("o_sq", [P, 2 * P], at=a_scope)
        ors = sb("o_rs", [P, 2 * P], at=a_scope)
        ost = sb("o_out", [P, 2 * P], at=a_scope)
        osp = sb("o_split", [P, 2, 2 * P], F32R, at=a_scope)
        a_scope.close()
        ma_scope.close()

        f_scope = ExitStack()
        hT = sb("h_split", [P, 2, KT, S], F32R, at=f_scope)
        ya = sb("y_f32", [P, KT, S], at=f_scope)
        fw = sb("f_work", [P, S], at=f_scope)
        fb = sb("f_branch", [P, S], at=f_scope)
        f_scope.close()
        xn_scope.close()
        o_scope = ExitStack()
        xres = sb("x_residual", [P, ST, D], at=o_scope)
        o_scope.close()
        ys, orow = hT, ya
        outT = [qkf[:, 0], qkf[:, 1]]
        sqT = [fw[:], fb[:]]

        ps = ctx.enter_context(nc.psum_tensor("ps", [P, 8, HALF], F32))

        x_loaded = [sem(f"x_loaded{i}") for i in range(4)]
        first_loaded = sem("first_loaded")
        small_loaded = sem("small_loaded")
        rope_loaded = sem("rope_loaded")
        raw_loaded = [sem(f"raw_loaded{i}") for i in range(2)]
        spilled = [sem("spilled_m"), sem("spilled_a")]
        h_loaded = [sem("h_m_loaded"), sem("h_a_loaded")]
        g_spilled = [sem(f"g_spilled{i}") for i in range(2)]
        g_loaded = [sem(f"g_loaded{i}") for i in range(2)]
        res_loaded = sem("res_loaded")
        stored = sem("stored")
        step_begun = sem("step_begun")
        w_split = sem("w_split")
        proj_done = sem("proj_done")
        proj_read = sem("proj_read")
        consts_set = sem("consts_set")
        x_stat = sem("x_stat")
        x_scaled = sem("x_scaled")
        x_tr = sem("x_transposed")
        x_hi = sem("x_hi")
        x_lo = sem("x_lo")
        prep_pe = sem("prep_pe")
        prep_dve = sem("prep_dve")
        prep_act = sem("prep_act")
        hcols = signal("hcols", 4)
        score_done = signal("score_done", 8)
        diag_done = signal("diag_done", 8)
        w_done = signal("w_done", 8)
        ptf_done = signal("ptf_done", 8)
        pthi_done = signal("pthi_done", 8)
        ptlo_done = signal("ptlo_done", 8)
        kwhi_done = signal("kwhi_done", 7)
        kwlo_done = signal("kwlo_done", 7)
        inter_done = signal("inter_done", 7)
        intra_done = signal("intra_done", 8)
        upd_done = signal("upd_done", 7)
        intersc_done = signal("intersc_done", 7)
        num_done = signal("num_done", 8)
        den_chain = signal("den_chain", 40)
        h_done = signal("h_done", 8)
        state_done = signal("state_done", 7)
        chi_done = signal("chi_done", 7)
        clo_done = signal("clo_done", 7)
        gate_dve = signal("gate_dve", 12)
        gate_act = signal("gate_act", 10)
        conv_dve = signal("conv_dve", 14)
        conv_act = signal("conv_act", 6)
        qk_hi = signal("qk_hi", 2)
        qk_lo = signal("qk_lo", 2)
        tr_done = signal("tr_done", 10, 6)
        tr_read = signal("tr_read", 10, 6)
        tr_hi = signal("tr_hi", 4)
        hsp_hi = signal("hsp_hi", 4)
        hsplit_done = signal("hsplit_done", 4)
        hs_act = signal("hs_act", 3)
        hs_done = signal("hs_done", 1)

        shuf_done = sem("shuf_done")
        rope_done = sem("rope_done")

        a_qk_hi = signal("a_qk_hi", 4)
        k_doubled = sem("k_doubled")
        a_qk_lo = signal("a_qk_lo", 4)
        a_score = signal("a_score", 16)
        a_max = signal("a_max", 16)
        a_exp = signal("a_exp", 16)
        a_mix = signal("a_mix", 32)
        a_tr = signal("a_tr", 18)
        a_tr_hi = signal("a_tr_hi", 18)
        a_tr_read = signal("a_tr_read", 18)
        a_pv = signal("a_pv", 4)
        a_of = signal("a_of", 4)
        a_osq = signal("a_osq", 4)
        a_ss = signal("a_ss", 4)
        a_rs = signal("a_rs", 8)
        a_ost = signal("a_ost", 8)
        a_ohi = signal("a_ohi", 4)
        a_olo = signal("a_olo", 4)
        a_gate_dve = signal("a_gate_dve", 3)
        a_gate_act = signal("a_gate_act", 3)

        bias_set = sem("bias_set")
        f_abs = sem("f_abs")
        f_logsig = sem("f_logsig")
        f_act = sem("f_act")
        f_product = sem("f_product")
        f_y = sem("f_y")
        y_hi = sem("y_hi")
        y_lo = sem("y_lo")
        gcol_set = sem("gcol_set")
        o_tr = sem("o_tr")
        o_sums = sem("o_sums")
        o_rows = sem("o_rows")
        o_stat = sem("o_stat")
        o_out = sem("o_out")

        block = ctx.enter_context(nc.Block())

        def tile_no(base, per_head, h, j):
            return per_head * h + (base + j), (base + j) % 2

        @block.sync
        def _(sp):
            def load_weights(base, per_head, h, j, src, col0):
                assert per_head % 2 == 0
                g, b = tile_no(base, per_head, h, j)
                if not (isinstance(g, int) and g < 2):
                    sp.wait_ge(w_split, 2 * g - 2)
                    if not isinstance(g, int):
                        sp.sem_inc(step_begun, 1)
                sp.dma_start(raw[b][:], src[:, :, bass.ds(col0, P)]).then_inc(raw_loaded[b], 16)

            sp.dma_start(ident[:], consts[:, K_ID:K_ID + P]).then_inc(first_loaded, 16)
            for t in range(4):
                sp.dma_start(xin[t], x_v[t]).then_inc(x_loaded[t], 16)
            sp.dma_start(pre_bc[:], pre_norm_g[0].partition_broadcast(P)).then_inc(first_loaded, 16)
            small = [
                (wg[:], w_in_v[:, :, C_MG:C_MG + 16]),
                (vrows[V_CW:V_CB, :], conv_w[0].rearrange("w (j p) -> (w j) p", p=P)),
                (vrows[V_CB:V_MG, :], conv_b[0].rearrange("(j p) -> j p", p=P)),
                (vrows[V_MG:V_BM, :], m_norm_g[0].rearrange("(j p) -> j p", p=P)),
                (vrows[V_BM:V_AG, :], b_merge[0].rearrange("(j p) -> j p", p=P)),
                (vrows[V_AG:V_PG, :], a_norm_g),
                (vrows[V_PG:V_ROWS, :], post_norm_g[0].rearrange("(j p) -> j p", p=P)),
                (gbias[:], gate_b[0].rearrange("g h -> h g")),
                (rev[:], consts[:, K_REV:K_REV + P]),
                (masks_f[:], consts[:, K_MASK:K_MASK + 2 * P].rearrange("p (r j) -> p r j", r=2)),
                (lamb[:], lambda_qk[0].partition_broadcast(P)),
            ]
            for dst, src in small:
                sp.dma_start(dst, src, allow_slow_non_contiguous=True).then_inc(small_loaded, 16)
            assert len(small) == N_SMALL
            for j in range(2):
                load_weights(0, 0, 0, j, w_in_v, C_MQK + j * MH * MQK)
            for t in range(4, ST):
                sp.wait_ge(x_tr, 2 * (t - 4) + 2)
                sp.dma_start(xin[t % 4], x_v[t]).then_inc(x_loaded[t % 4], 16)
            for i in range(4):
                load_weights(0, 0, 0, 2 + i, w_in_v, C_GM + i * P)
            for e in range(2):
                load_weights(0, 0, 0, 6 + e, w_in_v, C_MV + e * P)
            sp.dma_start(cos[:], consts[:, K_COS:K_COS + S]).then_inc(rope_loaded, 16)
            sp.dma_start(sin[:], consts[:, K_SIN:K_SIN + S]).then_inc(rope_loaded, 16)

            def m_head(h, last):
                for e in range(2):
                    load_weights(G_M, 8, h, 2 * e, w_in_v, C_MO + e * P + h * MV)
                    load_weights(G_M, 8, h, 2 * e + 1, w_in_v, C_MZ + e * P + h * MV)
                if not last:
                    load_weights(G_M, 8, h, 4, w_in_v, C_MQK + MQK + h * MQK)
                    load_weights(G_M, 8, h, 5, w_in_v, C_MQK + (MH + 1) * MQK + h * MQK)
                    load_weights(G_M, 8, h, 6, w_in_v, C_MV + MV + h * MV)
                    load_weights(G_M, 8, h, 7, w_in_v, C_MV + MV + P + h * MV)
                else:
                    for j, c in enumerate((C_AQ, C_AK, C_AV, C_AZ)):
                        load_weights(G_M, 8, h, 4 + j, w_in_v, c)

            with sp.Fori(0, MH - 1) as h:
                m_head(h, False)
            m_head(MH - 1, True)

            def store_a(h, n):
                sp.wait_ge(a_olo.sem, a_olo.after(h, n))
                sp.dma_start(spill_a[:, bass.ds(h, 1), :, 2 * n * P:2 * (n + 1) * P].rearrange(
                    "i one p s -> p i (one s)"), osp[:].bitcast(F32)).then_inc(spilled[1], 16)

            def double_keys(hh):
                own = (slice(0, AD), slice(AD, P))
                for c in range(2):
                    sp.wait_ge(a_qk_lo.sem, a_qk_lo.after(hh, c))
                    sp.dma_start(ks[own[1 - c], c].bitcast(F32), ks[own[c], c].bitcast(F32)).then_inc(k_doubled, 16)

            def a_tiles(h, first):
                for j, c in enumerate((C_AQ, C_AK, C_AV, C_AZ)):
                    load_weights(G_A, 4, h, j, w_in_v, c + P + h * P)
                    if j == 2:
                        double_keys(h)
                    if not first:
                        store_a(h - 1, j)

            a_tiles(0, True)
            with sp.Fori(1, AH - 1) as h:
                a_tiles(h, False)

            for i in range(4):
                load_weights(G_GL, 0, 0, i, w_in_v, C_GM + (4 + i) * P)
                if i == 2:
                    double_keys(AH - 1)
                store_a(AH - 2, i)
            for j in range(2):
                load_weights(G_G, 0, 0, j, w_in_v, C_GM + (8 + j) * P)
                store_a(AH - 1, j)
            for j in range(2, 4):
                store_a(AH - 1, j)
            sp.wait_ge(spilled[0], 16 + 16 * 4 * MH)
            sp.wait_ge(spilled[1], 16 + 16 * 4 * AH)

            def load_h(n, k):
                dst, spill = ((hT, spill_m), (xs, spill_a))[n]
                sp.dma_start(dst[:, :, bass.ds(k, 1)].rearrange("p i one s -> p i (one s)").bitcast(F32),
                             spill[:, bass.ds(k, 1)].rearrange("i one p s -> p i (one s)")).then_inc(h_loaded[n], 16)

            for j in range(2):
                load_h(0, j)
            with sp.Fori(1, 4) as c:
                for j in range(2):
                    load_weights(G_G, 2, c, j, w_in_v, C_GM + (8 + j) * P + 2 * P * c)
                    load_h(0, 2 * c + j)

            def load_gate(i, par):
                sp.dma_start(qkf[:, par], spill_g[bass.ds(i, 1)].rearrange("one p s -> (one p) s")) \
                    .then_inc(g_loaded[par], 16)

            def branch(n, base, weights, first):
                with sp.Fori(first, KT // 2) as c:
                    for j in range(2):
                        load_weights(base, 2, c, j, weights, 2 * P * c + j * P)
                        sp.wait_ge(f_logsig, KT * n + 2 * c + (j - 1))
                        load_gate(KT * n + 2 * c + j, j)
                        if n == 0:
                            load_h(1, 2 * c + j)

            for j in range(2):
                load_weights(G_FA, 0, 0, j, wm_v, j * P)
                sp.wait_ge(g_spilled[j], 16 * KT)
                load_gate(j, j)
            sp.wait_ge(proj_done, 2 * G_FA)
            for j in range(2):
                load_h(1, j)
            branch(0, G_FA, wm_v, 1)
            branch(1, G_FB, wa_v, 0)
            for j in range(2):
                load_weights(G_O, 0, 0, j, wo_v, j * P)
            sp.wait_ge(proj_done, 2 * G_O)

            def load_residual(t):
                sp.dma_start(xres[:, bass.ds(t, 1)].rearrange("p one d -> p (one d)"),
                             x_v[bass.ds(t, 1)].rearrange("one p d -> (one p) d")).then_inc(res_loaded, 16)

            for j in range(2):
                load_residual(j)
            with sp.Fori(1, KT // 2) as c:
                for j in range(2):
                    load_weights(G_O, 2, c, j, wo_v, c * 2 * P + j * P)
                    load_residual(2 * c + j)
            for t in range(ST):
                sp.wait_ge(o_out, t + 1)
                sp.dma_start(out_v[t], orow[:, t]).then_inc(stored, 16)
            sp.wait_ge(stored, 16 * ST)

        @block.gpsimd
        def _(pool):
            def split_weights(base, per_head, h, j):
                g, b = tile_no(base, per_head, h, j)
                pool.wait_ge(raw_loaded[b], 16 * ((per_head // 2) * h + ((base + j) // 2 + 1)))
                if not (isinstance(g, int) and g < 2):
                    pool.wait_ge(proj_done, 2 * g - 2)
                pool.tensor_tensor(wsp[b][:, 0], raw[b][:], ones[:, 0:1].unsqueeze(2).to_broadcast([P, KT, P]),
                                   ALU.mult).then_inc(w_split, 1)
                pool.wait_ge(w_split, 2 * g + 1)
                pool.tensor_tensor(wsp[b][:, 1], raw[b][:], wsp[b][:, 0].bitcast(F32),
                                   ALU.subtract).then_inc(w_split, 1)

            def rope(hh, n):
                for half in range(2):
                    cols = slice(half * HALF, (half + 1) * HALF)
                    turn = 4 * hh + (n + half)
                    pool.wait_ge(shuf_done, turn + 1)
                    own, other = qkf[:, n // 2, cols], (rawa, rawb)[n // 2][:, cols]
                    pool.tensor_tensor(own, own, cos[:, cols], ALU.mult).then_inc(rope_done, 1)
                    pool.tensor_tensor(other, other, sin[:, cols], ALU.mult).then_inc(rope_done, 1)
                    pool.wait_ge(rope_done, 3 * turn + 2)
                    pool.tensor_tensor(own, own, other, ALU.add).then_inc(rope_done, 1)

            def with_rope(base, per_head, h, j, hh):
                split_weights(base, per_head, h, j)
                split_weights(base, per_head, h, j + 1)
                split_weights(base, per_head, h, j + 2)
                rope(hh, 0)
                split_weights(base, per_head, h, j + 3)
                rope(hh, 2)

            pool.wait_ge(consts_set, 2)
            for j in range(G_M):
                split_weights(0, 0, 0, j)
            pool.wait_ge(rope_loaded, 16 * 2)
            with pool.Fori(0, MH - 1) as h:
                for j in range(8):
                    split_weights(G_M, 8, h, j)
            for j in range(4):
                split_weights(G_M, 8, MH - 1, j)
            with_rope(G_M, 8, MH - 1, 4, 0)
            with pool.Fori(0, AH - 1) as h:
                with_rope(G_A, 4, h, 0, h + 1)
            with pool.Fori(0, (G_END - G_GL) // 2) as c:
                for j in range(2):
                    split_weights(G_GL, 2, c, j)

        @block.tensor
        def _(pe):
            def proj_half(base, per_head, h, j, half, moving=xs, amid=None):
                g, b = tile_no(base, per_head, h, j)
                if half == 0:
                    pe.wait_ge(w_split, 2 * g + 2)
                if not is_zero(g):
                    pe.wait_ge(proj_read, 2 * g + half - 1)
                cols = slice(half * HALF, (half + 1) * HALF)
                for k in range(KT):
                    if amid is not None and k == KT // 2:
                        amid()
                    for n, (wl, xl) in enumerate(PASSES):
                        mm = pe.matmul(ps[:, half, :], wsp[b][:, wl, k, :], moving[:, xl, k, cols],
                                       start=(k == 0 and n == 0), stop=(k == KT - 1 and n == 2))
                mm.then_inc(proj_done, 1)

            def product(dst, st, mv, start=True, stop=True):
                for n, (a, b) in enumerate(PASSES):
                    mm = pe.matmul(dst, st(a), mv(b), start=(start and n == 0), stop=(stop and n == 2))
                return mm

            def product_exact(dst, st, mv_one):
                for a in range(2):
                    mm = pe.matmul(dst, st(a), mv_one, start=(a == 0), stop=(a == 1))
                return mm

            pe.wait_ge(first_loaded, 16 * 2)
            for t in range(ST):
                pe.wait_ge(x_scaled, t + 1)
                if t >= 2:
                    pe.wait_ge(x_lo, 2 * (t - 2) + 2)
                for i in range(2):
                    bank = 2 + 2 * (t % 2) + i
                    for q in range(4):
                        mm = pe.transpose(ps[:, bank, q * P:(q + 1) * P],
                                          xin[t % 4][:, (4 * i + q) * P:(4 * i + q + 1) * P], ident[:])
                    mm.then_inc(x_tr, 1)
            pe.wait_ge(small_loaded, 16 * N_SMALL)
            pe.transpose(ps[:, 6, 0:V_ROWS], vrows[:], ident[0:V_ROWS, 0:V_ROWS]).then_inc(prep_pe, 1)
            pe.wait_ge(x_lo, 2 * ST)
            pe.wait_ge(prep_dve, prep_dve_at("wg_lo"))
            for t in range(ST):
                for k in range(KT):
                    for n, (xl, wl) in enumerate(PASSES):
                        mm = pe.matmul(ps[:, 7, t * 16:(t + 1) * 16], xs[:, xl, k, t * P:(t + 1) * P],
                                       wgs[:, wl, k, :], start=(k == 0 and n == 0), stop=(k == KT - 1 and n == 2))
            mm.then_inc(prep_pe, 1)
            proj_half(0, 0, 0, 0, 0)
            proj_half(0, 0, 0, 0, 1)
            pe.wait_ge(prep_dve, prep_dve_at("gates"))
            for kind in range(2):
                if kind == 1:
                    proj_half(0, 0, 0, 1, 0)
                    proj_half(0, 0, 0, 1, 1)
                    pe.wait_ge(prep_dve, prep_dve_at("i_bw"))
                for r in range(2):
                    for c in range(NC):
                        t = c if r == 0 else NC - 1 - c
                        n = r * NC + c
                        src = (2 * r + kind) * MH
                        mm = pe.transpose(ps[0:MH, 2 + n // 4, (n % 4) * P:(n % 4 + 1) * P],
                                          gs[:, t, src:src + MH], (ident if r == 0 else rev)[:])
                mm.then_inc(prep_pe, 1)
            for j in range(2, 6):
                proj_half(0, 0, 0, j, 0)
                proj_half(0, 0, 0, j, 1)
            pe.wait_ge(prep_act, prep_act_at("decay"))
            for m in range(MH):
                mm = pe.matmul(ps[:, 7, 256 + 16 * m:256 + 16 * m + 16], pick[:, m, :],
                               r_dec[:].rearrange("m r c -> m (r c)"), start=True, stop=True)
            mm.then_inc(prep_pe, 1)
            pe.wait_ge(prep_act, prep_act_at("w_k"))
            pe.wait_ge(prep_dve, prep_dve_at("w_k"))
            for n in range(2 * NC):
                r, c = divmod(n, NC)
                pe.transpose(ps[:, 2 + n // 4, (n % 4) * P:(n % 4 + 1) * P], r_four[:, r, c * P:(c + 1) * P], ident[:])
                mm = pe.transpose(ps[:, 6, 256 + n * MH:256 + (n + 1) * MH], r_wk[:, r, c * P:(c + 1) * P],
                                  ident[0:MH, 0:MH])
            mm.then_inc(prep_pe, 1)
            for half in range(2):
                proj_half(0, 0, 0, 6, half)
            pe.wait_ge(prep_dve, prep_dve_at("decay_all"))
            pe.matmul(ps[:, 7, 0:NC * 5 * MH], rev[:], colrev[:].rearrange("p c q m -> p (c q m)"),
                      start=True, stop=True).then_inc(prep_pe, 1)

            def tr_round(h, k, srcs, first=False):
                bank = (7, 2)[k % 2]
                if not first:
                    pe.wait_ge(tr_read.sem, tr_read.after(h, k) - 2)
                for q, src in enumerate(srcs):
                    mm = pe.transpose(ps[:, bank, q * P:(q + 1) * P], src, ident[:])
                mm.then_inc(tr_done.sem, 1)

            def kv_rounds(h, first=False):
                pe.wait_ge(conv_dve.sem, conv_dve.after(h + 1, 13))
                for i in range(2):
                    tr_round(h, 4 + i, [qkf[:, 1, c * P:(c + 1) * P] for c in range(4 * i, 4 * i + 4)], first)
                g, _ = tile_no(G_M, 8, h, 7)
                pe.wait_ge(proj_read, 2 * g + 2)
                for e in range(2):
                    for i in range(2):
                        tr_round(h, 6 + 2 * e + i, [vz[:, e, c * P:(c + 1) * P] for c in range(4 * i, 4 * i + 4)])

            def chunk(r, t):
                return t if r == 0 else NC - 1 - t

            def m_scores(h, t):
                if t == 0:
                    pe.wait_ge(qk_lo.sem, qk_lo.after(h, 1))
                    pe.wait_ge(tr_read.sem, tr_read.after(h - 1, 9))
                for r in range(2):
                    c = chunk(r, t)
                    sl = slice(c * P, (c + 1) * P)
                    product(ps[:, 2, r * P:(r + 1) * P], lambda a: kT[:, a, sl], lambda b: qT[:, b, sl])
                pe.wait_ge(diag_done.sem, diag_done.after(h, t))
                if t > 0:
                    pe.wait_ge(w_done.sem, w_done.after(h, t - 1))
                pe.matmul(ps[:, 3, 0:2 * P], ident_r[:], mask_r[:].rearrange("p r j -> p (r j)"),
                          start=True, stop=False)
                pe.matmul(ps[:, 3, 0:2 * P], ones[:], dg[:].rearrange("p r j -> p (r j)"),
                          start=False, stop=True).then_inc(score_done.sem, 1)

            def m_products(h, t):
                if t > 0:
                    pe.wait_ge(clo_done.sem, clo_done.after(h, t - 1))
                    pe.wait_ge(den_chain.sem, den_chain.after(h, 5 * t - 4))
                    for r in range(2):
                        c = chunk(r, t)
                        sl = slice(c * P, (c + 1) * P)
                        product(ps[:, 5, r * MV:(r + 1) * MV], lambda a: qT[:, a, sl], lambda b: cs[:, b, r, 0:MV])
                        mm = product(ps[:, 7, 4 + 2 * r:6 + 2 * r], lambda a: qT[:, a, sl],
                                     lambda b: cs[:, b, r, MV:MV + 2])
                    mm.then_inc(inter_done.sem, 1)
                    pe.wait_ge(num_done.sem, num_done.after(h, t - 1))
                pe.wait_ge(ptlo_done.sem, ptlo_done.after(h, t))
                if t == 0:
                    pe.wait_ge(tr_read.sem, tr_read.after(h - 1, 9))
                for r in range(2):
                    c = chunk(r, t)
                    product(ps[:, 4, r * MV:(r + 1) * MV], lambda a: pt[:, a, r, :], lambda b: vS[:, b, c, :])
                    mm = product_exact(ps[:, 7, 2 * r:2 * r + 2], lambda a: pt[:, a, r, :], ones_r[:])
                mm.then_inc(intra_done.sem, 1)
                if t < NC - 1:
                    pe.wait_ge(kwlo_done.sem, kwlo_done.after(h, t))
                    if t > 0:
                        pe.wait_ge(state_done.sem, state_done.after(h, t - 1))
                    for r in range(2):
                        c = chunk(r, t)
                        product(ps[:, 6, r * MV:(r + 1) * MV], lambda a: kw[:, a, r, :], lambda b: vS[:, b, c, :])
                        mm = product_exact(ps[:, 7, 8 + 2 * r:10 + 2 * r], lambda a: kw[:, a, r, :], ones_r[:])
                    mm.then_inc(upd_done.sem, 1)

            def h_rounds(h):
                pe.wait_ge(hs_done.sem, hs_done.after(h))
                for e in range(2):
                    for i in range(2):
                        tr_round(h, 2 * e + i, [hacc[:, c, e * P:(e + 1) * P] for c in range(4 * i, 4 * i + 4)],
                                 first=(2 * e + i < 2))

            def m_head(h, last):
                m_scores(h, 0)
                for t in range(NC):
                    proj_half(G_M, 8, h, t // 2, t % 2)
                    m_products(h, t)
                    if t < NC - 1:
                        m_scores(h, t + 1)
                for j in range(4, 6):
                    for half in range(2):
                        proj_half(G_M, 8, h, j, half)
                pe.wait_ge(den_chain.sem, den_chain.after(h, 5 * (NC - 1) + 1))
                h_rounds(h)
                for j in range(6, 8):
                    for half in range(2):
                        proj_half(G_M, 8, h, j, half)
                if not last:
                    kv_rounds(h)

            for half in range(2):
                proj_half(0, 0, 0, 7, half)
            pe.wait_ge(prep_dve, prep_dve_at("col_bw"))
            kv_rounds(-1, first=True)
            with pe.Fori(0, MH - 1) as h:
                m_head(h, False)
            m_head(MH - 1, True)

            def a_scores(h, q):
                if q == 0:
                    pe.wait_ge(k_doubled, 32 * h + 32)
                    pe.wait_ge(a_qk_lo.sem, a_qk_lo.after(h, 3))
                for c in range(2):
                    if q > 0:
                        pe.wait_ge(a_exp.sem, a_exp.after(h, 2 * (q - 1) + c))
                    elif not is_zero(h):
                        pe.wait_ge(a_exp.sem, a_exp.after(h, c) - 2)
                    for i in range(2):
                        for b in range(2):
                            mm = pe.matmul(ps[:, 2 + 2 * c + i, :], qs[:, c, q * P:(q + 1) * P],
                                           ks[:, c, b, i * HALF:(i + 1) * HALF], start=(b == 0), stop=(b == 1))
                    mm.then_inc(a_score.sem, 1)

            def a_round(h, k, srcs, first=False):
                if not first:
                    pe.wait_ge(a_tr_read.sem, a_tr_read.after(h, k) - 1)
                for n, src in enumerate(srcs):
                    mm = pe.transpose(ps[:, 6, n * P:(n + 1) * P], src, ident[:])
                mm.then_inc(a_tr.sem, 1)

            def mix_round(h, q, i):
                if i == 0:
                    pe.wait_ge(a_mix.sem, a_mix.after(h, 4 * q + 3))
                a_round(h, round_of(q, i), [am[q % 2][:, k * P:(k + 1) * P] for k in range(4 * i, 4 * i + 4)])

            def pv(h, n):
                pe.wait_ge(a_tr_read.sem, a_tr_read.after(h, round_of(2 * n + 1, 1)))
                if n > 0:
                    pe.wait_ge(a_rs.sem, a_rs.after(h, 2 * (n - 1)))
                elif not is_zero(h):
                    pe.wait_ge(a_rs.sem, a_rs.after(h, 0) - 2)
                for k in range(KT):
                    mm = product(ps[:, 7, 0:2 * P], lambda a: va[:, a, k, :], lambda b: at_s[:, b, k, :],
                                 start=(k == 0), stop=(k == KT - 1))
                mm.then_inc(a_pv.sem, 1)

            def squares(h, n):
                pe.wait_ge(a_osq.sem, a_osq.after(h, n))
                pe.matmul(ps[:, 7, 2 * P:4 * P], ones[:], osq[:], start=True, stop=True).then_inc(a_ss.sem, 1)

            def a_head(h, first, last):
                def filler(n, amid=None):
                    if not last:
                        proj_half(G_A, 4, h, n // 2, n % 2, amid=amid)
                    else:
                        proj_half(G_GL, 0, 0, n // 2, n % 2, amid=amid)

                def v_round(i):
                    a_round(h, V_ROUND[i], [vz[:, 0, c * P:(c + 1) * P] for c in range(4 * i, 4 * i + 4)],
                            first=(first and i == 0))

                a_scores(h, 0)
                if first:
                    pe.wait_ge(proj_read, 2 * (G_M + 8 * (MH - 1) + 7) + 2)
                v_round(0)
                filler(0)
                if not first:
                    squares(h - 1, 3)
                for q in range(ST):
                    mix_round(h, q, 0)
                    if q + 1 < ST:
                        a_scores(h, q + 1)
                    mix_round(h, q, 1)
                    if q % 2 == 0 and q > 0:
                        squares(h, q // 2 - 1)
                    if q + 1 < ST:
                        filler(q + 1, amid=(lambda: v_round(1)) if q == 0 else None)
                    if q % 2 == 1:
                        pv(h, q // 2)

            a_head(0, True, False)
            with pe.Fori(1, AH - 1) as h:
                a_head(h, False, False)
            a_head(AH - 1, False, True)
            squares(AH - 1, 3)

            with pe.Fori(0, 4) as c:
                for j in range(2):
                    proj_half(G_G, 2, c, j, 0)
                    proj_half(G_G, 2, c, j, 1)
            for n, (base, h) in enumerate(((G_FA, hT), (G_FB, xs))):
                pe.wait_ge(h_loaded[n], 16 * KT)
                with pe.Fori(0, KT // 2) as c:
                    for j in range(2):
                        proj_half(base, 2, c, j, 0, moving=h)
                        proj_half(base, 2, c, j, 1, moving=h)

            def out_rows(c, par):
                for i in range(2):
                    pe.wait_ge(proj_read, 2 * (G_O + c) + i + 1)
                    if not is_zero(c):
                        pe.wait_ge(o_rows, 2 * c + i - 1)
                    for q in range(4):
                        t = 4 * i + q
                        mm = pe.transpose(ps[:, 2 + 2 * par + i, q * P:(q + 1) * P],
                                          outT[par][:, t * P:(t + 1) * P], ident[:])
                    mm.then_inc(o_tr, 1)
                for t in range(ST):
                    mm = pe.matmul(ps[:, 6, 2 * t:2 * t + 2], sqT[par][:, t * P:(t + 1) * P], ones[:, 0:2],
                                   start=(is_zero(c) and t == 0),
                                   stop=(isinstance(c, int) and c == KT - 1 and t == ST - 1))
                mm.then_inc(o_sums, 1)

            pe.wait_ge(y_lo, KT)
            for c in range(2):
                proj_half(G_O, 0, 0, c, 0, moving=ys)
                proj_half(G_O, 0, 0, c, 1, moving=ys)
            out_rows(0, 0)
            with pe.Fori(1, KT // 2) as c2:
                for par in range(2):
                    proj_half(G_O, 2, c2, par, 0, moving=ys)
                    proj_half(G_O, 2, c2, par, 1, moving=ys)
                    out_rows(2 * c2 + (par - 1), 1 - par)
            out_rows(KT - 1, 1)

        @block.vector
        def _(dve):
            def mark(ins, name):
                assert name in PREP_DVE
                ins.then_inc(prep_dve, 1)

            def after_step(name):
                dve.wait_ge(prep_dve, prep_dve_at(name))

            dve.memset(eps[:], EPS).then_inc(consts_set, 1)
            dve.memset(ones[:], 1.0).then_inc(consts_set, 1)
            dve.memset(rawa[:], 0.0).then_inc(consts_set, 1)
            dve.memset(r_reset[:], 1.0).then_inc(consts_set, 1)
            dve.memset(r_carry[:], 0.0).then_inc(consts_set, 1)
            dve.memset(r_mp[:], 0.0).then_inc(consts_set, 1)
            dve.memset(r_four[:], 0.0).then_inc(consts_set, 1)
            dve.wait_ge(consts_set, 4)
            dve.tensor_copy(ones_r[:], ones[:, 0:2]).then_inc(consts_set, 1)
            starts = r_reset[:].rearrange("m r (c j) -> m r c j", j=P)[:, :, :, 0]
            dve.memset(starts, 0.0).then_inc(consts_set, 1)

            def x_low(t):
                for i in range(2):
                    dve.wait_ge(x_hi, 2 * t + i + 1)
                    dst = slice(4 * i, 4 * i + 4), slice(t * P, (t + 1) * P)
                    dve.tensor_tensor(xs[:, 1, dst[0], dst[1]],
                                      ps[:, 2 + 2 * (t % 2) + i, :].rearrange("p (k s) -> p k s", k=4),
                                      xs[:, 0, dst[0], dst[1]].bitcast(F32), ALU.subtract).then_inc(x_lo, 1)

            dve.wait_ge(first_loaded, 16 * 2)
            for t in range(ST):
                dve.wait_ge(x_stat, 3 * t + 3)
                dve.scalar_tensor_tensor(xin[t % 4], xin[t % 4], xstat[:, 1, t:t + 1], pre_bc[:],
                                         ALU.mult, ALU.mult).then_inc(x_scaled, 1)
                if t > 0:
                    x_low(t - 1)
            dve.wait_ge(small_loaded, 16 * N_SMALL)
            mark(dve.tensor_copy(wgs[:, 0], wg[:]), "wg_hi")
            x_low(ST - 1)
            after_step("wg_hi")
            mark(dve.tensor_tensor(wgs[:, 1], wg[:], wgs[:, 0].bitcast(F32), ALU.subtract), "wg_lo")
            mark(dve.tensor_copy(ident_r[:], ident[:]), "ident_r")
            mark(dve.tensor_copy(mask_r[:], masks_f[:]), "mask_r")
            dve.wait_ge(prep_pe, 1)
            mark(dve.tensor_copy(vecs[:], ps[:, 6, 0:V_ROWS]), "vecs")
            after_step("vecs")
            conv_cols = vecs[:, V_CW:V_MG].rearrange("p (w q m) -> p q w m", q=2, m=MH)
            mark(dve.tensor_copy(hcv[:], conv_cols[:, :, :, 0]), "conv0")
            mark(dve.tensor_scalar(again[:], vecs[:, V_AG:V_AG + 1], 1.0 - LAM_INIT, None, ALU.mult), "again")
            mark(dve.tensor_copy(bmerge[:], vecs[:, V_BM:V_AG]), "bmerge")
            mark(dve.tensor_copy(post_g[:], vecs[:, V_PG:V_ROWS]), "post_g")
            mark(dve.tensor_copy(pick[:], ident[0:MH, 0:MH].unsqueeze(2).to_broadcast([MH, MH, P])), "pick")
            lam2 = lamb[:].rearrange("p (j two) d -> p j two d", two=2)
            mark(dve.tensor_tensor(lamt[:], lam2[:, :, 0], lam2[:, :, 1], ALU.mult), "lam_products")
            after_step("lam_products")
            mark(dve.tensor_reduce(lams[:, 0:2], lamt[:], AX_X, ALU.add), "lam_sums")
            dve.wait_ge(prep_pe, 2)
            mark(dve.tensor_copy(gs[:], ps[:, 7, 0:ST * 16].rearrange("p (t g) -> p t g", t=ST)), "gates")

            def gate_rows(dst, kind, names):
                for r in range(2):
                    mark(dve.tensor_scalar(dst[:, r, :], ps[0:MH, 2 + 2 * r:4 + 2 * r, :].rearrange("m b j -> m (b j)"),
                                           gbias[:, 2 * r + kind:2 * r + kind + 1], None, ALU.add), names[r])

            def flat(t):
                return t[:].rearrange("m r j -> m (r j)")

            def chunks(t):
                return t[:].rearrange("m r (c j) -> m r c j", j=P)

            def conv_taps(hn, j):
                n = 7 * j
                g, _ = tile_no(0, 0, 0, j) if is_zero(hn) else tile_no(G_M, 8, hn - 1, 4 + j)
                if j == 1:
                    dve.wait_ge(conv_dve.sem, conv_dve.after(hn, 6))
                dve.wait_ge(proj_read, 2 * g + 2)
                dve.tensor_scalar(rawb[:], rawa[:, 0:S], hcv[:, j, 0:1], hcv[:, j, CONV:CONV + 1],
                                  ALU.mult, ALU.add).then_inc(conv_dve.sem, 1)
                for w in range(1, CONV):
                    dve.wait_ge(conv_dve.sem, conv_dve.after(hn, n + w - 1))
                    dve.scalar_tensor_tensor(rawb[:], rawa[:, w:w + S], hcv[:, j, w:w + 1], rawb[:],
                                             ALU.mult, ALU.add).then_inc(conv_dve.sem, 1)
                dve.wait_ge(conv_dve.sem, conv_dve.after(hn, n + CONV - 1))
                dve.scalar_tensor_tensor(qkf[:, j], rawb[:], -1.0, rawb[:], ALU.mult, ALU.min).then_inc(conv_dve.sem, 1)

            def conv_logsig(hn, j):
                dve.wait_ge(conv_act.sem, conv_act.after(hn, 3 * j + 1))
                dve.scalar_tensor_tensor(qkf[:, j], rawb[:], 0.0, qkf[:, j], ALU.min,
                                         ALU.subtract).then_inc(conv_dve.sem, 1)

            def conv_final(hn, j):
                dve.wait_ge(conv_act.sem, conv_act.after(hn, 3 * j + 2))
                dve.scalar_tensor_tensor(qkf[:, j], rawb[:], (MQK ** -0.5, 1.0)[j], qkf[:, j], ALU.mult,
                                         ALU.mult).then_inc(conv_dve.sem, 1)

            def qk_low(hn, j):
                dve.wait_ge(qk_hi.sem, qk_hi.after(hn, j))
                dve.tensor_tensor((qT, kT)[j][:, 1], qkf[:, j], (qT, kT)[j][:, 0].bitcast(F32),
                                  ALU.subtract).then_inc(qk_lo.sem, 1)

            def v_low(hn):
                for k in range(4):
                    e, i = divmod(k, 2)
                    dve.wait_ge(tr_hi.sem, tr_hi.after(hn, k))
                    dve.tensor_tensor(vS[:, 1, 4 * i:4 * i + 4, e * P:(e + 1) * P],
                                      ps[:, (7, 2)[k % 2], :].rearrange("p (c d) -> p c d", c=4),
                                      vS[:, 0, 4 * i:4 * i + 4, e * P:(e + 1) * P].bitcast(F32),
                                      ALU.subtract).then_inc(tr_read.sem, 1)

            dve.wait_ge(prep_pe, 3)
            gate_rows(r_i, 0, ("i_fw", "i_bw"))
            conv_taps(0, 0)
            dve.wait_ge(prep_pe, 4)
            gate_rows(r_f, 1, ("f_fw", "f_bw"))
            after_step("f_bw")
            mark(dve.scalar_tensor_tensor(flat(r_t), flat(r_f), -1.0, flat(r_f), ALU.mult, ALU.min), "abs_f")
            conv_logsig(0, 0)
            dve.wait_ge(prep_act, prep_act_at("ln_f"))
            mark(dve.scalar_tensor_tensor(flat(r_f), flat(r_f), 0.0, flat(r_t), ALU.min, ALU.subtract), "log_f")
            after_step("log_f")
            dve.wait_ge(consts_set, 9)
            mark(dve.tensor_tensor_scan(flat(r_t), flat(r_reset), flat(r_f), 0.0, ALU.mult, ALU.add), "a")
            after_step("a")
            mark(dve.tensor_tensor(flat(r_i), flat(r_i), flat(r_t), ALU.subtract), "b")
            mark(dve.tensor_copy(chunks(r_carry)[:, :, 1:NC, 0], chunks(r_t)[:, :, 0:NC - 1, P - 1]), "carry")
            after_step("carry")
            for r, name in enumerate(("max_fw", "max_bw")):
                mark(dve.tensor_tensor_scan(r_m[:, r], r_carry[:, r], r_i[:, r], 0.0, ALU.add, ALU.max), name)
            after_step("max_bw")
            a_end, m_end = chunks(r_t)[:, :, :, P - 1], chunks(r_m)[:, :, :, P - 1]
            mark(dve.tensor_tensor(r_mp[:, :, 1:NC], a_end[:, :, 0:NC - 1], m_end[:, :, 0:NC - 1], ALU.add), "m_prev")
            after_step("m_prev")
            mark(dve.tensor_tensor(r_dec[:], r_mp[:], m_end, ALU.subtract), "decay")

            def four(q):
                return r_four[32 * q:32 * q + MH]

            wide = [MH, 2, NC, P]
            mark(dve.tensor_scalar(four(Q_NEGM), r_m[:], -1.0, None, ALU.mult), "neg_m")
            mark(dve.tensor_copy(four(Q_B), r_i[:]), "b_copy")
            mark(dve.tensor_tensor(four(Q_WINTER).rearrange("m r (c j) -> m r c j", j=P),
                                   r_mp[:].unsqueeze(3).to_broadcast(wide), chunks(r_m), ALU.subtract), "w_inter")
            mark(dve.tensor_tensor(four(Q_EMJ), r_t[:], r_m[:], ALU.add), "a_plus_m")
            mark(dve.tensor_tensor(chunks(r_wk), chunks(r_i), m_end.unsqueeze(3).to_broadcast(wide),
                                   ALU.subtract), "w_k")
            dve.wait_ge(prep_act, prep_act_at("lam_exp"))
            mark(dve.scalar_tensor_tensor(neglam[:], lams[:, 3:4], -LAM_INIT, lams[:, 2:3], ALU.add,
                                          ALU.subtract), "neglam")
            conv_final(0, 0)
            conv_taps(0, 1)
            dve.wait_ge(prep_pe, 6)

            def col_banks(b):
                return ps[:, b:b + 2, :].rearrange("p b (c q x) -> p (b c) q x", c=4, q=4)[:, :, :, 0:MH]

            def wk_cols(r):
                n = NC * MH
                return ps[:, 6, 256 + r * n:256 + (r + 1) * n].rearrange("p (c m) -> p c m", c=NC)

            mark(dve.tensor_copy(col[:, 0:NC, 0:4, :], col_banks(2)), "col_fw")
            mark(dve.tensor_copy(colrev[:, :, 0:4, :], col_banks(4)), "col_rev")
            mark(dve.tensor_copy(col[:, 0:NC, Q_WK, :], wk_cols(0)), "wk_fw")
            mark(dve.tensor_copy(colrev[:, :, Q_WK, :], wk_cols(1)), "wk_rev")
            mark(dve.tensor_copy(decay[:], ps[:, 7, 256:256 + 16 * MH].rearrange("p (m c) -> p m c", m=MH)), "decay_all")
            dve.wait_ge(prep_pe, 7)
            mark(dve.tensor_copy(col[:, NC:2 * NC], ps[:, 7, 0:NC * 5 * MH].rearrange(
                "p (c q m) -> p c q m", c=NC, q=5)), "col_bw")
            after_step("col_bw")
            conv_logsig(0, 1)
            conv_final(0, 1)
            qk_low(0, 0)
            qk_low(0, 1)
            v_low(0)

            def gate_abs(h, e, part):
                g, _ = tile_no(G_M, 8, h, 2 * e + part)
                dve.wait_ge(proj_read, 2 * g + 2)
                src = rawb[:] if part == 0 else zg[:, e]
                if part == 0 and e == 1:
                    dve.wait_ge(gate_dve.sem, gate_dve.after(h, 5))
                dve.scalar_tensor_tensor(ab[:, part], src, -1.0, src, ALU.mult, ALU.min).then_inc(gate_dve.sem, 1)

            def gate_logsig(h, e, part):
                n = 6 * e + 2 * part
                dve.wait_ge(gate_act.sem, gate_act.after(h, 5 * e + 2 * part + 1))
                src = rawb[:] if part == 0 else zg[:, e]
                dve.scalar_tensor_tensor(ab[:, part], src, 0.0, ab[:, part], ALU.min,
                                         ALU.subtract).then_inc(gate_dve.sem, 1)
                if part == 1:
                    dve.wait_ge(gate_dve.sem, gate_dve.after(h, n + 1))
                    dve.tensor_tensor(ab[:, 1], ab[:, 0], ab[:, 1], ALU.add).then_inc(gate_dve.sem, 1)

            def gate_final(h, e):
                dve.wait_ge(gate_act.sem, gate_act.after(h, 5 * e + 4))
                dve.scalar_tensor_tensor(zg[:, e], zg[:, e], hg[:, e:e + 1], ab[:, 1], ALU.mult,
                                         ALU.mult).then_inc(gate_dve.sem, 1)

            def chunk(r, t):
                return t if r == 0 else NC - 1 - t

            def diagonals(h, t):
                if t == 0:
                    dve.wait_ge(hcols.sem, hcols.after(h, 0))
                else:
                    dve.wait_ge(score_done.sem, score_done.after(h, t - 1))
                for r in range(2):
                    d = dve.tensor_scalar(dg[:, r], ident[:], hc[:, 8 * r + t, Q_NEGM:Q_NEGM + 1], None, ALU.mult)
                d.then_inc(diag_done.sem, 1)

            def m_step(h, t):
                if t < NC - 1:
                    diagonals(h, t + 1)
                dve.wait_ge(w_done.sem, w_done.after(h, t))
                if t > 0:
                    dve.wait_ge(ptlo_done.sem, ptlo_done.after(h, t - 1))
                dve.tensor_tensor(ptf[:], ps[:, 2, 0:2 * P].rearrange("p (r j) -> p r j", r=2), wt[:],
                                  ALU.mult).then_inc(ptf_done.sem, 1)
                dve.wait_ge(pthi_done.sem, pthi_done.after(h, t))
                dve.tensor_tensor(pt[:, 1], ptf[:], pt[:, 0].bitcast(F32), ALU.subtract).then_inc(ptlo_done.sem, 1)
                if t < NC - 1:
                    dve.wait_ge(kwhi_done.sem, kwhi_done.after(h, t))
                    for r in range(2):
                        lo = dve.scalar_tensor_tensor(kw[:, 1, r], kseq[:, chunk(r, t)], hc[:, 8 * r + t, Q_WK:Q_WK + 1],
                                                      kw[:, 0, r].bitcast(F32), ALU.mult, ALU.subtract)
                    lo.then_inc(kwlo_done.sem, 1)
                if t == 2:
                    gate_abs(h, 0, 0)
                elif t == 3:
                    gate_logsig(h, 0, 0)
                elif t == 4:
                    gate_abs(h, 0, 1)
                elif t == 5:
                    gate_logsig(h, 0, 1)
                elif t == 6:
                    gate_final(h, 0)
                    gate_abs(h, 1, 0)
                elif t == 7:
                    gate_logsig(h, 1, 0)
                dve.wait_ge(intra_done.sem, intra_done.after(h, t))
                intra = ps[:, 4, :].rearrange("p (r e) -> p r e", r=2)
                if t > 0:
                    dve.wait_ge(intersc_done.sem, intersc_done.after(h, t - 1))
                    dve.tensor_tensor(num[:], intra, num[:], ALU.add).then_inc(num_done.sem, 1)
                else:
                    dve.tensor_copy(num[:], intra).then_inc(num_done.sem, 1)
                if t < NC - 1:
                    dve.wait_ge(upd_done.sem, upd_done.after(h, t))
                    upd = ps[:, 6, :].rearrange("p (r e) -> p r e", r=2)
                    nup = ps[:, 7, 8:12].rearrange("p (r two) -> p r two", r=2)
                    if t == 0:
                        dve.tensor_copy(cf[:, :, 0:MV], upd)
                        d = dve.tensor_copy(cf[:, :, MV:MV + 2], nup)
                    else:
                        dve.wait_ge(clo_done.sem, clo_done.after(h, t - 1))
                        for r in range(2):
                            dve.scalar_tensor_tensor(cf[:, r, 0:MV], cf[:, r, 0:MV], hd[:, 8 * r + t:8 * r + t + 1],
                                                     upd[:, r], ALU.mult, ALU.add)
                            d = dve.scalar_tensor_tensor(cf[:, r, MV:MV + 2], cf[:, r, MV:MV + 2],
                                                         hd[:, 8 * r + t:8 * r + t + 1], nup[:, r], ALU.mult, ALU.add)
                    d.then_inc(state_done.sem, 1)
                dve.tensor_copy(dsm[:, 0], ps[:, 7, 0:4].rearrange("p (r two) -> p r two", two=2)[:, :, 0]) \
                    .then_inc(den_chain.sem, 1)
                dve.wait_ge(den_chain.sem, den_chain.after(h, 5 * t))
                if t > 0:
                    for r in range(2):
                        d = dve.scalar_tensor_tensor(dsm[:, 1, r:r + 1], ps[:, 7, 4 + 2 * r:5 + 2 * r],
                                                     hc[:, 8 * r + t, Q_WINTER:Q_WINTER + 1], dsm[:, 0, r:r + 1],
                                                     ALU.mult, ALU.add)
                    d.then_inc(den_chain.sem, 1)
                else:
                    dve.tensor_copy(dsm[:, 1], dsm[:, 0]).then_inc(den_chain.sem, 1)
                dve.wait_ge(den_chain.sem, den_chain.after(h, 5 * t + 1))
                dve.tensor_scalar(dsm[:, 0], dsm[:, 1], -1.0, None, ALU.mult).then_inc(den_chain.sem, 1)
                dve.wait_ge(den_chain.sem, den_chain.after(h, 5 * t + 2))
                for r in range(2):
                    d = dve.scalar_tensor_tensor(dsm[:, 2, r:r + 1], dsm[:, 1, r:r + 1],
                                                 hc[:, 8 * r + t, Q_EMJ:Q_EMJ + 1], dsm[:, 0, r:r + 1],
                                                 ALU.max, ALU.max)
                d.then_inc(den_chain.sem, 1)
                dve.wait_ge(den_chain.sem, den_chain.after(h, 5 * t + 3))
                dve.reciprocal(dsm[:, 3], dsm[:, 2]).then_inc(den_chain.sem, 1)
                if t < NC - 1:
                    dve.wait_ge(chi_done.sem, chi_done.after(h, t))
                    dve.tensor_tensor(cs[:, 1], cf[:], cs[:, 0].bitcast(F32), ALU.subtract).then_inc(clo_done.sem, 1)
                dve.wait_ge(den_chain.sem, den_chain.after(h, 5 * t + 4))
                dve.wait_ge(num_done.sem, num_done.after(h, t))
                if t > 0:
                    dve.wait_ge(h_done.sem, h_done.after(h, t - 1))
                for r in range(2):
                    c = chunk(r, t)
                    if t < NC // 2:
                        d = dve.tensor_scalar(hacc[:, c], num[:, r], dsm[:, 3, r:r + 1], None, ALU.mult)
                    else:
                        d = dve.scalar_tensor_tensor(hacc[:, c], num[:, r], dsm[:, 3, r:r + 1], hacc[:, c],
                                                     ALU.mult, ALU.add)
                d.then_inc(h_done.sem, 1)

            def h_out(h):
                for k in range(4):
                    e, i = divmod(k, 2)
                    dve.wait_ge(tr_done.sem, tr_done.after(h, k))
                    if k > 0:
                        dve.wait_ge(hsplit_done.sem, hsplit_done.after(h, k - 1))
                    dve.tensor_tensor(hst[:], ps[:, (7, 2)[k % 2], :], zg[:, e, i * HALF:(i + 1) * HALF],
                                      ALU.mult).then_inc(tr_read.sem, 1)
                    dve.wait_ge(hsp_hi.sem, hsp_hi.after(h, k))
                    dve.tensor_tensor(hsp[:, 1], hst[:], hsp[:, 0].bitcast(F32), ALU.subtract) \
                        .then_inc(hsplit_done.sem, 1)

            def shuffle(hh, n):
                swap = [(i + ROPE // 2) % ROPE if i < ROPE else i for i in range(32)]
                for half in range(2):
                    cols = slice(half * HALF, (half + 1) * HALF)
                    if is_zero(hh):
                        g, _ = tile_no(G_M, 8, MH - 1, 4 + n // 2)
                    else:
                        g, _ = tile_no(G_A, 4, hh - 1, n // 2)
                    dve.wait_ge(proj_read, 2 * g + half + 1)
                    dve.sem_inc(step_begun, 1)
                    dve.stream_shuffle((rawa, rawb)[n // 2][:, cols], qkf[:, n // 2, cols], swap).then_inc(shuf_done, 1)

            own = (slice(0, AD), slice(AD, P))

            def k_low(hh):
                for c in range(2):
                    dve.wait_ge(a_qk_hi.sem, a_qk_hi.after(hh, c))
                    dve.tensor_tensor(ks[own[c], c, 1], qkf[own[c], 1], ks[own[c], c, 0].bitcast(F32),
                                      ALU.subtract).then_inc(a_qk_lo.sem, 1)

            def q_low(hh, c):
                dve.wait_ge(a_qk_hi.sem, a_qk_hi.after(hh, 2 + c))
                dve.tensor_tensor(qs[own[1 - c], c], qkf[own[c], 0], qs[own[c], c].bitcast(F32),
                                  ALU.subtract).then_inc(a_qk_lo.sem, 1)

            def m_head(h, last):
                dve.tensor_copy(hc[:], col[:, :, :, bass.ds(h, 1)].rearrange("p c q one -> p c (q one)")) \
                    .then_inc(hcols.sem, 1)
                dve.tensor_copy(hd[:], decay[:, bass.ds(h, 1), :].rearrange("p one c -> p (one c)")).then_inc(hcols.sem, 1)
                dve.tensor_copy(hg[:], vecs[:, bass.ds(V_MG + 2 * h, 2)]).then_inc(hcols.sem, 1)
                nxt = (h + 1) if not last else 0
                dve.tensor_copy(hcv[:], conv_cols[:, :, :, bass.ds(nxt, 1)].rearrange("p q w one -> p q (w one)")) \
                    .then_inc(hcols.sem, 1)
                diagonals(h, 0)
                for t in range(NC):
                    m_step(h, t)
                gate_abs(h, 1, 1)
                gate_logsig(h, 1, 1)
                if not last:
                    conv_taps(h + 1, 0)
                else:
                    shuffle(0, 0)
                gate_final(h, 1)
                dve.wait_ge(hs_act.sem, hs_act.after(h, 2))
                for c in range(NC):
                    d = dve.tensor_scalar(hacc[:, c], hacc[:, c], hstat[:, 1, c:c + 1], None, ALU.mult)
                d.then_inc(hs_done.sem, 1)
                if not last:
                    conv_logsig(h + 1, 0)
                    conv_final(h + 1, 0)
                    conv_taps(h + 1, 1)
                else:
                    shuffle(0, 2)
                h_out(h)
                if not last:
                    conv_logsig(h + 1, 1)
                    conv_final(h + 1, 1)
                    qk_low(h + 1, 0)
                    qk_low(h + 1, 1)
                    v_low(h + 1)
                else:
                    k_low(0)
                    for c in range(2):
                        q_low(0, c)

            with dve.Fori(0, MH - 1) as h:
                m_head(h, False)
            m_head(MH - 1, True)

            def mix(h, q):
                b = q % 2
                dve.wait_ge(a_exp.sem, a_exp.after(h, 2 * q + 1))
                dve.reciprocal(rden[:, 0], den[:, b]).then_inc(a_mix.sem, 1)
                dve.wait_ge(a_mix.sem, a_mix.after(h, 4 * q))
                dve.tensor_scalar(rden[:, 1, 0:1], rden[:, 0, 1:2], neglam[:], None, ALU.mult).then_inc(a_mix.sem, 1)
                if q >= 2:
                    dve.wait_ge(a_tr.sem, a_tr.after(h, round_of(q - 2, 1)))
                dve.tensor_scalar(am[b][:], pr[:, 0], rden[:, 0, 0:1], None, ALU.mult).then_inc(a_mix.sem, 1)
                dve.wait_ge(a_mix.sem, a_mix.after(h, 4 * q + 2))
                dve.scalar_tensor_tensor(am[b][:], pr[:, 1], rden[:, 1, 0:1], am[b][:], ALU.mult,
                                         ALU.add).then_inc(a_mix.sem, 1)

            def maxima(h, q):
                for c in range(2):
                    dve.wait_ge(a_score.sem, a_score.after(h, 2 * q + c))
                    dve.tensor_reduce(nmax[:, q % 2, c:c + 1], ps[:, 2 + 2 * c:4 + 2 * c, :].rearrange("p b k -> p (b k)"),
                                      AX_X, ALU.max, negate=True).then_inc(a_max.sem, 1)

            def a_low_round(h, k, dst):
                dve.wait_ge(a_tr_hi.sem, a_tr_hi.after(h, k))
                dve.tensor_tensor(dst(1), ps[:, 6, :].rearrange("p (k s) -> p k s", k=4), dst(0).bitcast(F32),
                                  ALU.subtract).then_inc(a_tr_read.sem, 1)

            def v_dst(i):
                return lambda p: va[:, p, 4 * i:4 * i + 4, :]

            def at_dst(q, i):
                return lambda p: at_s[:, p, 4 * i:4 * i + 4, (q % 2) * P:(q % 2 + 1) * P]

            def o_square(h, n):
                dve.wait_ge(a_of.sem, a_of.after(h, n))
                dve.tensor_tensor(osq[:], of[:], of[:], ALU.mult).then_inc(a_osq.sem, 1)

            def o_out_gate(h, n):
                dve.wait_ge(a_rs.sem, a_rs.after(h, 2 * n + 1))
                if n > 0:
                    dve.wait_ge(a_olo.sem, a_olo.after(h, n - 1))
                dve.tensor_tensor(ost[:], of[:], ors[:], ALU.mult).then_inc(a_ost.sem, 1)
                dve.wait_ge(a_ost.sem, a_ost.after(h, 2 * n))
                dve.tensor_tensor(ost[:], ost[:], ga[:, 2 * n * P:2 * (n + 1) * P], ALU.mult).then_inc(a_ost.sem, 1)
                dve.wait_ge(a_ohi.sem, a_ohi.after(h, n))
                dve.tensor_tensor(osp[:, 1], ost[:], osp[:, 0].bitcast(F32), ALU.subtract).then_inc(a_olo.sem, 1)

            def a_head(h, first, last):
                maxima(h, 0)
                dve.scalar_tensor_tensor(aw[:], vz[:, 1], -1.0, vz[:, 1], ALU.mult, ALU.min) \
                    .then_inc(a_gate_dve.sem, 1)
                a_low_round(h, V_ROUND[0], v_dst(0))
                mix(h, 0)
                for q in range(ST):
                    a_low_round(h, round_of(q, 0), at_dst(q, 0))
                    if q + 1 < ST:
                        maxima(h, q + 1)
                    elif not last:
                        q_low(h + 1, 0)
                    a_low_round(h, round_of(q, 1), at_dst(q, 1))
                    if q + 1 < ST:
                        mix(h, q + 1)
                    elif not last:
                        q_low(h + 1, 1)
                    if q == 0:
                        a_low_round(h, V_ROUND[1], v_dst(1))
                    if q == 0:
                        if not first:
                            o_out_gate(h - 1, 3)
                        dve.wait_ge(a_gate_act.sem, a_gate_act.after(h, 1))
                        dve.scalar_tensor_tensor(aw[:], vz[:, 1], 0.0, aw[:], ALU.min, ALU.subtract) \
                            .then_inc(a_gate_dve.sem, 1)
                    if q == 1:
                        dve.wait_ge(a_gate_act.sem, a_gate_act.after(h, 2))
                        dve.scalar_tensor_tensor(ga[:], vz[:, 1], again[:], aw[:], ALU.mult, ALU.mult) \
                            .then_inc(a_gate_dve.sem, 1)
                    if not last and q == 6:
                        k_low(h + 1)
                    if q in (2, 4):
                        o_out_gate(h, q // 2 - 1)
                    if q == 7:
                        o_out_gate(h, 2)
                    if not last and q in (1, 3):
                        shuffle(h + 1, q - 1)
                    if q % 2 == 1:
                        o_square(h, q // 2)

            a_head(0, True, False)
            with dve.Fori(1, AH - 1) as h:
                a_head(h, False, False)
            a_head(AH - 1, False, True)
            o_out_gate(AH - 1, 3)

            def merge(n, base):
                with dve.Fori(0, KT // 2) as c:
                    for par in range(2):
                        i = KT * n + 2 * c + par
                        z = qkf[:, par]
                        dve.wait_ge(g_loaded[par], 16 * (KT // 2 * n + c + 1))
                        dve.wait_ge(f_product, i + 1)
                        dve.scalar_tensor_tensor(fw[:], z, -1.0, z, ALU.mult, ALU.min).then_inc(f_abs, 1)
                        dve.wait_ge(f_act, 3 * i + 2)
                        dve.scalar_tensor_tensor(fw[:], z, 0.0, fw[:], ALU.min, ALU.subtract).then_inc(f_logsig, 1)
                        g, _ = tile_no(base, 2, c, par)
                        dve.wait_ge(proj_read, 2 * g + 2)
                        dve.wait_ge(f_act, 3 * i + 3)
                        yd = ya[:, bass.ds(2 * c + par, 1), :].rearrange("p one s -> p (one s)")
                        if n == 0:
                            dve.tensor_tensor(yd, fw[:], fb[:], ALU.mult).then_inc(f_product, 1)
                        else:
                            dve.tensor_tensor(fw[:], fw[:], fb[:], ALU.mult).then_inc(f_product, 1)
                            dve.wait_ge(f_product, i + 2)
                            dve.tensor_tensor(yd, yd, fw[:], ALU.add).then_inc(f_y, 1)
                            dve.wait_ge(y_hi, 2 * c + par + 1)
                            dve.tensor_tensor(ys[:, 1, bass.ds(2 * c + par, 1), :].rearrange("p one s -> p (one s)"), yd,
                                              ys[:, 0, bass.ds(2 * c + par, 1), :].rearrange(
                                                  "p one s -> p (one s)").bitcast(F32),
                                              ALU.subtract).then_inc(y_lo, 1)

            dve.sem_inc(f_product, 1)
            merge(0, G_FA)
            merge(1, G_FB)

            def rows(c, par):
                for i in range(2):
                    dve.wait_ge(o_tr, 2 * c + i + 1)
                    dst = orow[:, 4 * i:4 * i + 4, bass.ds(c * P, P)]
                    dve.tensor_copy(dst, ps[:, 2 + 2 * par + i, :].rearrange("p (t s) -> p t s", t=4)).then_inc(o_rows, 1)

            with dve.Fori(0, KT // 2) as c2:
                for par in range(2):
                    rows(2 * c2 + par, par)
            dve.wait_ge(res_loaded, 16 * ST)
            dve.wait_ge(o_stat, 2)
            dve.wait_ge(o_rows, 2 * KT)
            for t in range(ST):
                dve.scalar_tensor_tensor(orow[:, t], orow[:, t], tail_stat[:, t:t + 1], xres[:, t],
                                         ALU.mult, ALU.add).then_inc(o_out, 1)

        @block.scalar
        def _(act):
            def mark(ins, name):
                assert name in PREP_ACT
                ins.then_inc(prep_act, 1)

            def read_half(base, per_head, h, j, half, dst, scale=1.0, bias=None):
                g, _ = tile_no(base, per_head, h, j)
                act.wait_ge(proj_done, 2 * g + half + 1)
                if bias is None:
                    act.activation(dst, ps[:, half, :], ACT.Copy, scale=scale).then_inc(proj_read, 1)
                else:
                    act.activation(dst, ps[:, half, :], ACT.Identity, bias=bias).then_inc(proj_read, 1)

            def exp_ln(t, sig, waits_own):
                act.activation(t, t, ACT.Exp).then_inc(sig, 1)
                act.wait_ge(sig, waits_own)
                act.activation(t, t, ACT.Ln, bias=1.0).then_inc(sig, 1)

            act.preload_act_table_set("natural_log_exp_and_others")
            act.sem_inc(spilled[0], 16)
            act.sem_inc(spilled[1], 16)

            def x_high(t):
                for i in range(2):
                    act.wait_ge(x_tr, 2 * t + i + 1)
                    act.activation(xs[:, 0, 4 * i:4 * i + 4, t * P:(t + 1) * P],
                                   ps[:, 2 + 2 * (t % 2) + i, :].rearrange("p (k s) -> p k s", k=4),
                                   ACT.Copy).then_inc(x_hi, 1)

            act.wait_ge(consts_set, 1)
            for t in range(ST):
                act.wait_ge(x_loaded[t % 4], 16 * (t // 4 + 1))
                act.activation(rawb[:], xin[t % 4], ACT.Square, accum_out=xstat[:, 0, t:t + 1]).then_inc(x_stat, 1)
                act.wait_ge(x_stat, 3 * t + 1)
                act.activation(xstat[:, 1, t:t + 1], xstat[:, 0, t:t + 1], ACT.Ln, bias=eps[:], scale=1.0 / D) \
                    .then_inc(x_stat, 1)
                act.wait_ge(x_stat, 3 * t + 2)
                act.activation(xstat[:, 1, t:t + 1], xstat[:, 1, t:t + 1], ACT.Exp, scale=-0.5).then_inc(x_stat, 1)
                if t > 0:
                    x_high(t - 1)
            x_high(ST - 1)

            def conv_exp_ln(hn, j):
                act.wait_ge(conv_dve.sem, conv_dve.after(hn, 7 * j + CONV))
                exp_ln(qkf[:, j], conv_act.sem, conv_act.after(hn, 3 * j))

            def conv_exp(hn, j):
                act.wait_ge(conv_dve.sem, conv_dve.after(hn, 7 * j + 5))
                act.activation(qkf[:, j], qkf[:, j], ACT.Exp).then_inc(conv_act.sem, 1)

            def qk_high(hn, j):
                act.wait_ge(conv_dve.sem, conv_dve.after(hn, 7 * j + 6))
                act.activation((qT, kT)[j][:, 0], qkf[:, j], ACT.Copy).then_inc(qk_hi.sem, 1)

            def read_conv(base, per_head, h, hn, j, tile):
                if j == 1:
                    act.wait_ge(conv_dve.sem, conv_dve.after(hn, CONV - 1))
                for half in range(2):
                    at = CONV // 2 + half * HALF
                    read_half(base, per_head, h, tile, half, rawa[:, at:at + HALF])

            def kv_high(h):
                for i in range(2):
                    act.wait_ge(tr_done.sem, tr_done.after(h, 4 + i))
                    act.activation(kseq[:, 4 * i:4 * i + 4], ps[:, (7, 2)[i], :].rearrange("p (c d) -> p c d", c=4),
                                   ACT.Copy).then_inc(tr_read.sem, 1)
                for k in range(4):
                    e, i = divmod(k, 2)
                    act.wait_ge(tr_done.sem, tr_done.after(h, 6 + k))
                    act.activation(vS[:, 0, 4 * i:4 * i + 4, e * P:(e + 1) * P],
                                   ps[:, (7, 2)[k % 2], :].rearrange("p (c d) -> p c d", c=4),
                                   ACT.Copy).then_inc(tr_hi.sem, 1)

            def read_gate(base, per_head, h, j, half, n, buf, bias):
                if half == 0 and not (isinstance(n, int) and n < 2):
                    act.wait_ge(g_spilled[j % 2], 16 * ((KT + 4) // 2 - 2 + h if not isinstance(n, int) else n // 2))
                read_half(base, per_head, h, j, half, buf[:, j % 2, half * HALF:(half + 1) * HALF], bias=bias)
                if half == 1:
                    g, _ = tile_no(base, per_head, h, j)
                    act.wait_ge(proj_read, 2 * g + 2)
                    act.dma_start(spill_g[bass.ds(n, 1)].rearrange("one p s -> (one p) s"), buf[:, j % 2]) \
                        .then_inc(g_spilled[j % 2], 16)

            def read_gates(base, j0, numbers, buf):
                for n in numbers:
                    for half in range(2):
                        read_gate(base, 0, 0, j0 + n - numbers[0], half, n, buf, bmerge[:, n:n + 1])

            act.wait_ge(prep_dve, prep_dve_at("bmerge"))
            act.wait_ge(consts_set, 3)
            read_conv(0, 0, 0, 0, 0, 0)
            conv_exp_ln(0, 0)
            read_conv(0, 0, 0, 0, 1, 1)
            act.wait_ge(prep_dve, prep_dve_at("abs_f"))
            t_flat = r_t[:].rearrange("m r j -> m (r j)")
            mark(act.activation(t_flat, t_flat, ACT.Exp), "exp_f")
            act.wait_ge(prep_act, prep_act_at("exp_f"))
            mark(act.activation(t_flat, t_flat, ACT.Ln, bias=1.0), "ln_f")
            conv_exp(0, 0)
            read_gates(0, 2, range(0, 2), gate_fill)
            mark(act.activation(lams[:, 2:4], lams[:, 0:2], ACT.Exp), "lam_exp")
            act.wait_ge(prep_dve, prep_dve_at("decay"))
            mark(act.activation(r_dec[:], r_dec[:], ACT.Exp), "decay")
            act.wait_ge(prep_dve, prep_dve_at("w_inter"))
            w_row, e_row = r_four[64:64 + MH], r_four[96:96 + MH]
            mark(act.activation(w_row, w_row, ACT.Exp), "w_inter")
            act.wait_ge(prep_dve, prep_dve_at("a_plus_m"))
            mark(act.activation(e_row, e_row, ACT.Exp, scale=-1.0), "emj")
            act.wait_ge(prep_dve, prep_dve_at("w_k"))
            mark(act.activation(r_wk[:], r_wk[:], ACT.Exp), "w_k")
            read_gates(0, 4, range(2, 4), gate_fill)
            conv_exp_ln(0, 1)
            conv_exp(0, 1)
            for e in range(2):
                for half in range(2):
                    read_half(0, 0, 0, 6 + e, half, vz[:, e, half * HALF:(half + 1) * HALF])
            for j in range(2):
                act.wait_ge(g_spilled[j], 16 * 2)
            qk_high(0, 0)
            qk_high(0, 1)
            kv_high(-1)

            def chunk(r, t):
                return t if r == 0 else NC - 1 - t

            def gate_exp_ln(h, e, part):
                n = 6 * e + (0, 2)[part]
                act.wait_ge(gate_dve.sem, gate_dve.after(h, n))
                exp_ln(ab[:, part], gate_act.sem, gate_act.after(h, 5 * e + 2 * part))

            def gate_exp(h, e):
                act.wait_ge(gate_dve.sem, gate_dve.after(h, 6 * e + 4))
                act.activation(ab[:, 1], ab[:, 1], ACT.Exp).then_inc(gate_act.sem, 1)

            def m_step(h, t):
                act.wait_ge(score_done.sem, score_done.after(h, t))
                if t == 0:
                    act.wait_ge(hcols.sem, hcols.after(h, 0))
                else:
                    act.wait_ge(ptf_done.sem, ptf_done.after(h, t - 1))
                for r in range(2):
                    a = act.activation(wt[:, r], ps[:, 3, r * P:(r + 1) * P], ACT.Exp,
                                       bias=hc[:, 8 * r + t, Q_B:Q_B + 1])
                a.then_inc(w_done.sem, 1)
                act.wait_ge(ptf_done.sem, ptf_done.after(h, t))
                if t > 0:
                    act.wait_ge(intra_done.sem, intra_done.after(h, t - 1))
                act.activation(pt[:, 0], ptf[:], ACT.Copy).then_inc(pthi_done.sem, 1)
                if t < NC - 1:
                    if t > 0:
                        act.wait_ge(upd_done.sem, upd_done.after(h, t - 1))
                    else:
                        act.wait_ge(tr_read.sem, tr_read.after(h - 1, 5))
                    for r in range(2):
                        a = act.activation(kw[:, 0, r], kseq[:, chunk(r, t)], ACT.Copy,
                                           scale=hc[:, 8 * r + t, Q_WK:Q_WK + 1])
                    a.then_inc(kwhi_done.sem, 1)
                if t == 3:
                    gate_exp_ln(h, 0, 0)
                elif t == 5:
                    gate_exp_ln(h, 0, 1)
                elif t == 6:
                    gate_exp(h, 0)
                elif t == 7:
                    gate_exp_ln(h, 1, 0)
                j, half = divmod(t, 2)
                cols = slice(half * HALF, (half + 1) * HALF)
                if t == 4:
                    act.wait_ge(gate_dve.sem, gate_dve.after(h, 1))
                read_half(G_M, 8, h, j, half, rawb[:, cols] if j % 2 == 0 else zg[:, j // 2, cols])
                if t > 0:
                    act.wait_ge(inter_done.sem, inter_done.after(h, t - 1))
                    act.wait_ge(h_done.sem, h_done.after(h, t - 1))
                    for r in range(2):
                        a = act.activation(num[:, r], ps[:, 5, r * MV:(r + 1) * MV], ACT.Copy,
                                           scale=hc[:, 8 * r + t, Q_WINTER:Q_WINTER + 1])
                    a.then_inc(intersc_done.sem, 1)
                if t < NC - 1:
                    act.wait_ge(state_done.sem, state_done.after(h, t))
                    act.activation(cs[:, 0], cf[:], ACT.Copy).then_inc(chi_done.sem, 1)

            own = (slice(0, AD), slice(AD, P))

            def k_high(hh):
                act.wait_ge(rope_done, 3 * (4 * hh + 3) + 3)
                for c in range(2):
                    act.activation(ks[own[c], c, 0], qkf[own[c], 1], ACT.Copy).then_inc(a_qk_hi.sem, 1)

            def q_high(hh):
                for c in range(2):
                    act.activation(qs[own[c], c], qkf[own[c], 0], ACT.Copy).then_inc(a_qk_hi.sem, 1)

            def read_rope(base, per_head, h, hh, n, half):
                if half == 0 and not is_zero(hh):
                    act.wait_ge(a_qk_lo.sem, a_qk_lo.after(hh, 3) - 4)
                read_half(base, per_head, h, (4 if is_zero(hh) else 0) + n // 2, half,
                          qkf[:, n // 2, half * HALF:(half + 1) * HALF], scale=(AD ** -0.5 if n == 0 else 1.0))

            def m_head(h, last):
                for t in range(NC):
                    m_step(h, t)
                gate_exp_ln(h, 1, 1)
                if not last:
                    read_conv(G_M, 8, h, h + 1, 0, 4)
                else:
                    for half in range(2):
                        read_rope(G_M, 8, h, 0, 0, half)
                gate_exp(h, 1)
                act.wait_ge(h_done.sem, h_done.after(h, NC - 1))
                junk = kseq[:].rearrange("p c d -> p (c d)").bitcast(mybir.dt.bfloat16)
                for c in range(NC):
                    a = act.activation(junk[:, c * MV:(c + 1) * MV], hacc[:, c], ACT.Square,
                                       accum_out=hstat[:, 0, c:c + 1])
                a.then_inc(hs_act.sem, 1)
                act.wait_ge(hs_act.sem, hs_act.after(h, 0))
                act.activation(hstat[:, 1], hstat[:, 0], ACT.Ln, bias=eps[:], scale=1.0 / MV).then_inc(hs_act.sem, 1)
                act.wait_ge(hs_act.sem, hs_act.after(h, 1))
                act.activation(hstat[:, 1], hstat[:, 1], ACT.Exp, scale=-0.5).then_inc(hs_act.sem, 1)
                if not last:
                    conv_exp_ln(h + 1, 0)
                    conv_exp(h + 1, 0)
                    read_conv(G_M, 8, h, h + 1, 1, 5)
                else:
                    for half in range(2):
                        read_rope(G_M, 8, h, 0, 2, half)
                for k in range(4):
                    e, i = divmod(k, 2)
                    act.wait_ge(tr_read.sem, tr_read.after(h, k))
                    act.wait_ge(spilled[0], 16 * (4 * h + (k + 1)))
                    act.activation(hsp[:, 0], hst[:], ACT.Copy).then_inc(hsp_hi.sem, 1)
                    act.wait_ge(hsplit_done.sem, hsplit_done.after(h, k))
                    act.dma_start(spill_m[:, bass.ds(2 * h + e, 1), :, i * HALF:(i + 1) * HALF].rearrange(
                        "i one p s -> p i (one s)"), hsp[:].bitcast(F32)).then_inc(spilled[0], 16)
                if not last:
                    conv_exp_ln(h + 1, 1)
                    for e in range(2):
                        for half in range(2):
                            read_half(G_M, 8, h, 6 + e, half, vz[:, e, half * HALF:(half + 1) * HALF])
                        if e == 0:
                            conv_exp(h + 1, 1)
                            qk_high(h + 1, 0)
                            qk_high(h + 1, 1)
                    kv_high(h)
                else:
                    for e in range(2):
                        for half in range(2):
                            read_half(G_M, 8, h, 6 + e, half, vz[:, e, half * HALF:(half + 1) * HALF])
                    k_high(0)
                    q_high(0)

            with act.Fori(0, MH - 1) as h:
                m_head(h, False)
            m_head(MH - 1, True)

            def exps(h, q, comps=(0, 1)):
                b = q % 2
                if q > 0 and 0 in comps:
                    act.wait_ge(a_mix.sem, a_mix.after(h, 4 * q - 1))
                for c in comps:
                    act.wait_ge(a_max.sem, a_max.after(h, 2 * q + c))
                    act.activation(pr[:, c], ps[:, 2 + 2 * c:4 + 2 * c, :].rearrange("p b k -> p (b k)"), ACT.Exp,
                                   bias=nmax[:, b, c:c + 1], accum_out=den[:, b, c:c + 1]).then_inc(a_exp.sem, 1)

            def high_round(h, k, dst):
                act.wait_ge(a_tr.sem, a_tr.after(h, k))
                act.activation(dst, ps[:, 6, :].rearrange("p (k s) -> p k s", k=4), ACT.Copy).then_inc(a_tr_hi.sem, 1)

            def at_dst(q, i):
                return at_s[:, 0, 4 * i:4 * i + 4, (q % 2) * P:(q % 2 + 1) * P]

            def o_read(h, n):
                act.wait_ge(a_pv.sem, a_pv.after(h, n))
                if n > 0:
                    act.wait_ge(a_ost.sem, a_ost.after(h, 2 * (n - 1)))
                act.activation(of[:], ps[:, 7, 0:2 * P], ACT.Copy).then_inc(a_of.sem, 1)

            def o_rstd(h, n):
                act.wait_ge(a_ss.sem, a_ss.after(h, n))
                if n > 0:
                    act.wait_ge(a_ost.sem, a_ost.after(h, 2 * (n - 1)))
                act.activation(ors[:], ps[:, 7, 2 * P:4 * P], ACT.Ln, bias=eps[:], scale=1.0 / AV).then_inc(a_rs.sem, 1)
                act.wait_ge(a_rs.sem, a_rs.after(h, 2 * n))
                act.activation(ors[:], ors[:], ACT.Exp, scale=-0.5).then_inc(a_rs.sem, 1)

            def o_high(h, n):
                act.wait_ge(a_ost.sem, a_ost.after(h, 2 * n + 1))
                act.wait_ge(spilled[1], 16 * (4 * h + (n + 1)))
                act.activation(osp[:, 0], ost[:], ACT.Copy).then_inc(a_ohi.sem, 1)

            def a_head(h, first, last):
                def read_filler(n):
                    j, half = divmod(n, 2)
                    if last:
                        read_gate(G_GL, 0, 0, j, half, 4 + j, qkf, bmerge[:, 4 + j:5 + j])
                        return
                    if j < 2:
                        read_rope(G_A, 4, h, h + 1, 2 * j, half)
                        return
                    if n == 4:
                        act.wait_ge(a_tr.sem, a_tr.after(h, V_ROUND[1]))
                    if n == 6:
                        act.wait_ge(a_gate_dve.sem, a_gate_dve.after(h, 2))
                    read_half(G_A, 4, h, j, half, vz[:, j - 2, half * HALF:(half + 1) * HALF])

                exps(h, 0)
                if not first:
                    act.wait_ge(a_pv.sem, a_pv.after(h - 1, 3))
                high_round(h, 0, va[:, 0, 0:4, :])
                act.wait_ge(a_gate_dve.sem, a_gate_dve.after(h, 0))
                exp_ln(aw[:], a_gate_act.sem, a_gate_act.after(h, 0))
                read_filler(0)
                if not first:
                    o_rstd(h - 1, 3)
                for q in range(ST):
                    if q % 2 == 0 and q > 0:
                        act.wait_ge(a_pv.sem, a_pv.after(h, q // 2 - 1))
                    high_round(h, round_of(q, 0), at_dst(q, 0))
                    if q + 1 < ST:
                        exps(h, q + 1, (0,))
                    elif not last:
                        q_high(h + 1)
                    high_round(h, round_of(q, 1), at_dst(q, 1))
                    if q + 1 < ST:
                        exps(h, q + 1, (1,))
                    if q == 0:
                        high_round(h, V_ROUND[1], va[:, 0, 4:8, :])
                    if q % 2 == 0 and q > 0:
                        o_rstd(h, q // 2 - 1)
                    if not last and q == 6:
                        act.wait_ge(a_score.sem, a_score.after(h, 15))
                        k_high(h + 1)
                    if q + 1 < ST:
                        read_filler(q + 1)
                    if q == 0 and not first:
                        o_high(h - 1, 3)
                    if q == 0:
                        act.wait_ge(a_gate_dve.sem, a_gate_dve.after(h, 1))
                        act.activation(aw[:], aw[:], ACT.Exp).then_inc(a_gate_act.sem, 1)
                    if q in (2, 4):
                        o_high(h, q // 2 - 1)
                    if q == 7:
                        o_high(h, 2)
                    if q % 2 == 1:
                        o_read(h, q // 2)

            act.wait_ge(spilled[0], 16 + 16 * 4 * MH)
            a_head(0, True, False)
            with act.Fori(1, AH - 1) as h:
                a_head(h, False, False)
            a_head(AH - 1, False, True)
            o_rstd(AH - 1, 3)
            o_high(AH - 1, 3)

            with act.Fori(0, 4) as c:
                for j in range(2):
                    act.activation(fbias[:, j:j + 1], bmerge[:, bass.ds(8 + j + 2 * c, 1)], ACT.Copy).then_inc(bias_set, 1)
                    act.wait_ge(bias_set, 2 * c + (j + 1))
                    for half in range(2):
                        read_gate(G_G, 2, c, j, half, 8 + j + 2 * c, qkf, fbias[:, j:j + 1])

            def merge(n, base):
                with act.Fori(0, KT // 2) as c:
                    for par in range(2):
                        i = KT * n + 2 * c + par
                        act.wait_ge(f_abs, i + 1)
                        act.activation(fw[:], fw[:], ACT.Exp).then_inc(f_act, 1)
                        act.wait_ge(f_act, 3 * i + 1)
                        act.activation(fw[:], fw[:], ACT.Ln, bias=1.0).then_inc(f_act, 1)
                        act.wait_ge(f_logsig, i + 1)
                        act.activation(fw[:], fw[:], ACT.Exp).then_inc(f_act, 1)
                        for half in range(2):
                            read_half(base, 2, c, par, half, fb[:, half * HALF:(half + 1) * HALF])
                        if n == 1:
                            act.wait_ge(f_y, 2 * c + par + 1)
                            act.sem_inc(step_begun, 1)
                            act.activation(ys[:, 0, bass.ds(2 * c + par, 1), :].rearrange("p one s -> p (one s)"),
                                           ya[:, bass.ds(2 * c + par, 1), :].rearrange("p one s -> p (one s)"),
                                           ACT.Copy).then_inc(y_hi, 1)

            merge(0, G_FA)
            merge(1, G_FB)

            def out_tile(c, par):
                if not (isinstance(c, int) and c < 2):
                    act.wait_ge(o_sums, c - 1)
                    act.sem_inc(step_begun, 1)
                act.activation(gcol[:, par:par + 1], post_g[:, bass.ds(c, 1)], ACT.Copy).then_inc(gcol_set, 1)
                act.wait_ge(gcol_set, c + 1)
                for half in range(2):
                    cols = slice(half * HALF, (half + 1) * HALF)
                    act.wait_ge(proj_done, 2 * (G_O + c) + half + 1)
                    act.activation(outT[par][:, cols], ps[:, half, :], ACT.Copy, scale=gcol[:, par:par + 1])
                    act.activation(sqT[par][:, cols], ps[:, half, :], ACT.Square).then_inc(proj_read, 1)

            for c in range(2):
                out_tile(c, c)
            with act.Fori(1, KT // 2) as c2:
                for par in range(2):
                    out_tile(2 * c2 + par, par)
            act.wait_ge(o_sums, KT)
            act.activation(tail_stat[:], ps[:, 6, 0:2 * ST].rearrange("p (t two) -> p t two", two=2)[:, :, 0], ACT.Ln,
                           bias=eps[:], scale=1.0 / D).then_inc(o_stat, 1)
            act.wait_ge(o_stat, 1)
            act.activation(tail_stat[:], tail_stat[:], ACT.Exp, scale=-0.5).then_inc(o_stat, 1)


_INS = ["x", "pre_norm_g", "w_in", "conv_w", "conv_b", "gate_b", "m_norm_g", "lambda_qk", "a_norm_g",
        "w_branch_m", "w_branch_a", "b_merge", "w_out", "post_norm_g"]


def constants():
    c = np.zeros((P, K_END), np.float32)
    i = np.arange(P)
    c[:, K_ID:K_ID + P] = i[:, None] == i[None, :]
    c[:, K_REV:K_REV + P] = i[:, None] + i[None, :] == P - 1
    c[:, K_MASK:K_MASK + P] = np.where(i[:, None] > i[None, :], MASKED, 0.0)
    c[:, K_MASK + P:K_MASK + 2 * P] = np.where(i[:, None] < i[None, :], MASKED, 0.0)
    inv = np.float32(THETA) ** (-np.arange(0, ROPE, 2, dtype=np.float32) / np.float32(ROPE))
    ang = (np.arange(S, dtype=np.float32)[None, :] * inv[:, None].astype(np.float32)).astype(np.float32)
    c[:, K_COS:K_COS + S] = 1.0
    half = ROPE // 2
    for first in (0, AD):
        for part, sign in ((0, -1.0), (1, 1.0)):
            rows = slice(first + part * half, first + (part + 1) * half)
            c[rows, K_COS:K_COS + S] = np.cos(ang)
            c[rows, K_SIN:K_SIN + S] = sign * np.sin(ang)
    return c


def kernel(**inputs):
    import concourse.bacc as bacc
    from concourse.bass_utils import run_bass_kernel_spmd

    nc = bacc.Bacc("TRN2", target_bir_lowering=False, num_devices=1)
    arrays = {f"in_{n}": np.ascontiguousarray(inputs[n]) for n in _INS}
    arrays["consts"] = constants()
    args = [nc.dram_tensor(n, a.shape, mybir.dt.from_np(a.dtype), kind="ExternalInput").ap()
            for n, a in arrays.items()]
    out = nc.dram_tensor("out", (1, S, D), F32, kind="ExternalOutput").ap()
    hybrid_block(nc, *args, out)
    r = run_bass_kernel_spmd(nc, [arrays], core_ids=[0])
    return r.results[0]["out"]
```

```python
import math
from contextlib import ExitStack

import numpy as np

import concourse.bass as bass
from concourse import mybir

P = 128
D = 1024
S = 1024
KT = D // P
ST = S // P
HALF = 512
MH, MQK, MV = 4, 128, 256
NC = S // P
AH, AD, AV = 8, 64, 128
CONV = 4
THETA, ROPE = 500000.0, AD // 4
EPS = 1e-6
LAM_INIT = 0.8 - 0.6 * math.exp(-0.3 * 0)
MASKED = -1e30

SPLITS = (2 * MH * MQK, MH * MV, 4 * MH, MH * MV, MH * MV, 2 * AH * AD, 2 * AH * AD, AH * AV, AH * AV, 2 * D)
C_MQK, C_MV, C_MG, C_MO, C_MZ, C_AQ, C_AK, C_AV, C_AZ, C_GM, IN_COLS = (
    int(c) for c in np.cumsum((0,) + SPLITS))

G_M = 8
G_A = G_M + 8 * MH
G_GL = G_A + 4 * (AH - 1)
G_G = G_GL + 4
G_FA = G_G + 8
G_FB = G_FA + KT
G_O = G_FB + KT
G_END = G_O + KT

F32 = mybir.dt.float32
F32R = mybir.dt.float32r
ALU = mybir.AluOpType
ACT = mybir.ActivationFunctionType
AX_X = mybir.AxisListType.X
PASSES = ((0, 0), (0, 1), (1, 0))

K_ID, K_REV, K_MASK, K_COS, K_SIN = 0, P, 2 * P, 4 * P, 4 * P + S
K_END = 4 * P + 2 * S

Q_M, Q_B, Q_WINTER, Q_EMJ, Q_WK = range(5)
ROWS = 32 + MH


V_CW, V_CB, V_MG = 0, CONV * 2 * MH, (CONV + 1) * 2 * MH
V_BM, V_AG, V_ROWS = V_MG + KT, V_MG + 3 * KT, V_MG + 3 * KT + 1


PREP_DVE = ("wg_zero", "wg_hi", "wg_lo", "ident_r", "mask_r", "vecs", "conv0", "again", "bmerge", "pick",
            "lam_products", "lam_sums", "i_fw", "i_bw", "f_fw", "f_bw", "abs_f", "log_f", "a", "b",
            "carry", "max", "m_prev", "decay", "w_inter", "a_plus_m", "w_k",
            "neglam", "col_fw", "col_rev", "decay_all", "col_bw")
PREP_ACT = ("lam_exp", "exp_f", "ln_f", "decay", "w_inter", "emj", "w_k")
N_SMALL = 13


def prep_dve_at(name):
    return PREP_DVE.index(name) + 1


def prep_act_at(name):
    return PREP_ACT.index(name) + 1


def is_zero(h):
    return isinstance(h, int) and h == 0


def round_of(q, i):
    return 1 + i if q == 0 else 2 + 2 * q + i


V_ROUND = (0, 3)


class Signal:

    def __init__(self, sem, per_head=1, base=0):
        self.sem, self.per_head, self.base = sem, per_head, base

    def after(self, h, k=0):
        return self.per_head * h + (self.base + k + 1)


def hybrid_block(nc, x, pre_norm_g, w_in, conv_w, conv_b, gate_b, m_norm_g, lambda_qk, a_norm_g,
                 w_branch_m, w_branch_a, b_merge, w_out, post_norm_g, consts, out):
    ctx = ExitStack()
    with ctx:
        def sb(name, shape, dt=F32, at=ctx):
            return at.enter_context(nc.sbuf_tensor(name, shape, dt))

        def sem(name):
            return ctx.enter_context(nc.semaphore(name))

        def signal(name, per_head=1, base=0):
            return Signal(sem(name), per_head, base)

        spill_m = nc.dram_tensor("spill_m", [2, KT, P, S], F32, kind="Internal").ap()
        spill_a = nc.dram_tensor("spill_a", [2, KT, P, S], F32, kind="Internal").ap()
        spill_g = nc.dram_tensor("spill_g", [2 * KT, P, S], F32, kind="Internal").ap()

        x_v = x[0].rearrange("(t p) d -> t p d", p=P)
        out_v = out[0].rearrange("(t p) d -> t p d", p=P)
        w_in_v = w_in[0].rearrange("(k p) c -> p k c", p=P)
        wm_v = w_branch_m[0].rearrange("(k p) c -> p k c", p=P)
        wa_v = w_branch_a[0].rearrange("(k p) c -> p k c", p=P)
        wo_v = w_out[0].rearrange("(k p) c -> p k c", p=P)

        raw = [sb(f"w_raw{i}", [P, KT, P]) for i in range(2)]
        wsp = [sb(f"w_split{i}", [P, 2, KT, P], F32R) for i in range(2)]
        ident = sb("ident", [P, P])
        ones = sb("ones", [P, P])
        ones_r = sb("ones_r", [P, 2], F32R)
        bmerge = sb("bmerge", [P, 2 * KT])
        fbias = sb("f_bias", [P, 2])
        tile_sums = sb("tile_sums", [P, 2, ST])
        row_sums = sb("row_sums", [P, ST])
        tail_stat = sb("tail_stat", [P, ST])
        eps = sb("eps", [P, 1])
        qkf = sb("qk_f32", [P, 2, S])
        xn_scope = ExitStack()
        xs = sb("xn_split", [P, 2, KT, S], F32R, at=xn_scope)

        ma_scope = ExitStack()
        rev = sb("rev", [P, P], at=ma_scope)
        cos = sb("cos", [P, S], at=ma_scope)
        sin = sb("sin", [P, S], at=ma_scope)
        mask_r = sb("mask_r", [P, 2, P], F32R, at=ma_scope)
        ident_r = sb("ident_r", [P, P], F32R, at=ma_scope)
        col = sb("gate_cols", [P, 16, 5, MH], at=ma_scope)
        decay = sb("decay", [P, MH, 16], at=ma_scope)
        vecs = sb("vectors", [P, V_ROWS], at=ma_scope)
        again = sb("again", [P, 1], at=ma_scope)
        hcv = sb("head_conv", [P, 2, CONV + 1], at=ma_scope)
        neglam = sb("neglam", [P, 1], at=ma_scope)
        rawa = sb("raw_a", [P, S + CONV], at=ma_scope)
        rawb = sb("raw_b", [P, S], at=ma_scope)
        vz = sb("v_f32", [P, 2, S], at=ma_scope)

        conv_in = [rawa[:], vz[:].rearrange("p e s -> p (e s)")[:, S - CONV:2 * S]]

        p_scope = ExitStack()
        xin = [vz[:, 0], vz[:, 1], qkf[:, 0], qkf[:, 1]]
        gate_fill = sb("gate_fill", [P, 2, S], at=p_scope)
        conv_sum0 = sb("conv_sum0", [P, S], at=p_scope)
        pre_bc = sb("pre_bc", [P, D], at=p_scope)
        xstat = sb("xstat", [P, 2, ST], at=p_scope)
        wg = sb("wg", [P, KT, 16], at=p_scope)
        wgs = sb("wg_split", [P, 2, KT, P], F32R, at=p_scope)
        gbias = sb("gbias", [P, 1], at=p_scope)
        r_i = sb("row_i", [ROWS, S], at=p_scope)
        r_f = sb("row_f", [ROWS, S], at=p_scope)
        r_t = sb("row_t", [ROWS, S], at=p_scope)
        r_m = sb("row_m", [ROWS, S], at=p_scope)
        r_reset = sb("row_reset", [ROWS, S], at=p_scope)
        r_carry = sb("row_carry", [ROWS, S], at=p_scope)
        r_mp = sb("row_mp", [ROWS, NC], at=p_scope)
        r_dec = sb("row_decay", [ROWS, NC], at=p_scope)
        r_wk, r_winter = r_f, r_carry
        pick = sb("pick", [ROWS, 2, MH, P], at=p_scope)
        colrev = sb("col_reversed", [P, NC, 5, MH], at=p_scope)
        lamb = sb("lamb", [P, 4, AD], at=p_scope)
        lamt = sb("lamt", [P, 2, AD], at=p_scope)
        lams = sb("lams", [P, 4], at=p_scope)
        masks_f = sb("masks_f", [P, 2, P], at=p_scope)
        vrows = sb("vector_rows", [V_ROWS, P], at=p_scope)
        p_scope.close()

        m_scope = ExitStack()
        qT = sb("q_split", [P, 2, S], F32R, at=m_scope)
        kT = sb("k_split", [P, 2, S], F32R, at=m_scope)
        kseq = sb("k_seq", [P, NC, P], at=m_scope)
        vS = sb("v_split", [P, 2, NC, MV + 2], F32R, at=m_scope)
        ab = sb("sigmoid_work", [P, 2, S], at=m_scope)
        zg = sb("gate_z", [P, 2, S], at=m_scope)
        hacc = sb("h_sum", [P, NC, MV], at=m_scope)
        wt = sb("w_exp", [P, 2, P], at=m_scope)
        ptf = sb("pt_f32", [P, 2, P], at=m_scope)
        pt = sb("pt_split", [P, 2, 2, P], F32R, at=m_scope)
        kw = sb("kw_split", [P, 2, 2, P], F32R, at=m_scope)
        num = sb("num", [P, 2, MV + 2], at=m_scope)
        cf = sb("state_f32", [P, 2, MV + 2], at=m_scope)
        cs = sb("state_split", [P, 2, 2, MV + 2], F32R, at=m_scope)
        dg = sb("diag", [P, 2, P], at=m_scope)
        dsm = sb("den", [P, 3, 2], at=m_scope)
        hc = sb("head_cols", [P, 16, 5], at=m_scope)
        hd = sb("head_decay", [P, 16], at=m_scope)
        hg = sb("head_gain", [P, 2], at=m_scope)
        hstat = sb("h_stat", [P, 2, NC], at=m_scope)
        hst = sb("hT_f32", [P, HALF], at=m_scope)
        hsp0 = sb("hT_split", [P, 2, HALF], F32R, at=m_scope)
        hsp = [hsp0[:], ab[:, 1].rearrange("p (i s) -> p i s", i=2).bitcast(F32R)]
        m_scope.close()

        a_scope = ExitStack()
        qs = sb("q_stack", [P, 2, S], F32R, at=a_scope)
        ks = sb("k_stack", [P, 2, 2, S], F32R, at=a_scope)
        va = sb("va_split", [P, 2, ST, AV], F32R, at=a_scope)
        at_s = sb("aT_split", [P, 2, KT, 2 * P], F32R, at=a_scope)
        pr = sb("probs", [P, 2, S], at=a_scope)
        am = [sb(f"mix{i}", [P, S], at=a_scope) for i in range(2)]
        ga = sb("gate_a", [P, S], at=a_scope)
        aw = sb("sigmoid_work_a", [P, S], at=a_scope)
        nmax = sb("negmax", [P, 2, 2], at=a_scope)
        den = sb("den_a", [P, 2, 2], at=a_scope)
        rden = sb("rden", [P, 3, 2], at=a_scope)
        of = sb("o_f32", [P, 2 * P], at=a_scope)
        osq = sb("o_sq", [P, 2 * P], at=a_scope)
        ors = sb("o_rs", [P, 2 * P], at=a_scope)
        ost = sb("o_out", [P, 2 * P], at=a_scope)
        osp = sb("o_split", [P, 2, 2 * P], F32R, at=a_scope)
        a_scope.close()
        ma_scope.close()

        f_scope = ExitStack()
        hT = sb("h_split", [P, 2, KT, S], F32R, at=f_scope)
        ya = sb("y_f32", [P, KT, S], at=f_scope)
        fw = sb("f_work", [P, S], at=f_scope)
        fb = sb("f_branch", [P, S], at=f_scope)
        f_scope.close()
        xn_scope.close()
        o_scope = ExitStack()
        xres = sb("x_residual", [P, ST, D], at=o_scope)
        o_scope.close()
        ys, orow = hT, ya
        outT = [qkf[:, 0], qkf[:, 1]]
        post_bc, junk_row = fw, fb

        ps = ctx.enter_context(nc.psum_tensor("ps", [P, 8, HALF], F32))

        x_loaded = [sem(f"x_loaded{i}") for i in range(4)]
        first_loaded = sem("first_loaded")
        small_loaded = sem("small_loaded")
        rope_loaded = sem("rope_loaded")
        raw_loaded = [sem(f"raw_loaded{i}") for i in range(2)]
        spilled_m = [sem(f"spilled_m{i}") for i in range(2)]
        spilled_a = sem("spilled_a")
        h_loaded = [sem("h_m_loaded"), sem("h_a_loaded")]
        g_spilled = [sem(f"g_spilled{i}") for i in range(2)]
        g_loaded = [sem(f"g_loaded{i}") for i in range(2)]
        res_loaded = sem("res_loaded")
        stored = sem("stored")
        step_begun = sem("step_begun")
        w_split = sem("w_split")
        proj_done = sem("proj_done")
        proj_read = sem("proj_read")
        consts_set = sem("consts_set")
        x_stat = sem("x_stat")
        x_scaled = sem("x_scaled")
        x_tr = sem("x_transposed")
        x_hi = sem("x_hi")
        x_lo = sem("x_lo")
        prep_pe = sem("prep_pe")
        prep_dve = sem("prep_dve")
        prep_act = sem("prep_act")
        pads_set = sem("pads_set")
        hcols = signal("hcols", 4)
        score_done = signal("score_done", 8)
        diag_done = signal("diag_done", 8)
        w_done = signal("w_done", 8)
        ptf_done = signal("ptf_done", 8)
        pthi_done = signal("pthi_done", 8)
        ptlo_done = signal("ptlo_done", 8)
        kwhi_done = signal("kwhi_done", 7)
        kwlo_done = signal("kwlo_done", 7)
        inter_done = signal("inter_done", 7)
        intra_done = signal("intra_done", 8)
        upd_done = signal("upd_done", 7)
        intersc_done = signal("intersc_done", 7)
        num_done = signal("num_done", 8)
        den_chain = signal("den_chain", 24)
        h_done = signal("h_done", 8)
        state_done = signal("state_done", 7)
        chi_done = signal("chi_done", 7)
        clo_done = signal("clo_done", 7)
        gate_dve = signal("gate_dve", 12)
        gate_act = signal("gate_act", 10)
        conv_dve = signal("conv_dve", 14)
        conv_act = signal("conv_act", 6)
        qk_hi = signal("qk_hi", 2)
        qk_lo = signal("qk_lo", 2)
        tr_done = signal("tr_done", 10, 6)
        tr_read = signal("tr_read", 10, 6)
        tr_hi = signal("tr_hi", 4)
        hsp_hi = signal("hsp_hi", 4)
        hsplit_done = signal("hsplit_done", 4)
        hs_act = signal("hs_act", 3)
        hs_done = signal("hs_done", 1)

        shuf_done = sem("shuf_done")
        rope_done = sem("rope_done")
        rope_k0 = sem("rope_k0")

        a_qk_hi = signal("a_qk_hi", 4)
        k_doubled = sem("k_doubled")
        a_qk_lo = signal("a_qk_lo", 4)
        a_score = signal("a_score", 16)
        a_max = signal("a_max", 16)
        a_exp = signal("a_exp", 16)
        a_mix = signal("a_mix", 32)
        a_tr = signal("a_tr", 18)
        a_tr_hi = signal("a_tr_hi", 18)
        a_tr_read = signal("a_tr_read", 18)
        a_pv = signal("a_pv", 4)
        a_of = signal("a_of", 4)
        a_osq = signal("a_osq", 4)
        a_ss = signal("a_ss", 4)
        a_rs = signal("a_rs", 8)
        a_ost = signal("a_ost", 8)
        a_ohi = signal("a_ohi", 4)
        a_olo = signal("a_olo", 4)
        a_gate_dve = signal("a_gate_dve", 3)
        a_gate_act = signal("a_gate_act", 3)

        bias_set = sem("bias_set")
        f_abs = sem("f_abs")
        f_logsig = sem("f_logsig")
        f_act = sem("f_act")
        f_product = sem("f_product")
        f_y = sem("f_y")
        y_hi = sem("y_hi")
        y_lo = sem("y_lo")
        post_loaded = sem("post_loaded")
        o_tr = sem("o_tr")
        o_squares = sem("o_squares")
        o_sums = sem("o_sums")
        o_rows = sem("o_rows")
        o_stat = sem("o_stat")
        o_out = sem("o_out")

        block = ctx.enter_context(nc.Block())

        def tile_no(base, per_head, h, j):
            return per_head * h + (base + j), (base + j) % 2

        @block.sync
        def _(sp):
            def load_weights(base, per_head, h, j, src, col0):
                assert per_head % 2 == 0
                g, b = tile_no(base, per_head, h, j)
                if not (isinstance(g, int) and g < 2):
                    sp.wait_ge(w_split, 2 * g - 2)
                    if not isinstance(g, int):
                        sp.sem_inc(step_begun, 1)
                sp.dma_start(raw[b][:], src[:, :, bass.ds(col0, P)]).then_inc(raw_loaded[b], 16)

            for t in range(4):
                sp.dma_start(xin[t], x_v[t]).then_inc(x_loaded[t], 16)
                if t == 0:
                    sp.dma_start(ident[:], consts[:, K_ID:K_ID + P]).then_inc(first_loaded, 16)
                    sp.dma_start(pre_bc[:], pre_norm_g[0].partition_broadcast(P)).then_inc(first_loaded, 16)
            small = [
                (wg[:], w_in_v[:, :, C_MG:C_MG + 16]),
                (vrows[V_CW:V_CB, :], conv_w[0].rearrange("w (j p) -> (w j) p", p=P)),
                (vrows[V_CB:V_MG, :], conv_b[0].rearrange("(j p) -> j p", p=P)),
                (vrows[V_MG:V_BM, :], m_norm_g[0].rearrange("(j p) -> j p", p=P)),
                (vrows[V_BM:V_AG, :], b_merge[0].rearrange("(j p) -> j p", p=P)),
                (vrows[V_AG:V_ROWS, :], a_norm_g),
                *((gbias[64 * kind + 32 * r:64 * kind + 32 * r + MH, :],
                   gate_b[0, 2 * r + kind:2 * r + kind + 1, :].rearrange("g h -> h g"))
                  for r in range(2) for kind in range(2)),
                (rev[:], consts[:, K_REV:K_REV + P]),
                (masks_f[:], consts[:, K_MASK:K_MASK + 2 * P].rearrange("p (r j) -> p r j", r=2)),
                (lamb[:], lambda_qk[0].partition_broadcast(P)),
            ]
            for dst, src in small:
                sp.dma_start(dst, src, allow_slow_non_contiguous=True).then_inc(small_loaded, 16)
            assert len(small) == N_SMALL
            for j in range(2):
                load_weights(0, 0, 0, j, w_in_v, C_MQK + j * MH * MQK)
            for t in range(4, ST):
                sp.wait_ge(x_tr, 2 * (t - 4) + 2)
                sp.dma_start(xin[t % 4], x_v[t]).then_inc(x_loaded[t % 4], 16)
            for i in range(4):
                load_weights(0, 0, 0, 2 + i, w_in_v, C_GM + i * P)
            for e in range(2):
                load_weights(0, 0, 0, 6 + e, w_in_v, C_MV + e * P)
            sp.dma_start(cos[:], consts[:, K_COS:K_COS + S]).then_inc(rope_loaded, 16)
            sp.dma_start(sin[:], consts[:, K_SIN:K_SIN + S]).then_inc(rope_loaded, 16)

            def m_head(h, last):
                for e in range(2):
                    load_weights(G_M, 8, h, 2 * e, w_in_v, C_MO + e * P + h * MV)
                    load_weights(G_M, 8, h, 2 * e + 1, w_in_v, C_MZ + e * P + h * MV)
                if not last:
                    load_weights(G_M, 8, h, 4, w_in_v, C_MQK + MQK + h * MQK)
                    load_weights(G_M, 8, h, 5, w_in_v, C_MQK + (MH + 1) * MQK + h * MQK)
                    load_weights(G_M, 8, h, 6, w_in_v, C_MV + MV + h * MV)
                    load_weights(G_M, 8, h, 7, w_in_v, C_MV + MV + P + h * MV)
                else:
                    for j, c in enumerate((C_AQ, C_AK, C_AV, C_AZ)):
                        load_weights(G_M, 8, h, 4 + j, w_in_v, c)

            with sp.Fori(0, MH - 1) as h:
                m_head(h, False)
            m_head(MH - 1, True)

            def store_a(h, n):
                sp.wait_ge(a_olo.sem, a_olo.after(h, n))
                sp.dma_start(spill_a[:, bass.ds(h, 1), :, 2 * n * P:2 * (n + 1) * P].rearrange(
                    "i one p s -> p i (one s)"), osp[:].bitcast(F32)).then_inc(spilled_a, 16)

            def double_keys(hh):
                own = (slice(0, AD), slice(AD, P))
                for c in range(2):
                    sp.wait_ge(a_qk_lo.sem, a_qk_lo.after(hh, c))
                    sp.dma_start(ks[own[1 - c], c].bitcast(F32), ks[own[c], c].bitcast(F32)).then_inc(k_doubled, 16)

            def a_tiles(h, first):
                for j, c in enumerate((C_AQ, C_AK, C_AV, C_AZ)):
                    load_weights(G_A, 4, h, j, w_in_v, c + P + h * P)
                    if j == (1 if first else 2):
                        double_keys(h)
                    if not first:
                        store_a(h - 1, j)

            a_tiles(0, True)
            with sp.Fori(1, AH - 1) as h:
                a_tiles(h, False)

            for i in range(4):
                load_weights(G_GL, 0, 0, i, w_in_v, C_GM + (4 + i) * P)
                if i == 2:
                    double_keys(AH - 1)
                store_a(AH - 2, i)
            for j in range(2):
                load_weights(G_G, 0, 0, j, w_in_v, C_GM + (8 + j) * P)
                store_a(AH - 1, j)
            for j in range(2, 4):
                store_a(AH - 1, j)
            for i in range(2):
                sp.wait_ge(spilled_m[i], 16 + 16 * 2 * MH)
            sp.wait_ge(spilled_a, 16 + 16 * 4 * AH)

            def load_h(n, k):
                dst, spill = ((hT, spill_m), (xs, spill_a))[n]
                sp.dma_start(dst[:, :, bass.ds(k, 1)].rearrange("p i one s -> p i (one s)").bitcast(F32),
                             spill[:, bass.ds(k, 1)].rearrange("i one p s -> p i (one s)")).then_inc(h_loaded[n], 16)

            for j in range(2):
                load_h(0, j)
            with sp.Fori(1, 4) as c:
                for j in range(2):
                    load_weights(G_G, 2, c, j, w_in_v, C_GM + (8 + j) * P + 2 * P * c)
                    load_h(0, 2 * c + j)

            def load_gate(i, par):
                sp.dma_start(qkf[:, par], spill_g[bass.ds(i, 1)].rearrange("one p s -> (one p) s")) \
                    .then_inc(g_loaded[par], 16)

            def branch(n, base, weights, first):
                with sp.Fori(first, KT // 2) as c:
                    for j in range(2):
                        load_weights(base, 2, c, j, weights, 2 * P * c + j * P)
                        sp.wait_ge(f_logsig, KT * n + 2 * c + (j - 1))
                        load_gate(KT * n + 2 * c + j, j)
                        if n == 0:
                            load_h(1, 2 * c + j)

            for j in range(2):
                load_weights(G_FA, 0, 0, j, wm_v, j * P)
                sp.wait_ge(g_spilled[j], 16 * KT)
                load_gate(j, j)
            sp.wait_ge(proj_done, 2 * G_FA)
            for j in range(2):
                load_h(1, j)
            branch(0, G_FA, wm_v, 1)
            branch(1, G_FB, wa_v, 0)
            for j in range(2):
                load_weights(G_O, 0, 0, j, wo_v, j * P)
            sp.wait_ge(proj_done, 2 * G_O)

            def load_residual(t):
                sp.dma_start(xres[:, bass.ds(t, 1)].rearrange("p one d -> p (one d)"),
                             x_v[bass.ds(t, 1)].rearrange("one p d -> (one p) d")).then_inc(res_loaded, 16)

            for j in range(2):
                load_residual(j)
            sp.wait_ge(f_y, KT)
            sp.dma_start(post_bc[:], post_norm_g[0].partition_broadcast(P)).then_inc(post_loaded, 16)
            with sp.Fori(1, KT // 2) as c:
                for j in range(2):
                    load_weights(G_O, 2, c, j, wo_v, c * 2 * P + j * P)
                    load_residual(2 * c + j)
            for t in range(ST):
                sp.wait_ge(o_out, t + 1)
                sp.dma_start(out_v[t], orow[:, t]).then_inc(stored, 16)
            sp.wait_ge(stored, 16 * ST)

        @block.gpsimd
        def _(pool):
            def split_weights(base, per_head, h, j):
                g, b = tile_no(base, per_head, h, j)
                pool.wait_ge(raw_loaded[b], 16 * ((per_head // 2) * h + ((base + j) // 2 + 1)))
                if not (isinstance(g, int) and g < 2):
                    pool.wait_ge(proj_done, 2 * g - 2)
                pool.tensor_tensor(wsp[b][:, 0], raw[b][:], ones[:, 0:1].unsqueeze(2).to_broadcast([P, KT, P]),
                                   ALU.mult).then_inc(w_split, 1)
                pool.wait_ge(w_split, 2 * g + 1)
                pool.tensor_tensor(wsp[b][:, 1], raw[b][:], wsp[b][:, 0].bitcast(F32),
                                   ALU.subtract).then_inc(w_split, 1)

            def rope(hh, n):
                for half in range(2):
                    cols = slice(half * HALF, (half + 1) * HALF)
                    turn = 4 * hh + (n + half)
                    pool.wait_ge(shuf_done, turn + 1)
                    own, other = qkf[:, n // 2, cols], (rawa, rawb)[n // 2][:, cols]
                    pool.tensor_tensor(own, own, cos[:, cols], ALU.mult).then_inc(rope_done, 1)
                    pool.tensor_tensor(other, other, sin[:, cols], ALU.mult).then_inc(rope_done, 1)
                    pool.wait_ge(rope_done, 3 * turn + 2)
                    pool.tensor_tensor(own, own, other, ALU.add).then_inc(rope_done, 1)

            def with_rope(base, per_head, h, j, hh):
                split_weights(base, per_head, h, j)
                split_weights(base, per_head, h, j + 1)
                split_weights(base, per_head, h, j + 2)
                rope(hh, 0)
                split_weights(base, per_head, h, j + 3)
                rope(hh, 2)

            pool.wait_ge(consts_set, 2)
            for j in range(G_M):
                split_weights(0, 0, 0, j)
            pool.wait_ge(rope_loaded, 16 * 2)
            with pool.Fori(0, MH - 1) as h:
                for j in range(8):
                    split_weights(G_M, 8, h, j)
            for j in range(4):
                split_weights(G_M, 8, MH - 1, j)
            for j in range(4, 8):
                split_weights(G_M, 8, MH - 1, j)
            rope(0, 0)
            pool.wait_ge(rope_done, 3 * 1 + 3)
            pool.sem_inc(rope_done, 6)
            with pool.Fori(0, AH - 1) as h:
                with_rope(G_A, 4, h, 0, h + 1)
            with pool.Fori(0, (G_END - G_GL) // 2) as c:
                for j in range(2):
                    split_weights(G_GL, 2, c, j)

        @block.tensor
        def _(pe):
            def proj_half(base, per_head, h, j, half, moving=xs, amid=None, amid_at=KT // 2, begin=0, end=KT):
                g, b = tile_no(base, per_head, h, j)
                if half == 0 and begin == 0:
                    pe.wait_ge(w_split, 2 * g + 2)
                if begin == 0 and not is_zero(g):
                    pe.wait_ge(proj_read, 2 * g + half - 1)
                cols = slice(half * HALF, (half + 1) * HALF)
                for k in range(begin, end):
                    if amid is not None and k == amid_at:
                        amid()
                    for n, (wl, xl) in enumerate(PASSES):
                        mm = pe.matmul(ps[:, half, :], wsp[b][:, wl, k, :], moving[:, xl, k, cols],
                                       start=(k == 0 and n == 0), stop=(k == KT - 1 and n == 2))
                if end == KT:
                    mm.then_inc(proj_done, 1)

            def product(dst, st, mv, start=True, stop=True):
                for n, (a, b) in enumerate(PASSES):
                    mm = pe.matmul(dst, st(a), mv(b), start=(start and n == 0), stop=(stop and n == 2))
                return mm

            def product_exact(dst, st, mv_one):
                for a in range(2):
                    mm = pe.matmul(dst, st(a), mv_one, start=(a == 0), stop=(a == 1))
                return mm

            pe.wait_ge(first_loaded, 16 * 2)
            for t in range(ST):
                pe.wait_ge(x_scaled, t + 1)
                if t >= 2:
                    pe.wait_ge(x_lo, 2 * (t - 2) + 2)
                for i in range(2):
                    bank = 2 + 2 * (t % 2) + i
                    for q in range(4):
                        mm = pe.transpose(ps[:, bank, q * P:(q + 1) * P],
                                          xin[t % 4][:, (4 * i + q) * P:(4 * i + q + 1) * P], ident[:])
                    mm.then_inc(x_tr, 1)
            pe.wait_ge(small_loaded, 16 * N_SMALL)
            pe.transpose(ps[:, 6, 0:V_ROWS], vrows[:], ident[0:V_ROWS, 0:V_ROWS]).then_inc(prep_pe, 1)
            pe.wait_ge(x_lo, 2 * ST)
            pe.wait_ge(prep_dve, prep_dve_at("vecs"))
            for half in range(2):
                for k in range(KT):
                    for n, (wl, xl) in enumerate(PASSES):
                        mm = pe.matmul(ps[:, 6 + half, :], wgs[:, wl, k, :],
                                       xs[:, xl, k, half * HALF:(half + 1) * HALF],
                                       start=(k == 0 and n == 0), stop=(k == KT - 1 and n == 2))
            mm.then_inc(prep_pe, 1)
            for j in range(6):
                proj_half(0, 0, 0, j, 0)
                proj_half(0, 0, 0, j, 1)
            pe.wait_ge(prep_act, prep_act_at("decay"))
            for m in range(MH):
                for r in range(2):
                    at = 256 + 2 * NC * m + NC * r
                    mm = pe.matmul(ps[:, 7, at:at + NC], pick[:, r, m, :], r_dec[:], start=True, stop=True)
            mm.then_inc(prep_pe, 1)
            pe.wait_ge(prep_act, prep_act_at("w_k"))
            for q, row in enumerate((r_m, r_i, r_winter, r_t, r_wk)):
                for c in range(NC):
                    mm = pe.transpose(ps[:, 2 + q, c * ROWS:(c + 1) * ROWS], row[:, c * P:(c + 1) * P],
                                      ident[0:ROWS, 0:ROWS])
            mm.then_inc(prep_pe, 1)
            for half in range(2):
                proj_half(0, 0, 0, 6, half)
            pe.wait_ge(prep_dve, prep_dve_at("decay_all"))
            pe.matmul(ps[:, 7, 0:NC * 5 * MH], rev[:], colrev[:].rearrange("p c q m -> p (c q m)"),
                      start=True, stop=True).then_inc(prep_pe, 1)

            def tr_round(h, k, srcs, first=False):
                bank = (7, 2)[k % 2]
                if not first:
                    pe.wait_ge(tr_read.sem, tr_read.after(h, k) - 2)
                for q, src in enumerate(srcs):
                    mm = pe.transpose(ps[:, bank, q * P:(q + 1) * P], src, ident[:])
                mm.then_inc(tr_done.sem, 1)

            def k_rounds(h):
                pe.wait_ge(conv_dve.sem, conv_dve.after(h + 1, 13))
                for i in range(2):
                    tr_round(h, 6 + i, [qkf[:, 1, c * P:(c + 1) * P] for c in range(4 * i, 4 * i + 4)])

            def v_rounds(h, e, first=False):
                g, _ = tile_no(G_M, 8, h, 6 + e)
                pe.wait_ge(proj_read, 2 * g + 2)
                for i in range(2):
                    tr_round(h, 4 + 4 * e + i, [vz[:, e, c * P:(c + 1) * P] for c in range(4 * i, 4 * i + 4)], first)

            def chunk(r, t):
                return t if r == 0 else NC - 1 - t

            def m_scores(h, t):
                if t == 0:
                    pe.wait_ge(qk_lo.sem, qk_lo.after(h, 1))
                    pe.wait_ge(tr_read.sem, tr_read.after(h - 1, 9))
                for r in range(2):
                    c = chunk(r, t)
                    sl = slice(c * P, (c + 1) * P)
                    product(ps[:, 2, r * P:(r + 1) * P], lambda a: kT[:, a, sl], lambda b: qT[:, b, sl])
                pe.wait_ge(diag_done.sem, diag_done.after(h, t))
                pe.matmul(ps[:, 2, 2 * P:4 * P], ident_r[:], mask_r[:].rearrange("p r j -> p (r j)"),
                          start=True, stop=False)
                pe.matmul(ps[:, 2, 2 * P:4 * P], ones[:], dg[:].rearrange("p r j -> p (r j)"),
                          start=False, stop=True).then_inc(score_done.sem, 1)

            def m_products(h, t):
                if t > 0:
                    pe.wait_ge(clo_done.sem, clo_done.after(h, t - 1))
                    pe.wait_ge(num_done.sem, num_done.after(h, t - 1))
                    for r in range(2):
                        c = chunk(r, t)
                        sl = slice(c * P, (c + 1) * P)
                        mm = product(ps[:, (5, 3)[r], 0:MV + 2], lambda a: qT[:, a, sl], lambda b: cs[:, b, r, :])
                    mm.then_inc(inter_done.sem, 1)
                pe.wait_ge(ptlo_done.sem, ptlo_done.after(h, t))
                for r in range(2):
                    c = chunk(r, t)
                    mm = product(ps[:, (4, 7)[r], 0:MV + 2], lambda a: pt[:, a, r, :], lambda b: vS[:, b, c, :])
                mm.then_inc(intra_done.sem, 1)
                if t < NC - 1:
                    pe.wait_ge(kwlo_done.sem, kwlo_done.after(h, t))
                    if t > 0:
                        pe.wait_ge(state_done.sem, state_done.after(h, t - 1))
                    for r in range(2):
                        c = chunk(r, t)
                        product(ps[:, 6, r * MV:(r + 1) * MV], lambda a: kw[:, a, r, :], lambda b: vS[:, b, c, 0:MV])
                        at = MV + 4 + 2 * r
                        mm = product_exact(ps[:, 7, at:at + 2], lambda a: kw[:, a, r, :], ones_r[:])
                    mm.then_inc(upd_done.sem, 1)

            def h_rounds(h, e):
                for i in range(2):
                    tr_round(h, 2 * e + i, [hacc[:, c, e * P:(e + 1) * P] for c in range(4 * i, 4 * i + 4)],
                             first=(e == 0))

            def m_head(h, last):
                proj_half(G_M, 8, h, 0, 0, amid=lambda: v_rounds(h - 1, 1))
                m_scores(h, 0)
                for t in range(NC):
                    proj_half(G_M, 8, h, (t + 1) // 2, (t + 1) % 2)
                    m_products(h, t)
                    if t < NC - 1:
                        m_scores(h, t + 1)
                proj_half(G_M, 8, h, 4, 1)
                proj_half(G_M, 8, h, 5, 0)
                pe.wait_ge(num_done.sem, num_done.after(h, NC - 1))
                pe.wait_ge(hs_done.sem, hs_done.after(h))
                h_rounds(h, 0)
                proj_half(G_M, 8, h, 5, 1)
                h_rounds(h, 1)
                for half in range(2):
                    proj_half(G_M, 8, h, 6, half)
                proj_half(G_M, 8, h, 7, 0, amid=None if last else lambda: v_rounds(h, 0), amid_at=5)
                proj_half(G_M, 8, h, 7, 1, amid=None if last else lambda: k_rounds(h), amid_at=7)

            pe.wait_ge(prep_dve, prep_dve_at("col_bw"))
            proj_half(0, 0, 0, 7, 0, amid=lambda: v_rounds(-1, 0, first=True))
            proj_half(0, 0, 0, 7, 1, amid=lambda: k_rounds(-1))
            with pe.Fori(0, MH - 1) as h:
                m_head(h, False)
            m_head(MH - 1, True)

            def a_scores(h, q):
                if q == 0:
                    pe.wait_ge(k_doubled, 32 * h + 32)
                    pe.wait_ge(a_qk_lo.sem, a_qk_lo.after(h, 3))
                for c in range(2):
                    if q > 0:
                        pe.wait_ge(a_exp.sem, a_exp.after(h, 2 * (q - 1) + c))
                    elif not is_zero(h):
                        pe.wait_ge(a_exp.sem, a_exp.after(h, c) - 2)
                    for i in range(2):
                        for b in range(2):
                            mm = pe.matmul(ps[:, 2 + 2 * c + i, :], qs[:, c, q * P:(q + 1) * P],
                                           ks[:, c, b, i * HALF:(i + 1) * HALF], start=(b == 0), stop=(b == 1))
                    mm.then_inc(a_score.sem, 1)

            def a_round(h, k, srcs, first=False):
                if not first:
                    pe.wait_ge(a_tr_read.sem, a_tr_read.after(h, k) - 1)
                for n, src in enumerate(srcs):
                    mm = pe.transpose(ps[:, 6, n * P:(n + 1) * P], src, ident[:])
                mm.then_inc(a_tr.sem, 1)

            def mix_round(h, q, i):
                if i == 0:
                    pe.wait_ge(a_mix.sem, a_mix.after(h, 4 * q + 3))
                a_round(h, round_of(q, i), [am[q % 2][:, k * P:(k + 1) * P] for k in range(4 * i, 4 * i + 4)])

            def pv(h, n):
                pe.wait_ge(a_tr_read.sem, a_tr_read.after(h, round_of(2 * n + 1, 1)))
                if n > 0:
                    pe.wait_ge(a_rs.sem, a_rs.after(h, 2 * (n - 1)))
                elif not is_zero(h):
                    pe.wait_ge(a_rs.sem, a_rs.after(h, 0) - 2)
                for k in range(KT):
                    mm = product(ps[:, 7, 0:2 * P], lambda a: va[:, a, k, :], lambda b: at_s[:, b, k, :],
                                 start=(k == 0), stop=(k == KT - 1))
                mm.then_inc(a_pv.sem, 1)

            def squares(h, n):
                pe.wait_ge(a_osq.sem, a_osq.after(h, n))
                pe.matmul(ps[:, 7, 2 * P:4 * P], ones[:], osq[:], start=True, stop=True).then_inc(a_ss.sem, 1)

            def a_head(h, first, last):
                def filler(n, amid=None, begin=0, end=KT):
                    if not last:
                        proj_half(G_A, 4, h, n // 2, n % 2, amid=amid, begin=begin, end=end)
                    else:
                        proj_half(G_GL, 0, 0, n // 2, n % 2, amid=amid, begin=begin, end=end)

                def v_round(i):
                    a_round(h, V_ROUND[i], [vz[:, 0, c * P:(c + 1) * P] for c in range(4 * i, 4 * i + 4)],
                            first=(first and i == 0))

                a_scores(h, 0)
                if first:
                    pe.wait_ge(proj_read, 2 * (G_M + 8 * (MH - 1) + 7) + 2)
                v_round(0)
                filler(0)
                if not first:
                    squares(h - 1, 3)
                for q in range(ST):
                    mix_round(h, q, 0)
                    if q + 1 < ST:
                        a_scores(h, q + 1)
                    else:
                        filler(7, begin=4, end=6)
                    mix_round(h, q, 1)
                    if q % 2 == 0 and q > 0:
                        squares(h, q // 2 - 1)
                    if q < 5:
                        filler(q + 1, amid=(lambda: v_round(1)) if q == 0 else None)
                    elif q == 5:
                        filler(6, end=4)
                    elif q == 6:
                        filler(6, begin=4)
                        filler(7, end=4)
                    else:
                        filler(7, begin=6)
                    if q % 2 == 1:
                        pv(h, q // 2)

            a_head(0, True, False)
            with pe.Fori(1, AH - 1) as h:
                a_head(h, False, False)
            a_head(AH - 1, False, True)
            squares(AH - 1, 3)

            with pe.Fori(0, 4) as c:
                for j in range(2):
                    proj_half(G_G, 2, c, j, 0)
                    proj_half(G_G, 2, c, j, 1)
            for n, (base, h) in enumerate(((G_FA, hT), (G_FB, xs))):
                pe.wait_ge(h_loaded[n], 16 * KT)
                with pe.Fori(0, KT // 2) as c:
                    for j in range(2):
                        proj_half(base, 2, c, j, 0, moving=h)
                        proj_half(base, 2, c, j, 1, moving=h)

            def out_rows(c, par):
                for i in range(2):
                    pe.wait_ge(proj_read, 2 * (G_O + c) + i + 1)
                    if not is_zero(c):
                        pe.wait_ge(o_squares, 2 * c + i - 1)
                    for q in range(4):
                        t = 4 * i + q
                        mm = pe.transpose(ps[:, 2 + 2 * par + i, q * P:(q + 1) * P],
                                          outT[par][:, t * P:(t + 1) * P], ident[:])
                    mm.then_inc(o_tr, 1)

            pe.wait_ge(y_lo, KT - 1)
            for half in range(2):
                proj_half(G_O, 0, 0, 0, half, moving=ys, end=KT - 1)
            pe.wait_ge(y_lo, KT)
            for half in range(2):
                proj_half(G_O, 0, 0, 0, half, moving=ys, begin=KT - 1)
            for half in range(2):
                proj_half(G_O, 0, 0, 1, half, moving=ys)
            out_rows(0, 0)
            with pe.Fori(1, KT // 2) as c2:
                for par in range(2):
                    proj_half(G_O, 2, c2, par, 0, moving=ys)
                    proj_half(G_O, 2, c2, par, 1, moving=ys)
                    out_rows(2 * c2 + (par - 1), 1 - par)
            out_rows(KT - 1, 1)

        @block.vector
        def _(dve):
            def mark(ins, name):
                assert name in PREP_DVE
                ins.then_inc(prep_dve, 1)

            def after_step(name):
                dve.wait_ge(prep_dve, prep_dve_at(name))

            dve.memset(eps[:], EPS).then_inc(consts_set, 1)
            dve.memset(ones[:], 1.0).then_inc(consts_set, 1)
            dve.memset(rawa[:], 0.0).then_inc(consts_set, 1)
            dve.memset(r_reset[:], 1.0).then_inc(consts_set, 1)
            dve.memset(r_carry[:], 0.0).then_inc(consts_set, 1)
            dve.memset(r_mp[:], 0.0).then_inc(consts_set, 1)
            dve.memset(r_i[:], 0.0).then_inc(consts_set, 1)
            dve.memset(r_f[:], 0.0).then_inc(consts_set, 1)
            dve.wait_ge(consts_set, 4)
            dve.tensor_copy(ones_r[:], ones[:, 0:2]).then_inc(consts_set, 1)
            starts = r_reset[:].rearrange("m (c j) -> m c j", j=P)[:, :, 0]
            dve.memset(starts, 0.0).then_inc(consts_set, 1)

            def x_low(t):
                for i in range(2):
                    dve.wait_ge(x_hi, 2 * t + i + 1)
                    dst = slice(4 * i, 4 * i + 4), slice(t * P, (t + 1) * P)
                    dve.tensor_tensor(xs[:, 1, dst[0], dst[1]],
                                      ps[:, 2 + 2 * (t % 2) + i, :].rearrange("p (k s) -> p k s", k=4),
                                      xs[:, 0, dst[0], dst[1]].bitcast(F32), ALU.subtract).then_inc(x_lo, 1)

            dve.wait_ge(first_loaded, 16 * 2)
            for t in range(ST):
                dve.wait_ge(x_stat, 3 * t + 3)
                dve.scalar_tensor_tensor(xin[t % 4], xin[t % 4], xstat[:, 1, t:t + 1], pre_bc[:],
                                         ALU.mult, ALU.mult).then_inc(x_scaled, 1)
                if t > 0:
                    x_low(t - 1)
            dve.wait_ge(small_loaded, 16 * N_SMALL)
            mark(dve.tensor_scalar(wgs[:].rearrange("p i k c -> p (i k c)"),
                                   ones[:, 0:1].to_broadcast([P, 2 * KT * P]), 0.0, None, ALU.mult), "wg_zero")

            def wg_cols(part):
                return wgs[:, part].rearrange("p k (kind r x) -> p k r kind x", kind=2, r=2)[:, :, :, :, 0:MH]

            wg_v = wg[:].rearrange("p k (r kind m) -> p k r kind m", r=2, kind=2)
            after_step("wg_zero")
            for r in range(2):
                for kind in range(2):
                    w = dve.tensor_copy(wg_cols(0)[:, :, r, kind], wg_v[:, :, r, kind])
            mark(w, "wg_hi")
            x_low(ST - 1)
            after_step("wg_hi")
            for r in range(2):
                for kind in range(2):
                    w = dve.tensor_tensor(wg_cols(1)[:, :, r, kind], wg_v[:, :, r, kind],
                                          wg_cols(0)[:, :, r, kind].bitcast(F32), ALU.subtract)
            mark(w, "wg_lo")
            mark(dve.tensor_copy(ident_r[:], ident[:]), "ident_r")
            mark(dve.tensor_copy(mask_r[:], masks_f[:]), "mask_r")
            dve.wait_ge(prep_pe, 1)
            mark(dve.tensor_copy(vecs[:], ps[:, 6, 0:V_ROWS]), "vecs")
            after_step("vecs")
            conv_cols = vecs[:, V_CW:V_MG].rearrange("p (w q m) -> p q w m", q=2, m=MH)
            mark(dve.tensor_copy(hcv[:], conv_cols[:, :, :, 0]), "conv0")
            mark(dve.tensor_scalar(again[:], vecs[:, V_AG:V_AG + 1], 1.0 - LAM_INIT, None, ALU.mult), "again")
            mark(dve.tensor_copy(bmerge[:], vecs[:, V_BM:V_AG]), "bmerge")
            mark(dve.tensor_copy(pick[:], ident[0:ROWS, 0:64].rearrange("p (r x) -> p r x", r=2)[:, :, 0:MH].unsqueeze(3)
                                 .to_broadcast([ROWS, 2, MH, P])), "pick")
            lam2 = lamb[:].rearrange("p (j two) d -> p j two d", two=2)
            mark(dve.tensor_tensor(lamt[:], lam2[:, :, 0], lam2[:, :, 1], ALU.mult), "lam_products")
            after_step("lam_products")
            mark(dve.tensor_reduce(lams[:, 0:2], lamt[:], AX_X, ALU.add), "lam_sums")
            dve.wait_ge(prep_pe, 2)

            def gate_rows(dst, kind, names):
                for r in range(2):
                    at = slice(64 * kind + 32 * r, 64 * kind + 32 * r + MH)
                    src = ps[at, 6:8, :].rearrange("m b j -> m (b j)")
                    mark(dve.tensor_scalar(dst[32 * r:32 * r + MH], src if r == 0 else src[:, ::-1],
                                           gbias[at, :], None, ALU.add), names[r])

            def chunks(t):
                return t[:].rearrange("m (c j) -> m c j", j=P)

            def conv_sum(hn, j):
                return rawb[:] if j == 0 else conv_sum0[:] if is_zero(hn) else ab[:, 0]

            def clear_pads():
                dve.memset(conv_in[1][:, 0:CONV // 2], 0.0)
                dve.memset(conv_in[1][:, S + CONV // 2:S + CONV], 0.0).then_inc(pads_set, 1)

            def conv_taps(hn, j):
                n = 5 * j
                g, _ = tile_no(0, 0, 0, j) if is_zero(hn) else tile_no(G_M, 8, hn - 1, 4 + j)
                src, y = conv_in[j], conv_sum(hn, j)
                if j == 1:
                    dve.wait_ge(pads_set, hn + 1)
                dve.wait_ge(proj_read, 2 * g + 2)
                dve.tensor_scalar(y, src[:, 0:S], hcv[:, j, 0:1], hcv[:, j, CONV:CONV + 1],
                                  ALU.mult, ALU.add).then_inc(conv_dve.sem, 1)
                for w in range(1, CONV):
                    dve.wait_ge(conv_dve.sem, conv_dve.after(hn, n + w - 1))
                    dve.scalar_tensor_tensor(y, src[:, w:w + S], hcv[:, j, w:w + 1], y,
                                             ALU.mult, ALU.add).then_inc(conv_dve.sem, 1)
                dve.wait_ge(conv_dve.sem, conv_dve.after(hn, n + CONV - 1))
                dve.scalar_tensor_tensor(qkf[:, j], y, -1.0, y, ALU.mult, ALU.min).then_inc(conv_dve.sem, 1)

            def conv_logsig(hn, j):
                dve.wait_ge(conv_act.sem, conv_act.after(hn, 2 * j + 1))
                dve.scalar_tensor_tensor(qkf[:, j], conv_sum(hn, j), 0.0, qkf[:, j], ALU.min,
                                         ALU.subtract).then_inc(conv_dve.sem, 1)

            def conv_final(hn, j):
                dve.wait_ge(conv_act.sem, conv_act.after(hn, 4 + j))
                dve.scalar_tensor_tensor(qkf[:, j], conv_sum(hn, j), (MQK ** -0.5, 1.0)[j], qkf[:, j], ALU.mult,
                                         ALU.mult).then_inc(conv_dve.sem, 1)

            def qk_low(hn, j):
                dve.wait_ge(qk_hi.sem, qk_hi.after(hn, j))
                dve.tensor_tensor((qT, kT)[j][:, 1], qkf[:, j], (qT, kT)[j][:, 0].bitcast(F32),
                                  ALU.subtract).then_inc(qk_lo.sem, 1)

            def v_low(hn, e):
                for i in range(2):
                    dve.wait_ge(tr_hi.sem, tr_hi.after(hn, 2 * e + i))
                    dve.tensor_tensor(vS[:, 1, 4 * i:4 * i + 4, e * P:(e + 1) * P],
                                      ps[:, (7, 2)[i], :].rearrange("p (c d) -> p c d", c=4),
                                      vS[:, 0, 4 * i:4 * i + 4, e * P:(e + 1) * P].bitcast(F32),
                                      ALU.subtract).then_inc(tr_read.sem, 1)

            gate_rows(r_i, 0, ("i_fw", "i_bw"))
            gate_rows(r_f, 1, ("f_fw", "f_bw"))
            after_step("f_bw")
            mark(dve.scalar_tensor_tensor(r_t[:], r_f[:], -1.0, r_f[:], ALU.mult, ALU.min), "abs_f")
            dve.wait_ge(prep_act, prep_act_at("ln_f"))
            mark(dve.scalar_tensor_tensor(r_f[:], r_f[:], 0.0, r_t[:], ALU.min, ALU.subtract), "log_f")
            after_step("log_f")
            dve.wait_ge(consts_set, 10)
            mark(dve.tensor_tensor_scan(r_t[:], r_reset[:], r_f[:], 0.0, ALU.mult, ALU.add), "a")
            after_step("a")
            mark(dve.tensor_tensor(r_i[:], r_i[:], r_t[:], ALU.subtract), "b")
            mark(dve.tensor_copy(chunks(r_carry)[:, 1:NC, 0], chunks(r_t)[:, 0:NC - 1, P - 1]), "carry")
            after_step("carry")
            mark(dve.tensor_tensor_scan(r_m[:], r_carry[:], r_i[:], 0.0, ALU.add, ALU.max), "max")
            after_step("max")
            a_end, m_end = chunks(r_t)[:, :, P - 1], chunks(r_m)[:, :, P - 1]
            mark(dve.tensor_tensor(r_mp[:, 1:NC], a_end[:, 0:NC - 1], m_end[:, 0:NC - 1], ALU.add), "m_prev")
            after_step("m_prev")
            mark(dve.tensor_tensor(r_dec[:], r_mp[:], m_end, ALU.subtract), "decay")
            wide = [ROWS, NC, P]
            mark(dve.tensor_tensor(chunks(r_winter), r_mp[:].unsqueeze(2).to_broadcast(wide), chunks(r_m),
                                   ALU.subtract), "w_inter")
            mark(dve.tensor_tensor(r_t[:], r_t[:], r_m[:], ALU.add), "a_plus_m")
            mark(dve.tensor_tensor(chunks(r_wk), chunks(r_i), m_end.unsqueeze(2).to_broadcast(wide),
                                   ALU.subtract), "w_k")
            conv_taps(0, 0)
            dve.wait_ge(x_tr, 2 * ST)
            clear_pads()
            conv_taps(0, 1)
            conv_logsig(0, 0)
            conv_logsig(0, 1)
            dve.wait_ge(prep_act, prep_act_at("lam_exp"))
            mark(dve.scalar_tensor_tensor(neglam[:], lams[:, 3:4], -LAM_INIT, lams[:, 2:3], ALU.add,
                                          ALU.subtract), "neglam")
            conv_final(0, 0)
            dve.wait_ge(prep_pe, 4)
            cols_ps = ps[:, 2:7, 0:NC * ROWS].rearrange("p q (c x) -> p c q x", x=ROWS)
            mark(dve.tensor_copy(col[:, 0:NC], cols_ps[:, :, :, 0:MH]), "col_fw")
            mark(dve.tensor_copy(colrev[:], cols_ps[:, :, :, 32:ROWS]), "col_rev")
            mark(dve.tensor_copy(decay[:], ps[:, 7, 256:256 + 16 * MH].rearrange("p (m c) -> p m c", m=MH)), "decay_all")
            dve.wait_ge(prep_pe, 5)
            mark(dve.tensor_copy(col[:, NC:2 * NC], ps[:, 7, 0:NC * 5 * MH].rearrange(
                "p (c q m) -> p c q m", c=NC, q=5)), "col_bw")
            after_step("col_bw")
            v_low(0, 0)
            ones_cols = ones[:, 0:2 * NC].rearrange("p (c two) -> p c two", two=2)
            dve.tensor_copy(vS[:, 0, :, MV:MV + 2], ones_cols)
            dve.tensor_scalar(vS[:, 1, :, MV:MV + 2], ones_cols, 0.0, None, ALU.mult)
            conv_final(0, 1)
            qk_low(0, 0)
            qk_low(0, 1)
            v_low(0, 1)

            def gate_abs(h, e, part):
                g, _ = tile_no(G_M, 8, h, 2 * e + part)
                dve.wait_ge(proj_read, 2 * g + 2)
                src = rawb[:] if part == 0 else zg[:, e]
                if part == 1 and e == 0:
                    dve.wait_ge(spilled_m[1], 16 * (2 * h + 1))
                if part == 0 and e == 1:
                    dve.wait_ge(gate_dve.sem, gate_dve.after(h, 5))
                dve.scalar_tensor_tensor(ab[:, part], src, -1.0, src, ALU.mult, ALU.min).then_inc(gate_dve.sem, 1)

            def gate_logsig(h, e, part):
                n = 6 * e + 2 * part
                dve.wait_ge(gate_act.sem, gate_act.after(h, 5 * e + 2 * part + 1))
                src = rawb[:] if part == 0 else zg[:, e]
                dve.scalar_tensor_tensor(ab[:, part], src, 0.0, ab[:, part], ALU.min,
                                         ALU.subtract).then_inc(gate_dve.sem, 1)
                if part == 1:
                    dve.wait_ge(gate_dve.sem, gate_dve.after(h, n + 1))
                    dve.tensor_tensor(ab[:, 1], ab[:, 0], ab[:, 1], ALU.add).then_inc(gate_dve.sem, 1)

            def gate_final(h, e):
                dve.wait_ge(gate_act.sem, gate_act.after(h, 5 * e + 4))
                dve.scalar_tensor_tensor(zg[:, e], zg[:, e], hg[:, e:e + 1], ab[:, 1], ALU.mult,
                                         ALU.mult).then_inc(gate_dve.sem, 1)

            def chunk(r, t):
                return t if r == 0 else NC - 1 - t

            def diagonals(h, t):
                if t == 0:
                    dve.wait_ge(hcols.sem, hcols.after(h, 0))
                else:
                    dve.wait_ge(score_done.sem, score_done.after(h, t - 1))
                for r in range(2):
                    d = dve.tensor_scalar(dg[:, r], ident[:], hc[:, 8 * r + t, Q_M:Q_M + 1], -1.0, ALU.mult, ALU.mult)
                d.then_inc(diag_done.sem, 1)

            def m_step(h, t):
                if t < NC - 1:
                    diagonals(h, t + 1)
                dve.wait_ge(w_done.sem, w_done.after(h, t))
                if t > 0:
                    dve.wait_ge(ptlo_done.sem, ptlo_done.after(h, t - 1))
                dve.tensor_tensor(ptf[:], ps[:, 2, 0:2 * P].rearrange("p (r j) -> p r j", r=2), wt[:],
                                  ALU.mult).then_inc(ptf_done.sem, 1)
                dve.wait_ge(pthi_done.sem, pthi_done.after(h, t))
                dve.tensor_tensor(pt[:, 1], ptf[:], pt[:, 0].bitcast(F32), ALU.subtract).then_inc(ptlo_done.sem, 1)
                if t < NC - 1:
                    dve.wait_ge(kwhi_done.sem, kwhi_done.after(h, t))
                    for r in range(2):
                        lo = dve.scalar_tensor_tensor(kw[:, 1, r], kseq[:, chunk(r, t)], hc[:, 8 * r + t, Q_WK:Q_WK + 1],
                                                      kw[:, 0, r].bitcast(F32), ALU.mult, ALU.subtract)
                    lo.then_inc(kwlo_done.sem, 1)
                if t == 1:
                    clear_pads()
                if t == 2:
                    gate_abs(h, 0, 0)
                elif t == 3:
                    gate_logsig(h, 0, 0)
                elif t == 4:
                    gate_abs(h, 0, 1)
                elif t == 5:
                    gate_logsig(h, 0, 1)
                elif t == 6:
                    gate_final(h, 0)
                    gate_abs(h, 1, 0)
                elif t == 7:
                    gate_logsig(h, 1, 0)
                if t > 0:
                    dve.wait_ge(intersc_done.sem, intersc_done.after(h, t - 1))

                def add_intra(r):
                    src = ps[:, (4, 7)[r], 0:MV + 2]
                    if t > 0:
                        return dve.tensor_tensor(num[:, r], src, num[:, r], ALU.add)
                    return dve.tensor_copy(num[:, r], src)

                dve.wait_ge(intra_done.sem, intra_done.after(h, t))
                add_intra(0)
                if t < NC - 1:
                    dve.wait_ge(upd_done.sem, upd_done.after(h, t))
                    upd = ps[:, 6, :].rearrange("p (r e) -> p r e", r=2)
                    nup = ps[:, 7, MV + 4:MV + 8].rearrange("p (r two) -> p r two", r=2)
                    if t == 0:
                        dve.tensor_copy(cf[:, :, 0:MV], upd)
                        d = dve.tensor_copy(cf[:, :, MV:MV + 2], nup)
                    else:
                        dve.wait_ge(clo_done.sem, clo_done.after(h, t - 1))
                        for r in range(2):
                            dve.scalar_tensor_tensor(cf[:, r, 0:MV], cf[:, r, 0:MV], hd[:, 8 * r + t:8 * r + t + 1],
                                                     upd[:, r], ALU.mult, ALU.add)
                            d = dve.scalar_tensor_tensor(cf[:, r, MV:MV + 2], cf[:, r, MV:MV + 2],
                                                         hd[:, 8 * r + t:8 * r + t + 1], nup[:, r], ALU.mult, ALU.add)
                    d.then_inc(state_done.sem, 1)
                add_intra(1).then_inc(num_done.sem, 1)
                dve.wait_ge(num_done.sem, num_done.after(h, t))
                dve.tensor_scalar(dsm[:, 0], num[:, :, MV], -1.0, None, ALU.mult).then_inc(den_chain.sem, 1)
                dve.wait_ge(den_chain.sem, den_chain.after(h, 3 * t))
                for r in range(2):
                    d = dve.scalar_tensor_tensor(dsm[:, 1, r:r + 1], num[:, r, MV:MV + 1],
                                                 hc[:, 8 * r + t, Q_EMJ:Q_EMJ + 1], dsm[:, 0, r:r + 1],
                                                 ALU.max, ALU.max)
                d.then_inc(den_chain.sem, 1)
                dve.wait_ge(den_chain.sem, den_chain.after(h, 3 * t + 1))
                dve.reciprocal(dsm[:, 2], dsm[:, 1]).then_inc(den_chain.sem, 1)
                if t < NC - 1:
                    dve.wait_ge(chi_done.sem, chi_done.after(h, t))
                    dve.tensor_tensor(cs[:, 1], cf[:], cs[:, 0].bitcast(F32), ALU.subtract).then_inc(clo_done.sem, 1)
                dve.wait_ge(den_chain.sem, den_chain.after(h, 3 * t + 2))
                if t > 0:
                    dve.wait_ge(h_done.sem, h_done.after(h, t - 1))
                for r in range(2):
                    c = chunk(r, t)
                    if t < NC // 2:
                        d = dve.tensor_scalar(hacc[:, c], num[:, r, 0:MV], dsm[:, 2, r:r + 1], None, ALU.mult)
                    else:
                        d = dve.scalar_tensor_tensor(hacc[:, c], num[:, r, 0:MV], dsm[:, 2, r:r + 1], hacc[:, c],
                                                     ALU.mult, ALU.add)
                d.then_inc(h_done.sem, 1)

            def h_out(h, e, between=None):
                for k in (2 * e, 2 * e + 1):
                    i = k % 2
                    dve.wait_ge(tr_done.sem, tr_done.after(h, k))
                    if k > 0:
                        dve.wait_ge(hsplit_done.sem, hsplit_done.after(h, k - 1))
                    dve.tensor_tensor(hst[:], ps[:, (7, 2)[k % 2], :], zg[:, e, i * HALF:(i + 1) * HALF],
                                      ALU.mult).then_inc(tr_read.sem, 1)
                    if i == 0 and between is not None:
                        between()
                    dve.wait_ge(hsp_hi.sem, hsp_hi.after(h, k))
                    dve.tensor_tensor(hsp[i][:, 1], hst[:], hsp[i][:, 0].bitcast(F32), ALU.subtract) \
                        .then_inc(hsplit_done.sem, 1)

            def shuffle(hh, n):
                swap = [(i + ROPE // 2) % ROPE if i < ROPE else i for i in range(32)]
                for half in range(2):
                    cols = slice(half * HALF, (half + 1) * HALF)
                    if is_zero(hh):
                        g, _ = tile_no(G_M, 8, MH - 1, 4 + n // 2)
                    else:
                        g, _ = tile_no(G_A, 4, hh - 1, n // 2)
                    dve.wait_ge(proj_read, 2 * g + half + 1)
                    dve.sem_inc(step_begun, 1)
                    dve.stream_shuffle((rawa, rawb)[n // 2][:, cols], qkf[:, n // 2, cols], swap).then_inc(shuf_done, 1)

            own = (slice(0, AD), slice(AD, P))

            def rope_first_k():
                dve.wait_ge(shuf_done, 4)
                dve.wait_ge(rope_loaded, 16 * 2)
                dve.tensor_tensor(qkf[:, 1], qkf[:, 1], cos[:], ALU.mult).then_inc(rope_k0, 1)
                dve.tensor_tensor(rawb[:], rawb[:], sin[:], ALU.mult).then_inc(rope_k0, 1)
                dve.wait_ge(rope_k0, 2)
                dve.tensor_tensor(qkf[:, 1], qkf[:, 1], rawb[:], ALU.add).then_inc(rope_k0, 1)

            def k_low(hh, comps=(0, 1)):
                for c in comps:
                    dve.wait_ge(a_qk_hi.sem, a_qk_hi.after(hh, c))
                    dve.tensor_tensor(ks[own[c], c, 1], qkf[own[c], 1], ks[own[c], c, 0].bitcast(F32),
                                      ALU.subtract).then_inc(a_qk_lo.sem, 1)

            def q_low(hh, c):
                dve.wait_ge(a_qk_hi.sem, a_qk_hi.after(hh, 2 + c))
                dve.tensor_tensor(qs[own[1 - c], c], qkf[own[c], 0], qs[own[c], c].bitcast(F32),
                                  ALU.subtract).then_inc(a_qk_lo.sem, 1)

            def m_head(h, last):
                dve.tensor_copy(hc[:], col[:, :, :, bass.ds(h, 1)].rearrange("p c q one -> p c (q one)")) \
                    .then_inc(hcols.sem, 1)
                dve.tensor_copy(hd[:], decay[:, bass.ds(h, 1), :].rearrange("p one c -> p (one c)")).then_inc(hcols.sem, 1)
                dve.tensor_copy(hg[:], vecs[:, bass.ds(V_MG + 2 * h, 2)]).then_inc(hcols.sem, 1)
                nxt = (h + 1) if not last else 0
                dve.tensor_copy(hcv[:], conv_cols[:, :, :, bass.ds(nxt, 1)].rearrange("p q w one -> p q (w one)")) \
                    .then_inc(hcols.sem, 1)
                diagonals(h, 0)
                for t in range(NC):
                    m_step(h, t)
                gate_abs(h, 1, 1)
                dve.wait_ge(hs_act.sem, hs_act.after(h, 2))
                for c in range(NC):
                    d = dve.tensor_scalar(hacc[:, c], hacc[:, c], hstat[:, 1, c:c + 1], None, ALU.mult)
                d.then_inc(hs_done.sem, 1)
                gate_logsig(h, 1, 1)
                gate_final(h, 1)
                h_out(h, 0)
                if not last:
                    conv_taps(h + 1, 0)
                    conv_taps(h + 1, 1)
                else:
                    shuffle(0, 0)
                h_out(h, 1, between=None if last else lambda: conv_logsig(h + 1, 0))
                if not last:
                    conv_logsig(h + 1, 1)
                    conv_final(h + 1, 0)
                    v_low(h + 1, 0)
                    conv_final(h + 1, 1)
                    qk_low(h + 1, 0)
                    qk_low(h + 1, 1)
                    v_low(h + 1, 1)
                else:
                    shuffle(0, 2)
                    rope_first_k()
                    k_low(0)
                    for c in range(2):
                        q_low(0, c)

            with dve.Fori(0, MH - 1) as h:
                m_head(h, False)
            m_head(MH - 1, True)

            def mix(h, q):
                b = q % 2
                dve.wait_ge(a_exp.sem, a_exp.after(h, 2 * q + 1))
                dve.reciprocal(rden[:, 0], den[:, b]).then_inc(a_mix.sem, 1)
                dve.wait_ge(a_mix.sem, a_mix.after(h, 4 * q))
                dve.tensor_scalar(rden[:, 1, 0:1], rden[:, 0, 1:2], neglam[:], None, ALU.mult).then_inc(a_mix.sem, 1)
                if q >= 2:
                    dve.wait_ge(a_tr.sem, a_tr.after(h, round_of(q - 2, 1)))
                dve.tensor_scalar(am[b][:], pr[:, 0], rden[:, 0, 0:1], None, ALU.mult).then_inc(a_mix.sem, 1)
                dve.wait_ge(a_mix.sem, a_mix.after(h, 4 * q + 2))
                dve.scalar_tensor_tensor(am[b][:], pr[:, 1], rden[:, 1, 0:1], am[b][:], ALU.mult,
                                         ALU.add).then_inc(a_mix.sem, 1)

            def maxima(h, q):
                for c in range(2):
                    dve.wait_ge(a_score.sem, a_score.after(h, 2 * q + c))
                    dve.tensor_reduce(nmax[:, q % 2, c:c + 1], ps[:, 2 + 2 * c:4 + 2 * c, :].rearrange("p b k -> p (b k)"),
                                      AX_X, ALU.max, negate=True).then_inc(a_max.sem, 1)

            def a_low_round(h, k, dst):
                dve.wait_ge(a_tr_hi.sem, a_tr_hi.after(h, k))
                dve.tensor_tensor(dst(1), ps[:, 6, :].rearrange("p (k s) -> p k s", k=4), dst(0).bitcast(F32),
                                  ALU.subtract).then_inc(a_tr_read.sem, 1)

            def v_dst(i):
                return lambda p: va[:, p, 4 * i:4 * i + 4, :]

            def at_dst(q, i):
                return lambda p: at_s[:, p, 4 * i:4 * i + 4, (q % 2) * P:(q % 2 + 1) * P]

            def o_square(h, n):
                dve.wait_ge(a_of.sem, a_of.after(h, n))
                dve.tensor_tensor(osq[:], of[:], of[:], ALU.mult).then_inc(a_osq.sem, 1)

            def o_out_gate(h, n):
                dve.wait_ge(a_rs.sem, a_rs.after(h, 2 * n + 1))
                if n > 0:
                    dve.wait_ge(a_olo.sem, a_olo.after(h, n - 1))
                dve.tensor_tensor(ost[:], of[:], ors[:], ALU.mult).then_inc(a_ost.sem, 1)
                dve.wait_ge(a_ost.sem, a_ost.after(h, 2 * n))
                dve.tensor_tensor(ost[:], ost[:], ga[:, 2 * n * P:2 * (n + 1) * P], ALU.mult).then_inc(a_ost.sem, 1)

            def o_out_low(h, n):
                dve.wait_ge(a_ohi.sem, a_ohi.after(h, n))
                dve.tensor_tensor(osp[:, 1], ost[:], osp[:, 0].bitcast(F32), ALU.subtract).then_inc(a_olo.sem, 1)

            def a_head(h, first, last):
                maxima(h, 0)
                dve.wait_ge(proj_read, 2 * (4 * h + G_A))
                dve.scalar_tensor_tensor(aw[:], vz[:, 1], -1.0, vz[:, 1], ALU.mult, ALU.min) \
                    .then_inc(a_gate_dve.sem, 1)
                a_low_round(h, V_ROUND[0], v_dst(0))
                mix(h, 0)
                for q in range(ST):
                    a_low_round(h, round_of(q, 0), at_dst(q, 0))
                    if q + 1 < ST:
                        maxima(h, q + 1)
                    elif not last:
                        k_low(h + 1, (1,))
                    a_low_round(h, round_of(q, 1), at_dst(q, 1))
                    if q + 1 < ST:
                        mix(h, q + 1)
                    elif not last:
                        for c in range(2):
                            q_low(h + 1, c)
                    if q == 0:
                        a_low_round(h, V_ROUND[1], v_dst(1))
                    if q == 0 and not first:
                        o_out_gate(h - 1, 3)
                    if q == 1:
                        if not first:
                            o_out_low(h - 1, 3)
                        dve.wait_ge(a_gate_act.sem, a_gate_act.after(h, 1))
                        dve.scalar_tensor_tensor(aw[:], vz[:, 1], 0.0, aw[:], ALU.min, ALU.subtract) \
                            .then_inc(a_gate_dve.sem, 1)
                    if not last and q == 6:
                        k_low(h + 1, (0,))
                    if q in (2, 4):
                        o_out_gate(h, q // 2 - 1)
                    if q in (3, 5):
                        o_out_low(h, q // 2 - 1)
                    if q == 7:
                        o_out_gate(h, 2)
                        o_out_low(h, 2)
                    if not last and q in (1, 3):
                        shuffle(h + 1, q - 1)
                    if q == 1:
                        dve.wait_ge(a_gate_act.sem, a_gate_act.after(h, 2))
                        dve.scalar_tensor_tensor(ga[:], vz[:, 1], again[:], aw[:], ALU.mult, ALU.mult) \
                            .then_inc(a_gate_dve.sem, 1)
                    if q % 2 == 1:
                        o_square(h, q // 2)

            a_head(0, True, False)
            with dve.Fori(1, AH - 1) as h:
                a_head(h, False, False)
            a_head(AH - 1, False, True)
            o_out_gate(AH - 1, 3)
            o_out_low(AH - 1, 3)

            def merge(n, base):
                with dve.Fori(0, KT // 2) as c:
                    for par in range(2):
                        i = KT * n + 2 * c + par
                        z = qkf[:, par]
                        dve.wait_ge(g_loaded[par], 16 * (KT // 2 * n + c + 1))
                        dve.wait_ge(f_product, i + 1)
                        dve.scalar_tensor_tensor(fw[:], z, -1.0, z, ALU.mult, ALU.min).then_inc(f_abs, 1)
                        dve.wait_ge(f_act, 3 * i + 2)
                        dve.scalar_tensor_tensor(fw[:], z, 0.0, fw[:], ALU.min, ALU.subtract).then_inc(f_logsig, 1)
                        g, _ = tile_no(base, 2, c, par)
                        dve.wait_ge(proj_read, 2 * g + 2)
                        dve.wait_ge(f_act, 3 * i + 3)
                        yd = ya[:, bass.ds(2 * c + par, 1), :].rearrange("p one s -> p (one s)")
                        if n == 0:
                            dve.tensor_tensor(yd, fw[:], fb[:], ALU.mult).then_inc(f_product, 1)
                        else:
                            dve.tensor_tensor(fw[:], fw[:], fb[:], ALU.mult).then_inc(f_product, 1)
                            dve.wait_ge(f_product, i + 2)
                            dve.tensor_tensor(yd, yd, fw[:], ALU.add).then_inc(f_y, 1)
                            dve.wait_ge(y_hi, 2 * c + par + 1)
                            dve.tensor_tensor(ys[:, 1, bass.ds(2 * c + par, 1), :].rearrange("p one s -> p (one s)"), yd,
                                              ys[:, 0, bass.ds(2 * c + par, 1), :].rearrange(
                                                  "p one s -> p (one s)").bitcast(F32),
                                              ALU.subtract).then_inc(y_lo, 1)

            dve.sem_inc(f_product, 1)
            merge(0, G_FA)
            merge(1, G_FB)

            dve.memset(row_sums[:], 0.0).then_inc(o_sums, 1)
            dve.wait_ge(post_loaded, 16)

            def rows(c, par):
                for i in range(2):
                    dve.wait_ge(o_tr, 2 * c + i + 1)
                    dst = orow[:, 4 * i:4 * i + 4, bass.ds(c * P, P)]
                    gain = post_bc[:, bass.ds(c * P, P)].unsqueeze(1).to_broadcast([P, 4, P])
                    dve.tensor_tensor(dst, ps[:, 2 + 2 * par + i, :].rearrange("p (t s) -> p t s", t=4), gain,
                                      ALU.mult).then_inc(o_rows, 1)
                dve.wait_ge(o_squares, 2 * c + 2)
                dve.wait_ge(o_sums, c + 1)
                dve.tensor_tensor(row_sums[:], row_sums[:], tile_sums[:, par], ALU.add).then_inc(o_sums, 1)

            with dve.Fori(0, KT // 2) as c2:
                for par in range(2):
                    rows(2 * c2 + par, par)
            dve.wait_ge(res_loaded, 16 * ST)
            dve.wait_ge(o_stat, 2)
            dve.wait_ge(o_rows, 2 * KT)
            for t in range(ST):
                dve.scalar_tensor_tensor(orow[:, t], orow[:, t], tail_stat[:, t:t + 1], xres[:, t],
                                         ALU.mult, ALU.add).then_inc(o_out, 1)

        @block.scalar
        def _(act):
            def mark(ins, name):
                assert name in PREP_ACT
                ins.then_inc(prep_act, 1)

            def read_half(base, per_head, h, j, half, dst, scale=1.0, bias=None):
                g, _ = tile_no(base, per_head, h, j)
                act.wait_ge(proj_done, 2 * g + half + 1)
                if bias is None:
                    act.activation(dst, ps[:, half, :], ACT.Copy, scale=scale).then_inc(proj_read, 1)
                else:
                    act.activation(dst, ps[:, half, :], ACT.Identity, bias=bias).then_inc(proj_read, 1)

            def exp_ln(t, sig, waits_own):
                act.activation(t, t, ACT.Exp).then_inc(sig, 1)
                act.wait_ge(sig, waits_own)
                act.activation(t, t, ACT.Ln, bias=1.0).then_inc(sig, 1)

            act.preload_act_table_set("natural_log_exp_and_others")
            for i in range(2):
                act.sem_inc(spilled_m[i], 16)
            act.sem_inc(spilled_a, 16)

            def x_high(t):
                for i in range(2):
                    act.wait_ge(x_tr, 2 * t + i + 1)
                    act.activation(xs[:, 0, 4 * i:4 * i + 4, t * P:(t + 1) * P],
                                   ps[:, 2 + 2 * (t % 2) + i, :].rearrange("p (k s) -> p k s", k=4),
                                   ACT.Copy).then_inc(x_hi, 1)

            act.wait_ge(consts_set, 1)
            for t in range(ST):
                act.wait_ge(x_loaded[t % 4], 16 * (t // 4 + 1))
                act.activation(rawb[:], xin[t % 4], ACT.Square, accum_out=xstat[:, 0, t:t + 1]).then_inc(x_stat, 1)
                act.wait_ge(x_stat, 3 * t + 1)
                act.activation(xstat[:, 1, t:t + 1], xstat[:, 0, t:t + 1], ACT.Ln, bias=eps[:], scale=1.0 / D) \
                    .then_inc(x_stat, 1)
                act.wait_ge(x_stat, 3 * t + 2)
                act.activation(xstat[:, 1, t:t + 1], xstat[:, 1, t:t + 1], ACT.Exp, scale=-0.5).then_inc(x_stat, 1)
                if t > 0:
                    x_high(t - 1)
            x_high(ST - 1)

            def conv_exp_ln(hn, j):
                act.wait_ge(conv_dve.sem, conv_dve.after(hn, 5 * j + CONV))
                exp_ln(qkf[:, j], conv_act.sem, conv_act.after(hn, 2 * j))

            def conv_exp(hn, j):
                act.wait_ge(conv_dve.sem, conv_dve.after(hn, 10 + j))
                act.activation(qkf[:, j], qkf[:, j], ACT.Exp).then_inc(conv_act.sem, 1)

            def qk_high(hn, j):
                act.wait_ge(conv_dve.sem, conv_dve.after(hn, 12 + j))
                act.activation((qT, kT)[j][:, 0], qkf[:, j], ACT.Copy).then_inc(qk_hi.sem, 1)

            def read_conv(base, per_head, h, hn, j, tile):
                for half in range(2):
                    read_conv_half(base, per_head, h, j, tile, half)

            def read_conv_half(base, per_head, h, j, tile, half):
                at = CONV // 2 + half * HALF
                read_half(base, per_head, h, tile, half, conv_in[j][:, at:at + HALF])

            def k_rows(h):
                for i in range(2):
                    act.wait_ge(tr_done.sem, tr_done.after(h, 6 + i))
                    act.activation(kseq[:, 4 * i:4 * i + 4], ps[:, (7, 2)[i], :].rearrange("p (c d) -> p c d", c=4),
                                   ACT.Copy).then_inc(tr_read.sem, 1)

            def v_high(h, e):
                for i in range(2):
                    act.wait_ge(tr_done.sem, tr_done.after(h, 4 + 4 * e + i))
                    act.activation(vS[:, 0, 4 * i:4 * i + 4, e * P:(e + 1) * P],
                                   ps[:, (7, 2)[i], :].rearrange("p (c d) -> p c d", c=4),
                                   ACT.Copy).then_inc(tr_hi.sem, 1)

            def read_gate(base, per_head, h, j, half, n, buf, bias):
                if half == 0 and not (isinstance(n, int) and n < 2):
                    act.wait_ge(g_spilled[j % 2], 16 * ((KT + 4) // 2 - 2 + h if not isinstance(n, int) else n // 2))
                read_half(base, per_head, h, j, half, buf[:, j % 2, half * HALF:(half + 1) * HALF], bias=bias)
                if half == 1:
                    g, _ = tile_no(base, per_head, h, j)
                    act.wait_ge(proj_read, 2 * g + 2)
                    act.dma_start(spill_g[bass.ds(n, 1)].rearrange("one p s -> (one p) s"), buf[:, j % 2]) \
                        .then_inc(g_spilled[j % 2], 16)

            def read_gates(base, j0, numbers, buf):
                for n in numbers:
                    for half in range(2):
                        read_gate(base, 0, 0, j0 + n - numbers[0], half, n, buf, bmerge[:, n:n + 1])

            act.wait_ge(prep_dve, prep_dve_at("bmerge"))
            act.wait_ge(consts_set, 3)
            act.wait_ge(prep_dve, prep_dve_at("lam_sums"))
            mark(act.activation(lams[:, 2:4], lams[:, 0:2], ACT.Exp), "lam_exp")
            act.wait_ge(prep_dve, prep_dve_at("abs_f"))
            mark(act.activation(r_t[:], r_t[:], ACT.Exp), "exp_f")
            act.wait_ge(prep_act, prep_act_at("exp_f"))
            mark(act.activation(r_t[:], r_t[:], ACT.Ln, bias=1.0), "ln_f")
            read_conv(0, 0, 0, 0, 0, 0)
            act.wait_ge(prep_dve, prep_dve_at("decay"))
            mark(act.activation(r_dec[:], r_dec[:], ACT.Exp), "decay")
            act.wait_ge(prep_dve, prep_dve_at("w_inter"))
            mark(act.activation(r_winter[:], r_winter[:], ACT.Exp), "w_inter")
            act.wait_ge(prep_dve, prep_dve_at("a_plus_m"))
            mark(act.activation(r_t[:], r_t[:], ACT.Exp, scale=-1.0), "emj")
            act.wait_ge(prep_dve, prep_dve_at("w_k"))
            mark(act.activation(r_wk[:], r_wk[:], ACT.Exp), "w_k")
            read_conv(0, 0, 0, 0, 1, 1)
            conv_exp_ln(0, 0)
            conv_exp_ln(0, 1)
            conv_exp(0, 0)
            read_gates(0, 2, range(0, 2), gate_fill)
            read_gates(0, 4, range(2, 4), gate_fill)
            act.wait_ge(conv_dve.sem, conv_dve.after(0, 5 + CONV - 1))
            def read_first_v(e, half):
                read_half(0, 0, 0, 6 + e, half, vz[:, e, half * HALF:(half + 1) * HALF])

            for half in range(2):
                read_first_v(0, half)
            for j in range(2):
                act.wait_ge(g_spilled[j], 16 * 2)
            v_high(-1, 0)
            conv_exp(0, 1)
            qk_high(0, 0)
            read_first_v(1, 0)
            k_rows(-1)
            qk_high(0, 1)
            read_first_v(1, 1)
            v_high(-1, 1)

            def chunk(r, t):
                return t if r == 0 else NC - 1 - t

            def gate_exp_ln(h, e, part):
                n = 6 * e + (0, 2)[part]
                act.wait_ge(gate_dve.sem, gate_dve.after(h, n))
                exp_ln(ab[:, part], gate_act.sem, gate_act.after(h, 5 * e + 2 * part))

            def gate_exp(h, e):
                act.wait_ge(gate_dve.sem, gate_dve.after(h, 6 * e + 4))
                act.activation(ab[:, 1], ab[:, 1], ACT.Exp).then_inc(gate_act.sem, 1)

            def read_oz(h, n):
                j, half = divmod(n, 2)
                cols = slice(half * HALF, (half + 1) * HALF)
                if n == 4:
                    act.wait_ge(gate_dve.sem, gate_dve.after(h, 1))
                read_half(G_M, 8, h, j, half, rawb[:, cols] if j % 2 == 0 else zg[:, j // 2, cols])

            def read_qk(h, j, half, last):
                if not last:
                    read_conv_half(G_M, 8, h, j, 4 + j, half)
                else:
                    read_rope(G_M, 8, h, 0, 2 * j, half)

            def m_step(h, t, last):
                act.wait_ge(score_done.sem, score_done.after(h, t))
                if t == 0:
                    act.wait_ge(hcols.sem, hcols.after(h, 0))
                else:
                    act.wait_ge(ptf_done.sem, ptf_done.after(h, t - 1))
                for r in range(2):
                    a = act.activation(wt[:, r], ps[:, 2, (2 + r) * P:(3 + r) * P], ACT.Exp,
                                       bias=hc[:, 8 * r + t, Q_B:Q_B + 1])
                a.then_inc(w_done.sem, 1)
                act.wait_ge(ptf_done.sem, ptf_done.after(h, t))
                if t > 0:
                    act.wait_ge(intra_done.sem, intra_done.after(h, t - 1))
                act.activation(pt[:, 0], ptf[:], ACT.Copy).then_inc(pthi_done.sem, 1)
                if t < NC - 1:
                    if t > 0:
                        act.wait_ge(upd_done.sem, upd_done.after(h, t - 1))
                    else:
                        act.wait_ge(tr_read.sem, tr_read.after(h - 1, 7))
                    for r in range(2):
                        a = act.activation(kw[:, 0, r], kseq[:, chunk(r, t)], ACT.Copy,
                                           scale=hc[:, 8 * r + t, Q_WK:Q_WK + 1])
                    a.then_inc(kwhi_done.sem, 1)
                if t == 3:
                    gate_exp_ln(h, 0, 0)
                elif t == 5:
                    gate_exp_ln(h, 0, 1)
                elif t == 6:
                    gate_exp(h, 0)
                elif t == 7:
                    gate_exp_ln(h, 1, 0)
                if t < NC - 1:
                    read_oz(h, t + 1)
                else:
                    read_qk(h, 0, 0, last)
                if t > 0:
                    act.wait_ge(inter_done.sem, inter_done.after(h, t - 1))
                    act.wait_ge(h_done.sem, h_done.after(h, t - 1))
                    for r in range(2):
                        a = act.activation(num[:, r], ps[:, (5, 3)[r], 0:MV + 2], ACT.Copy,
                                           scale=hc[:, 8 * r + t, Q_WINTER:Q_WINTER + 1])
                    a.then_inc(intersc_done.sem, 1)
                if t < NC - 1:
                    act.wait_ge(state_done.sem, state_done.after(h, t))
                    act.activation(cs[:, 0], cf[:], ACT.Copy).then_inc(chi_done.sem, 1)

            own = (slice(0, AD), slice(AD, P))

            def k_high(hh):
                if is_zero(hh):
                    act.wait_ge(rope_k0, 3)
                else:
                    act.wait_ge(rope_done, 3 * (4 * hh + 3) + 3)
                for c in range(2):
                    act.activation(ks[own[c], c, 0], qkf[own[c], 1], ACT.Copy).then_inc(a_qk_hi.sem, 1)

            def q_high(hh, comps=(0, 1)):
                for c in comps:
                    act.activation(qs[own[c], c], qkf[own[c], 0], ACT.Copy).then_inc(a_qk_hi.sem, 1)

            def read_rope(base, per_head, h, hh, n, half):
                if half == 0 and not is_zero(hh):
                    act.wait_ge(a_qk_lo.sem, a_qk_lo.after(hh, 3) - 4)
                read_half(base, per_head, h, (4 if is_zero(hh) else 0) + n // 2, half,
                          qkf[:, n // 2, half * HALF:(half + 1) * HALF], scale=(AD ** -0.5 if n == 0 else 1.0))

            def m_head(h, last):
                def read_v(e, half):
                    read_half(G_M, 8, h, 6 + e, half, vz[:, e, half * HALF:(half + 1) * HALF])

                read_oz(h, 0)
                for t in range(NC):
                    m_step(h, t, last)
                act.wait_ge(h_done.sem, h_done.after(h, NC - 1))
                junk = kseq[:].rearrange("p c d -> p (c d)").bitcast(mybir.dt.bfloat16)
                for c in range(NC):
                    a = act.activation(junk[:, c * MV:(c + 1) * MV], hacc[:, c], ACT.Square,
                                       accum_out=hstat[:, 0, c:c + 1])
                a.then_inc(hs_act.sem, 1)
                act.wait_ge(hs_act.sem, hs_act.after(h, 0))
                act.activation(hstat[:, 1], hstat[:, 0], ACT.Ln, bias=eps[:], scale=1.0 / MV).then_inc(hs_act.sem, 1)
                act.wait_ge(hs_act.sem, hs_act.after(h, 1))
                act.activation(hstat[:, 1], hstat[:, 1], ACT.Exp, scale=-0.5).then_inc(hs_act.sem, 1)
                gate_exp_ln(h, 1, 1)
                read_qk(h, 0, 1, last)
                gate_exp(h, 1)
                read_qk(h, 1, 0, last)
                for e in range(2):
                    for k in (2 * e, 2 * e + 1):
                        i = k % 2
                        act.wait_ge(tr_read.sem, tr_read.after(h, k))
                        act.wait_ge(spilled_m[i], 16 * (2 * h + (e + 1)))
                        act.activation(hsp[i][:, 0], hst[:], ACT.Copy).then_inc(hsp_hi.sem, 1)
                        if k == 2 and not last:
                            conv_exp_ln(h + 1, 1)
                        act.wait_ge(hsplit_done.sem, hsplit_done.after(h, k))
                        act.dma_start(spill_m[:, bass.ds(2 * h + e, 1), :, i * HALF:(i + 1) * HALF].rearrange(
                            "i one p s -> p i (one s)"), hsp[i].bitcast(F32)).then_inc(spilled_m[i], 16)
                    if e == 0:
                        read_qk(h, 1, 1, last)
                        read_v(0, 0)
                        if not last:
                            conv_exp_ln(h + 1, 0)
                            act.wait_ge(conv_dve.sem, conv_dve.after(h + 1, 5 + CONV - 1))
                            read_v(0, 1)

                if not last:
                    conv_exp(h + 1, 0)
                    conv_exp(h + 1, 1)
                    v_high(h, 0)
                    qk_high(h + 1, 0)
                    read_v(1, 0)
                    k_rows(h)
                    qk_high(h + 1, 1)
                    read_v(1, 1)
                    v_high(h, 1)
                else:
                    read_v(0, 1)
                    k_high(0)
                    read_v(1, 0)
                    act.wait_ge(rope_done, 3 * 1 + 3)
                    q_high(0)
                    read_v(1, 1)

            with act.Fori(0, MH - 1) as h:
                m_head(h, False)
            m_head(MH - 1, True)

            def exps(h, q, comps=(0, 1)):
                b = q % 2
                if q > 0 and 0 in comps:
                    act.wait_ge(a_mix.sem, a_mix.after(h, 4 * q - 1))
                for c in comps:
                    act.wait_ge(a_max.sem, a_max.after(h, 2 * q + c))
                    act.activation(pr[:, c], ps[:, 2 + 2 * c:4 + 2 * c, :].rearrange("p b k -> p (b k)"), ACT.Exp,
                                   bias=nmax[:, b, c:c + 1], accum_out=den[:, b, c:c + 1]).then_inc(a_exp.sem, 1)

            def high_round(h, k, dst):
                act.wait_ge(a_tr.sem, a_tr.after(h, k))
                act.activation(dst, ps[:, 6, :].rearrange("p (k s) -> p k s", k=4), ACT.Copy).then_inc(a_tr_hi.sem, 1)

            def at_dst(q, i):
                return at_s[:, 0, 4 * i:4 * i + 4, (q % 2) * P:(q % 2 + 1) * P]

            def o_read(h, n):
                act.wait_ge(a_pv.sem, a_pv.after(h, n))
                if n > 0:
                    act.wait_ge(a_ost.sem, a_ost.after(h, 2 * (n - 1)))
                act.activation(of[:], ps[:, 7, 0:2 * P], ACT.Copy).then_inc(a_of.sem, 1)

            def o_rstd(h, n):
                act.wait_ge(a_ss.sem, a_ss.after(h, n))
                if n > 0:
                    act.wait_ge(a_ost.sem, a_ost.after(h, 2 * (n - 1)))
                act.activation(ors[:], ps[:, 7, 2 * P:4 * P], ACT.Ln, bias=eps[:], scale=1.0 / AV).then_inc(a_rs.sem, 1)
                act.wait_ge(a_rs.sem, a_rs.after(h, 2 * n))
                act.activation(ors[:], ors[:], ACT.Exp, scale=-0.5).then_inc(a_rs.sem, 1)

            def o_high(h, n):
                act.wait_ge(a_ost.sem, a_ost.after(h, 2 * n + 1))
                act.wait_ge(spilled_a, 16 * (4 * h + (n + 1)))
                act.activation(osp[:, 0], ost[:], ACT.Copy).then_inc(a_ohi.sem, 1)

            def a_head(h, first, last):
                def read_filler(n):
                    j, half = divmod(n, 2)
                    if last:
                        read_gate(G_GL, 0, 0, j, half, 4 + j, qkf, bmerge[:, 4 + j:5 + j])
                        return
                    if j < 2:
                        read_rope(G_A, 4, h, h + 1, 2 * j, half)
                        return
                    if n == 4:
                        act.wait_ge(a_tr.sem, a_tr.after(h, V_ROUND[1]))
                    if n == 6:
                        act.wait_ge(a_gate_dve.sem, a_gate_dve.after(h, 2))
                    read_half(G_A, 4, h, j, half, vz[:, j - 2, half * HALF:(half + 1) * HALF])

                exps(h, 0)
                if not first:
                    act.wait_ge(a_pv.sem, a_pv.after(h - 1, 3))
                high_round(h, 0, va[:, 0, 0:4, :])
                act.wait_ge(a_gate_dve.sem, a_gate_dve.after(h, 0))
                exp_ln(aw[:], a_gate_act.sem, a_gate_act.after(h, 0))
                read_filler(0)
                if not first:
                    o_rstd(h - 1, 3)
                for q in range(ST):
                    if q % 2 == 0 and q > 0:
                        act.wait_ge(a_pv.sem, a_pv.after(h, q // 2 - 1))
                    high_round(h, round_of(q, 0), at_dst(q, 0))
                    if q + 1 < ST:
                        exps(h, q + 1, (0,))
                    elif not last:
                        q_high(h + 1, (0,))
                    high_round(h, round_of(q, 1), at_dst(q, 1))
                    if q == 7 and not last:
                        q_high(h + 1, (1,))
                    if q + 1 < ST:
                        exps(h, q + 1, (1,))
                    if q == 0:
                        high_round(h, V_ROUND[1], va[:, 0, 4:8, :])
                    if q % 2 == 0 and q > 0:
                        o_rstd(h, q // 2 - 1)
                    if not last and q == 6:
                        act.wait_ge(a_score.sem, a_score.after(h, 15))
                        k_high(h + 1)
                    if q < 5:
                        read_filler(q + 1)
                    elif q > 5:
                        read_filler(q)
                    if q == 0 and not first:
                        o_high(h - 1, 3)
                    if q == 1:
                        act.wait_ge(a_gate_dve.sem, a_gate_dve.after(h, 1))
                        act.activation(aw[:], aw[:], ACT.Exp).then_inc(a_gate_act.sem, 1)
                    if q in (2, 4):
                        o_high(h, q // 2 - 1)
                    if q == 7:
                        o_high(h, 2)
                    if q % 2 == 1:
                        o_read(h, q // 2)

            for i in range(2):
                act.wait_ge(spilled_m[i], 16 + 16 * 2 * MH)
            a_head(0, True, False)
            with act.Fori(1, AH - 1) as h:
                a_head(h, False, False)
            a_head(AH - 1, False, True)
            o_rstd(AH - 1, 3)
            o_high(AH - 1, 3)

            with act.Fori(0, 4) as c:
                for j in range(2):
                    act.activation(fbias[:, j:j + 1], bmerge[:, bass.ds(8 + j + 2 * c, 1)], ACT.Copy).then_inc(bias_set, 1)
                    act.wait_ge(bias_set, 2 * c + (j + 1))
                    for half in range(2):
                        read_gate(G_G, 2, c, j, half, 8 + j + 2 * c, qkf, fbias[:, j:j + 1])

            def merge(n, base):
                with act.Fori(0, KT // 2) as c:
                    for par in range(2):
                        i = KT * n + 2 * c + par
                        act.wait_ge(f_product, i + 1)
                        read_half(base, 2, c, par, 0, fb[:, 0:HALF])
                        act.wait_ge(f_abs, i + 1)
                        act.activation(fw[:], fw[:], ACT.Exp).then_inc(f_act, 1)
                        act.wait_ge(f_act, 3 * i + 1)
                        act.activation(fw[:], fw[:], ACT.Ln, bias=1.0).then_inc(f_act, 1)
                        act.wait_ge(f_logsig, i + 1)
                        act.activation(fw[:], fw[:], ACT.Exp).then_inc(f_act, 1)
                        read_half(base, 2, c, par, 1, fb[:, HALF:2 * HALF])
                        if n == 1:
                            act.wait_ge(f_y, 2 * c + par + 1)
                            act.sem_inc(step_begun, 1)
                            act.activation(ys[:, 0, bass.ds(2 * c + par, 1), :].rearrange("p one s -> p (one s)"),
                                           ya[:, bass.ds(2 * c + par, 1), :].rearrange("p one s -> p (one s)"),
                                           ACT.Copy).then_inc(y_hi, 1)

            merge(0, G_FA)
            merge(1, G_FB)

            def out_tile(c, par):
                if not (isinstance(c, int) and c < 2):
                    act.wait_ge(o_tr, 2 * c - 2)
                for half in range(2):
                    act.wait_ge(proj_done, 2 * (G_O + c) + half + 1)
                    act.activation(outT[par][:, half * HALF:(half + 1) * HALF], ps[:, half, :],
                                   ACT.Copy).then_inc(proj_read, 1)

            def row_squares(c, par):
                if not (isinstance(c, int) and c < 2):
                    act.wait_ge(o_sums, c)
                for i in range(2):
                    act.wait_ge(o_rows, 2 * c + i + 1)
                    for q in range(4):
                        t = 4 * i + q
                        a = act.activation(junk_row[:, t * P:(t + 1) * P], ps[:, 2 + 2 * par + i, q * P:(q + 1) * P],
                                           ACT.Square, accum_out=tile_sums[:, par, t:t + 1])
                    a.then_inc(o_squares, 1)

            out_tile(0, 0)
            out_tile(1, 1)
            row_squares(0, 0)
            with act.Fori(1, KT // 2) as c2:
                out_tile(2 * c2, 0)
                row_squares(2 * c2 - 1, 1)
                out_tile(2 * c2 + 1, 1)
                row_squares(2 * c2, 0)
            row_squares(KT - 1, 1)
            act.wait_ge(o_sums, KT + 1)
            act.activation(tail_stat[:], row_sums[:], ACT.Ln, bias=eps[:], scale=1.0 / D).then_inc(o_stat, 1)
            act.wait_ge(o_stat, 1)
            act.activation(tail_stat[:], tail_stat[:], ACT.Exp, scale=-0.5).then_inc(o_stat, 1)


_INS = ["x", "pre_norm_g", "w_in", "conv_w", "conv_b", "gate_b", "m_norm_g", "lambda_qk", "a_norm_g",
        "w_branch_m", "w_branch_a", "b_merge", "w_out", "post_norm_g"]


def constants():
    c = np.zeros((P, K_END), np.float32)
    i = np.arange(P)
    c[:, K_ID:K_ID + P] = i[:, None] == i[None, :]
    c[:, K_REV:K_REV + P] = i[:, None] + i[None, :] == P - 1
    c[:, K_MASK:K_MASK + P] = np.where(i[:, None] > i[None, :], MASKED, 0.0)
    c[:, K_MASK + P:K_MASK + 2 * P] = np.where(i[:, None] < i[None, :], MASKED, 0.0)
    inv = np.float32(THETA) ** (-np.arange(0, ROPE, 2, dtype=np.float32) / np.float32(ROPE))
    ang = (np.arange(S, dtype=np.float32)[None, :] * inv[:, None].astype(np.float32)).astype(np.float32)
    c[:, K_COS:K_COS + S] = 1.0
    half = ROPE // 2
    for first in (0, AD):
        for part, sign in ((0, -1.0), (1, 1.0)):
            rows = slice(first + part * half, first + (part + 1) * half)
            c[rows, K_COS:K_COS + S] = np.cos(ang)
            c[rows, K_SIN:K_SIN + S] = sign * np.sin(ang)
    return c


def kernel(**inputs):
    import concourse.bacc as bacc
    from concourse.bass_utils import run_bass_kernel_spmd

    nc = bacc.Bacc("TRN2", target_bir_lowering=False, num_devices=1)
    arrays = {f"in_{n}": np.ascontiguousarray(inputs[n]) for n in _INS}
    arrays["consts"] = constants()
    args = [nc.dram_tensor(n, a.shape, mybir.dt.from_np(a.dtype), kind="ExternalInput").ap()
            for n, a in arrays.items()]
    out = nc.dram_tensor("out", (1, S, D), F32, kind="ExternalOutput").ap()
    hybrid_block(nc, *args, out)
    r = run_bass_kernel_spmd(nc, [arrays], core_ids=[0])
    return r.results[0]["out"]
```
